# Optimizing a Trainium2 kernel written in Bass

```python
import math
import jax, jax.numpy as jnp
from jax import lax
import numpy as np

D_MODEL = 1024
BATCH = 1
SEQ = 1024
DEPTH = 1

CHUNK = 64
Q_BLOCK = 128
SB_HEADS = 8
SB_HEAD_DIM = 64
SB_WIDTH = SB_HEADS * SB_HEAD_DIM
CA_HEADS = 8
CA_HEAD_DIM = 64
CA_WIDTH = CA_HEADS * CA_HEAD_DIM
CA_LEFT_CHUNKS = 8
CA_BAND = (CA_LEFT_CHUNKS + 1) * CHUNK
CA_PAD = CA_LEFT_CHUNKS * CHUNK
REL_CLIP = 128
N_REL = 2 * REL_CLIP + 1
IN_COLS = 3 * SB_WIDTH + 3 * CA_WIDTH + 2 * D_MODEL
PEER_HEADS = 8
PEER_N_KEYS = 128
PEER_N_EXPERTS = PEER_N_KEYS * PEER_N_KEYS
PEER_QUERY_DIM = 256
PEER_HALF = PEER_QUERY_DIM // 2
PEER_TOPK = 16
PEER_TOKEN_BLOCK = 128
RMS_EPS = 1e-6
NEG_INF = -1e30

kernel_name = "hybrid_stickbreak_chunkattn_peer"

def rmsnorm(x, g):
    xf = x.astype(jnp.float32)
    y = xf * lax.rsqrt(jnp.mean(xf * xf, axis=-1, keepdims=True) + RMS_EPS)
    return (y * g.astype(jnp.float32)).astype(x.dtype)

def split_in_proj(p):
    widths = (SB_WIDTH,) * 3 + (CA_WIDTH,) * 3 + (D_MODEL, D_MODEL)
    cuts = np.cumsum(widths)[:-1].tolist()
    return jnp.split(p, cuts, axis=-1)

def stick_breaking_attention(q, k, v):
    B, S, H, Dh = q.shape
    scale = 1.0 / math.sqrt(Dh)
    kf = k.astype(jnp.float32)
    vf = v.astype(jnp.float32)
    key_pos = jnp.arange(S)

    def one_block(i):
        start = i * Q_BLOCK
        qb = lax.dynamic_slice_in_dim(q, start, Q_BLOCK, axis=1).astype(jnp.float32)
        z = jnp.einsum('bqhd,bkhd->bhqk', qb, kf) * scale
        qpos = start + jnp.arange(Q_BLOCK)
        causal = (key_pos[None, :] < qpos[:, None])[None, None]
        log_1m = jnp.where(causal, jax.nn.log_sigmoid(-z), 0.0)
        after = lax.cumsum(log_1m, axis=3, reverse=True) - log_1m
        w = jnp.where(causal, jnp.exp(jax.nn.log_sigmoid(z) + after), 0.0)
        return jnp.einsum('bhqk,bkhd->bqhd', w, vf)

    out = lax.map(one_block, jnp.arange(S // Q_BLOCK))
    return jnp.moveaxis(out, 0, 1).reshape(B, S, H, Dh)

def chunked_rel_attention(q, k, v, rel_table):
    B, S, H, Dh = q.shape
    scale = 1.0 / math.sqrt(Dh)
    kp = jnp.pad(k, ((0, 0), (CA_PAD, 0), (0, 0), (0, 0)))
    vp = jnp.pad(v, ((0, 0), (CA_PAD, 0), (0, 0), (0, 0)))
    rel = jnp.arange(CHUNK)[:, None] + CA_PAD - jnp.arange(CA_BAND)[None, :]
    bias = rel_table.astype(jnp.float32)[:, jnp.clip(rel, -REL_CLIP, REL_CLIP) + REL_CLIP]

    def one_chunk(c):
        start = c * CHUNK
        qc = lax.dynamic_slice_in_dim(q, start, CHUNK, axis=1).astype(jnp.float32)
        kb = lax.dynamic_slice_in_dim(kp, start, CA_BAND, axis=1).astype(jnp.float32)
        vb = lax.dynamic_slice_in_dim(vp, start, CA_BAND, axis=1).astype(jnp.float32)
        s = jnp.einsum('bqhd,bkhd->bhqk', qc, kb) * scale + bias[None]
        valid = (start - CA_PAD + jnp.arange(CA_BAND)) >= 0
        s = jnp.where(valid[None, None, None, :], s, NEG_INF)
        p = jax.nn.softmax(s, axis=-1)
        return jnp.einsum('bhqk,bkhd->bqhd', p, vb)

    out = lax.map(one_chunk, jnp.arange(S // CHUNK))
    return jnp.moveaxis(out, 0, 1).reshape(B, S, H, Dh)

def peer_ffn(h, w_query, sub_keys, expert_u, expert_v):
    B, S, D = h.shape
    tokens = h.reshape(B * S // PEER_TOKEN_BLOCK, PEER_TOKEN_BLOCK, D)
    keys_f = sub_keys.astype(jnp.float32)

    def one_block(xb):
        xf = xb.astype(jnp.float32)
        q = (xb @ w_query).astype(jnp.float32).reshape(PEER_TOKEN_BLOCK, PEER_HEADS, 2, PEER_HALF)
        scores = jnp.einsum('thpc,hpnc->thpn', q, keys_f)
        top_v, top_i = lax.top_k(scores, PEER_TOPK)
        cand_v = (top_v[:, :, 0, :, None] + top_v[:, :, 1, None, :]).reshape(
            PEER_TOKEN_BLOCK, PEER_HEADS, PEER_TOPK * PEER_TOPK)
        cand_i = (top_i[:, :, 0, :, None] * PEER_N_KEYS + top_i[:, :, 1, None, :]).reshape(
            PEER_TOKEN_BLOCK, PEER_HEADS, PEER_TOPK * PEER_TOPK)
        best_v, best_pos = lax.top_k(cand_v, PEER_TOPK)
        expert_idx = jnp.take_along_axis(cand_i, best_pos, axis=-1)
        g = jax.nn.softmax(best_v, axis=-1)
        u = expert_u[expert_idx].astype(jnp.float32)
        a = jax.nn.gelu(jnp.einsum('thkd,td->thk', u, xf), approximate=False)
        vsel = expert_v[expert_idx].astype(jnp.float32)
        return jnp.einsum('thk,thkd->td', g * a, vsel).astype(xb.dtype)

    out = lax.map(one_block, tokens)
    return out.reshape(B, S, D)

def setup_inputs(seed: int = 0) -> dict:
    key = jax.random.key(seed)
    ks = jax.random.split(key, 16)
    f32 = jnp.float32
    nrm = lambda k, shape, s: jax.random.normal(k, shape, f32) * s
    return {
        "x": nrm(ks[0], (BATCH, SEQ, D_MODEL), 1.0),
        "norm_mix": 1.0 + nrm(ks[1], (DEPTH, D_MODEL), 0.02),
        "w_in": nrm(ks[2], (DEPTH, D_MODEL, IN_COLS), D_MODEL ** -0.5),
        "w_sb_proj": nrm(ks[3], (DEPTH, SB_WIDTH, D_MODEL), SB_WIDTH ** -0.5),
        "w_ca_proj": nrm(ks[4], (DEPTH, CA_WIDTH, D_MODEL), CA_WIDTH ** -0.5),
        "ca_rel_bias": nrm(ks[5], (DEPTH, CA_HEADS, N_REL), 0.5),
        "w_out": nrm(ks[6], (DEPTH, D_MODEL, D_MODEL), D_MODEL ** -0.5),
        "norm_ffn": 1.0 + nrm(ks[7], (DEPTH, D_MODEL), 0.02),
        "peer_w_query": nrm(ks[8], (DEPTH, D_MODEL, PEER_HEADS * PEER_QUERY_DIM), D_MODEL ** -0.5),
        "peer_sub_keys": nrm(ks[9], (DEPTH, PEER_HEADS, 2, PEER_N_KEYS, PEER_HALF), PEER_HALF ** -0.5),
        "peer_u": nrm(ks[10], (DEPTH, PEER_N_EXPERTS, D_MODEL), D_MODEL ** -0.5),
        "peer_v": nrm(ks[11], (DEPTH, PEER_N_EXPERTS, D_MODEL), 0.5),
        "norm_final": 1.0 + nrm(ks[12], (D_MODEL,), 0.02),
    }

def reference(x, norm_mix, w_in, w_sb_proj, w_ca_proj, ca_rel_bias, w_out, norm_ffn,
              peer_w_query, peer_sub_keys, peer_u, peer_v, norm_final):
    B, S, _ = x.shape
    for layer in range(DEPTH):
        h = rmsnorm(x, norm_mix[layer])
        proj = h @ w_in[layer]
        q_sb, k_sb, v_sb, q_ca, k_ca, v_ca, gate_sb, gate_ca = split_in_proj(proj)
        sb4 = lambda t: t.reshape(B, S, SB_HEADS, SB_HEAD_DIM)
        ca4 = lambda t: t.reshape(B, S, CA_HEADS, CA_HEAD_DIM)
        o_sb = stick_breaking_attention(sb4(q_sb), sb4(k_sb), sb4(v_sb)).reshape(B, S, SB_WIDTH)
        o_ca = chunked_rel_attention(ca4(q_ca), ca4(k_ca), ca4(v_ca),
                                     ca_rel_bias[layer]).reshape(B, S, CA_WIDTH)
        br_sb = (o_sb.astype(x.dtype) @ w_sb_proj[layer]).astype(jnp.float32)
        br_ca = (o_ca.astype(x.dtype) @ w_ca_proj[layer]).astype(jnp.float32)
        merged = (jax.nn.sigmoid(gate_sb.astype(jnp.float32)) * br_sb
                  + jax.nn.sigmoid(gate_ca.astype(jnp.float32)) * br_ca)
        x = x + merged.astype(x.dtype) @ w_out[layer]
        h2 = rmsnorm(x, norm_ffn[layer])
        x = x + peer_ffn(h2, peer_w_query[layer], peer_sub_keys[layer],
                         peer_u[layer], peer_v[layer])
    return rmsnorm(x, norm_final)


_drawn_inputs = setup_inputs


def setup_inputs(seed=0):
    import zlib

    import numpy as np

    out = dict(_drawn_inputs(seed))
    spreads = {}
    factors = {}
    for name, (base, spread) in spreads.items():
        noise = np.random.default_rng([zlib.crc32(name.encode()), seed]).standard_normal(out[name].shape)
        drawn = base * np.exp(spread * noise) if base else spread * noise
        out[name] = __import__('jax').numpy.asarray(drawn.astype(out[name].dtype))
    for name, factor in factors.items():
        out[name] = (out[name] * factor).astype(out[name].dtype)
    return out
```

```python
from contextlib import ExitStack

import concourse.bass as bass
from concourse import mybir

ALU = mybir.AluOpType
ACT = mybir.ActivationFunctionType
F32 = mybir.dt.float32
I32 = mybir.dt.int32
U32 = mybir.dt.uint32
AX_X = mybir.AxisListType.X

P = 128
D = 1024
S = 1024
NB = S // P
NC = D // P
HD = 64
HEADS = 8
WIDTH = HEADS * HD
NCT = WIDTH // P
HALF = 512
EPS = 1e-6
MASKED = -1e30
CHUNK = 64
LOWEST = -3.0e38
BAND = 5 * P
REL = 128
NREL = 2 * REL + 1
EXT = BAND + P
PH = 8
NK = 128
NS = 2 * PH
TOPK = 16
NEXP = NK * NK
EXP_AND_LN = 6
NSEL = PH * TOPK


def normalise_and_project(nc, x, norm_mix, w_in, rel_reversed, ident, hT, qkT_dram, v_dram, ext_dram, bias_dram):
    XR = 4
    NW = 3
    with ExitStack() as ctx:
        def sb(name, shape, dt=F32):
            return ctx.enter_context(nc.sbuf_tensor(name, shape, dt))

        def sem(name):
            return ctx.enter_context(nc.semaphore(name))

        xt = sb("xt", [P, XR, D])
        xs = sb("xs", [P, XR, D])
        sq = sb("sq", [P, XR, D])
        ss = sb("ss", [P, XR])
        root = sb("root", [P, XR])
        rstd = sb("rstd", [P, XR])
        eps = sb("eps", [P, 1])
        g1 = sb("g1", [P, NC])
        w = sb("w_qkv", [P, NW, NC, HALF])
        rel = sb("ca_rel", [HEADS, NREL])
        ext = sb("ca_ext", [HEADS, EXT])
        hidden = sb("ca_hidden", [CHUNK, HEADS, CHUNK])
        stage = sb("proj_stage", [P, 4, HALF])
        turned = ctx.enter_context(nc.psum_tensor("turned", [P, 2, NC, P], F32))
        acc = ctx.enter_context(nc.psum_tensor("proj_acc", [P, 4, HALF], F32))

        x_in = [sem(f"x_in{i}") for i in range(XR)]
        g1_in, eps_set = sem("g1_in"), sem("eps_set")
        squared, rooted, rstd_set, x_scaled = sem("squared"), sem("rooted"), sem("rstd_set"), sem("x_scaled")
        x_turned, h_set = sem("x_turned"), sem("h_set")
        w_loaded = [sem(f"w_loaded{i}") for i in range(NW)]
        acc_full, staged = sem("acc_full"), sem("staged")
        stored = [sem(f"stored{i}") for i in range(4)]
        rel_in, ext_set, ext_out, window_out, hidden_set = sem("rel_in"), sem("ext_set"), sem("ext_out"), sem("window_out"), sem("hidden_set")

        x_rows = x.rearrange("a (b p) d -> (a b) p d", p=P)
        w_rows = w_in[0].rearrange("(c p) n -> p c n", p=P)
        UNITS = 8

        def window(row, column):
            return bass.AP(tensor=bias_dram.tensor, offset=row * (EXT - 1) + column + P - 1,
                           ap=[[EXT - 1, CHUNK], [P * EXT, HEADS], [1, CHUNK]])

        block = ctx.enter_context(nc.Block())

        @block.sync
        def _(sp):
            sp.dma_start(g1[:, :], norm_mix[0].rearrange("(c p) -> p c", p=P), allow_slow_non_contiguous=True).then_inc(g1_in, 16)
            for j in range(XR):
                sp.dma_start(xt[:, j, :], x_rows[j]).then_inc(x_in[j], 16)
            for n in range(NW):
                sp.dma_start(w[:, n, :, :], w_rows[:, :, n * WIDTH:(n + 1) * WIDTH]).then_inc(w_loaded[n], 16)
            with sp.Fori(1, NB // XR) as i:
                for j in range(XR):
                    sp.wait_ge(x_scaled, (i - 1) * XR + j + 1)
                    sp.dma_start(xt[:, j, :], x_rows[bass.ds(i * XR + j, 1)][0]).then_inc(x_in[j], 16)
            sp.dma_start(rel[:, :], rel_reversed).then_inc(rel_in, 16)
            sp.wait_ge(ext_set, 3)
            sp.dma_start(ext_dram, ext[:, :]).then_inc(ext_out, 16)
            sp.wait_ge(ext_out, 16)
            for h in range(HEADS):
                sp.dma_start(bias_dram[h], ext_dram[h:h + 1, :].to_broadcast([P, EXT])).then_inc(window_out, 16)
            sp.wait_ge(window_out, 16 * HEADS)
            sp.wait_ge(hidden_set, 1)
            sp.dma_start(window(0, BAND - CHUNK), hidden[:, :, :]).then_inc(window_out, 16)
            sp.dma_start(window(CHUNK, 0), hidden[:, :, :]).then_inc(window_out, 16)
            sp.wait_ge(window_out, 16 * (HEADS + 2))
            for n in range(NW):
                sp.wait_ge(acc_full, (n + 1) * UNITS)
                sp.dma_start(w[:, n, :, :], w_rows[:, :, (NW + n) * WIDTH:(NW + n + 1) * WIDTH]).then_inc(w_loaded[n], 16)

        @block.gpsimd
        def _(pool):
            nc.gpsimd.memset(hidden[:, :, :], MASKED).then_inc(hidden_set, 1)
            for a in range(2):
                for n in range(NW):
                    for u in range(UNITS):
                        pool.wait_ge(staged, a * NW * UNITS + n * UNITS + u + 1)
                        if n < 2:
                            dst = qkT_dram[bass.ds(a, 1), n, (u % 4) * P:(u % 4 + 1) * P, (u // 4) * HALF:(u // 4 + 1) * HALF][0]
                        else:
                            dst = v_dram[bass.ds(a, 1), u * P:(u + 1) * P, :][0]
                        pool.dma_start(dst, stage[:, u % 4, :]).then_inc(stored[u % 4], 16)
            for j in range(4):
                pool.wait_ge(stored[j], 16 * 2 * NW * UNITS // 4)

        @block.scalar
        def _(act):
            act.wait_ge(eps_set, 1)
            def turn(i):
                for j in range(XR):
                    act.wait_ge(x_in[j], 16 * i + 16)
                    act.wait_ge(x_scaled, XR * i)
                    nc.scalar.activation(sq[:, j, :], xt[:, j, :], ACT.Square, accum_out=ss[:, j:j + 1]).then_inc(squared, 1)
                act.wait_ge(squared, XR * i + XR)
                nc.scalar.activation(root[:, :], ss[:, :], ACT.Sqrt, scale=1.0 / D, bias=eps[:, 0:1]).then_inc(rooted, 1)

            turn(0)
            with act.Fori(1, NB // XR) as i:
                turn(i)
            for a in range(2):
                for n in range(NW):
                    for u in range(UNITS):
                        act.wait_ge(acc_full, a * NW * UNITS + n * UNITS + u + 1)
                        act.wait_ge(stored[u % 4], a * (16 * NW * 2) + 16 * (n * 2 + u // 4))
                        nc.scalar.activation(stage[:, u % 4, :], acc[:, u % 4, :], ACT.Copy,
                                             scale=float(HD) ** -0.5 if n == 0 else 1.0).then_inc(staged, 1)

        @block.vector
        def _(dve):
            nc.vector.memset(eps[:, :], EPS).then_inc(eps_set, 1)
            dve.wait_ge(g1_in, 16)
            def turn(i):
                dve.wait_ge(rooted, i + 1)
                nc.vector.reciprocal(rstd[:, :], root[:, :]).then_inc(rstd_set, 1)
                dve.wait_ge(rstd_set, i + 1)
                dve.wait_ge(x_turned, XR * i)
                for j in range(XR):
                    nc.vector.tensor_scalar(xs[:, j, :], xt[:, j, :], rstd[:, j:j + 1], None, ALU.mult).then_inc(x_scaled, 1)
                for j in range(XR):
                    dve.wait_ge(x_turned, XR * i + j + 1)
                    nc.vector.tensor_tensor(hT[:, :, bass.ds((i * XR + j) * P, P)], turned[:, j % 2, :, :],
                                            g1[:, :].unsqueeze(2).to_broadcast([P, NC, P]), ALU.mult).then_inc(h_set, 1)

            turn(0)
            with dve.Fori(1, NB // XR) as i:
                turn(i)

            dve.wait_ge(rel_in, 16)
            nc.vector.memset(ext[:, 0:EXT - NREL], 0.0).then_inc(ext_set, 1)
            nc.vector.tensor_copy(ext[:, EXT - NREL:], rel[:, :]).then_inc(ext_set, 1)
            dve.wait_ge(ext_set, 2)
            nc.vector.tensor_scalar(ext[:, 0:EXT - NREL], ext[:, 0:EXT - NREL], rel[:, 0:1], None, ALU.add).then_inc(ext_set, 1)

        @block.tensor
        def _(pe):
            def turn(i):
                for j in range(XR):
                    pe.wait_ge(x_scaled, XR * i + j + 1)
                    pe.wait_ge(h_set, XR * i + j - 1 if j >= 2 or not isinstance(i, int) else 0)
                    for c in range(NC):
                        mm = nc.tensor.transpose(turned[:, j % 2, c, :], xs[:, j, c * P:(c + 1) * P], ident[:, :])
                    mm.then_inc(x_turned, 1)

            turn(0)
            with pe.Fori(1, NB // XR) as i:
                turn(i)
            for a in range(2):
                for n in range(NW):
                    for u in range(UNITS):
                        if u == 0:
                            pe.wait_ge(w_loaded[n], 16 * a + 16)
                        pe.wait_ge(h_set, NB // 2 if u < 4 and n < 2 else NB)
                        back = n * UNITS + u - 4
                        pe.wait_ge(staged, a * NW * UNITS + back + 1 if back >= 0 else a * (NW * UNITS + back + 1))
                        for c in range(NC):
                            if n < 2:
                                lhs = w[:, n, c, (u % 4) * P:(u % 4 + 1) * P]
                                rhs = hT[:, c, (u // 4) * HALF:(u // 4 + 1) * HALF]
                            else:
                                lhs = hT[:, c, u * P:(u + 1) * P]
                                rhs = w[:, n, c, :]
                            mm = nc.tensor.matmul(acc[:, u % 4, :], lhs, rhs, start=(c == 0), stop=(c == NC - 1))
                        mm.then_inc(acc_full, 1)

def stick_breaking(nc, qkT_dram, v_dram, neg_suffix, neg_ones, ident, masked, oT_dram):
    LARGE = 30.0
    SLOTS = 6
    AHEAD = 4
    STEPS = [(t, j, max(0, j - 4 * t) * P) for t in range(2) for j in range(4 * t + 3, -1, -1)]
    NSTEP = 2 * len(STEPS)
    step = [(h, *STEPS[i]) for i in range(len(STEPS)) for h in range(2)]
    LAST = [n for n, (h, t, j, c0) in enumerate(step) if j == 0]
    with ExitStack() as ctx:
        def sb(name, shape, dt=F32):
            return ctx.enter_context(nc.sbuf_tensor(name, shape, dt))

        def sem(name):
            return ctx.enter_context(nc.semaphore(name))

        qk = sb("sb_qk", [HD, 2, 2, S])
        v = sb("sb_v", [P, 2, NB, HD])
        low = sb("sb_low", [P, SLOTS, HALF])
        soft = sb("sb_soft", [P, SLOTS, HALF])
        wts = sb("sb_wts", [P, SLOTS, HALF])
        total = sb("sb_total", [P, 2, HALF])
        out = sb("sb_out", [HD, 2, HALF])
        zeros = sb("sb_zeros", [P, P])
        z = ctx.enter_context(nc.psum_tensor("sb_z", [P, SLOTS, HALF], F32))
        o = ctx.enter_context(nc.psum_tensor("sb_o", [HD, 2, HALF], F32))

        head_in = [sem("sb_head_in0"), sem("sb_head_in1")]
        z_set, low_set, exp_set, log_set = sem("sb_z_set"), sem("sb_low_set"), sem("sb_exp"), sem("sb_log")
        soft_set, total_set, after_set = sem("sb_soft"), sem("sb_total"), sem("sb_after")
        wts_set, wts_used, o_set, o_copied = sem("sb_wts"), sem("sb_wts_used"), sem("sb_o"), sem("sb_copied")
        o_stored = [sem("sb_stored0"), sem("sb_stored1")]
        zeros_set = sem("sb_zeros_set")
        PAIRS = HEADS // 2

        block = ctx.enter_context(nc.Block())

        @block.sync
        def _(sp):
            def turn(i):
                for h in range(2):
                    sp.wait_ge(wts_used, NSTEP * i)
                    row = i * P + h * HD
                    for n in range(2):
                        sp.dma_start(qk[:, h, n, :], qkT_dram[0, n, bass.ds(row, HD), :]).then_inc(head_in[h], 16)
                    sp.dma_start(v[:, h, :, :], v_dram[0, :, bass.ds(row, HD)].rearrange("(b p) d -> p b d", p=P)).then_inc(head_in[h], 16)

            turn(0)
            with sp.Fori(1, PAIRS) as i:
                turn(i)

        @block.gpsimd
        def _(pool):
            nc.gpsimd.memset(zeros[:, :], 0.0).then_inc(zeros_set, 1)
            pool.wait_ge(zeros_set, 1)
            def turn(i):
                for n, (h, t, j, c0) in enumerate(step):
                    first = j == 4 * t + 3
                    if j > 0:
                        old = HALF if first else max(0, j + 1 - 4 * t) * P
                        pool.wait_ge(soft_set, NSTEP * i + n + 1)
                        pool.wait_ge(after_set, NSTEP * i + n + 1)
                        s = soft[:, n % SLOTS, :]
                        if old < HALF:
                            last = nc.gpsimd.tensor_tensor(total[:, h, old:], total[:, h, old:], s[:, old:], ALU.add)
                        if old > c0:
                            last = nc.gpsimd.tensor_tensor(total[:, h, c0:old], s[:, c0:old], zeros[:, :], ALU.add)
                        last.then_inc(total_set, 1)
                    if j == 0:
                        k = LAST.index(n)
                        pool.wait_ge(o_copied, 4 * i + k + 1)
                        pool.dma_start(oT_dram[0, bass.ds(i * P + h * HD, HD), t * HALF:(t + 1) * HALF],
                                       out[:, k % 2, :]).then_inc(o_stored[k % 2], 16)

            turn(0)
            with pool.Fori(1, PAIRS) as i:
                turn(i)
            for k in range(2):
                pool.wait_ge(o_stored[k], 16 * 2 * PAIRS)

        def adds_before(n):
            return sum(1 for (h, t, j, c0) in step[:n] if j > 0)

        TOTALS = adds_before(NSTEP)

        @block.tensor
        def _(pe):
            def scores(i, n):
                h, t, j, c0 = step[n]
                if n < 2:
                    pe.wait_ge(head_in[h], 48 * i + 48)
                pe.wait_ge(wts_set, NSTEP * i + n - SLOTS + 1 if n >= SLOTS else NSTEP * i)
                diag = j >= 4 * t
                mm = nc.tensor.matmul(z[:, n % SLOTS, c0:], qk[:, h, 1, j * P:(j + 1) * P],
                                      qk[:, h, 0, t * HALF + c0:(t + 1) * HALF], start=True, stop=True)
                if diag:
                    mm = nc.tensor.matmul(z[:, n % SLOTS, c0:c0 + P], ident[:, :], masked[:, :], start=False, stop=True,
                                          skip_group_check=True)
                mm.then_inc(z_set, 1)

            def after(i, n):
                h, t, j, c0 = step[n]
                pe.wait_ge(soft_set, NSTEP * i + n + 1)
                mm = nc.tensor.matmul(z[:, n % SLOTS, c0:], neg_suffix[:, :], soft[:, n % SLOTS, c0:],
                                      start=False, stop=True, skip_group_check=True)
                if j < 4 * t + 3:
                    old = max(0, j + 1 - 4 * t) * P
                    pe.wait_ge(total_set, TOTALS * i + adds_before(n - 1))
                    mm = nc.tensor.matmul(z[:, n % SLOTS, old:], neg_ones[:, :], total[:, h, old:],
                                          start=False, stop=True, skip_group_check=True)
                mm.then_inc(after_set, 1)

            def values(i, n):
                h, t, j, c0 = step[n]
                pe.wait_ge(wts_set, NSTEP * i + n + 1)
                if j == 4 * t + 3:
                    pe.wait_ge(o_copied, 4 * i + (h + 1 if t else 0))
                mm = nc.tensor.matmul(o[:, h, c0:], v[:, h, j, :], wts[:, n % SLOTS, c0:],
                                      start=(j == 4 * t + 3), stop=(j == 0), skip_group_check=True)
                mm.then_inc(wts_used, 1)

            def turn(i):
                for n in range(AHEAD):
                    scores(i, n)
                for n in range(NSTEP):
                    if n + AHEAD < NSTEP:
                        scores(i, n + AHEAD)
                    after(i, n)
                    if n >= 2:
                        values(i, n - 2)
                values(i, NSTEP - 2)
                values(i, NSTEP - 1)

            turn(0)
            with pe.Fori(1, PAIRS) as i:
                turn(i)

        @block.scalar
        def _(act):
            def log_part(i, n):
                h, t, j, c0 = step[n]
                act.wait_ge(low_set, NSTEP * i + n + 1)
                s = low[:, n % SLOTS, c0:]
                nc.scalar.activation(s, s, ACT.Exp).then_inc(exp_set, 1)
                act.wait_ge(exp_set, NSTEP * i + n + 1)
                nc.scalar.activation(s, s, ACT.Ln, bias=1.0).then_inc(log_set, 1)

            def weights(i, n):
                h, t, j, c0 = step[n]
                act.wait_ge(after_set, NSTEP * i + n + 1)
                if n >= SLOTS:
                    act.wait_ge(wts_used, NSTEP * i + n - SLOTS + 1)
                nc.scalar.activation(wts[:, n % SLOTS, c0:], z[:, n % SLOTS, c0:], ACT.Exp).then_inc(wts_set, 1)

            act.add_instruction(mybir.InstLoadActFuncSet(name=nc.get_next_instruction_name(), act_func_set_id=EXP_AND_LN))
            def turn(i):
                for n in range(3):
                    log_part(i, n)
                for n in range(NSTEP):
                    if n + 3 < NSTEP:
                        log_part(i, n + 3)
                    weights(i, n)

            turn(0)
            with act.Fori(1, PAIRS) as i:
                turn(i)

        @block.vector
        def _(dve):
            def limit(i, n):
                h, t, j, c0 = step[n]
                dve.wait_ge(z_set, NSTEP * i + n + 1)
                nc.vector.tensor_single_scalar(low[:, n % SLOTS, c0:], z[:, n % SLOTS, c0:], LARGE, ALU.min).then_inc(low_set, 1)

            def softplus(i, n):
                h, t, j, c0 = step[n]
                dve.wait_ge(log_set, NSTEP * i + n + 1)
                if n >= SLOTS:
                    dve.wait_ge(total_set, TOTALS * i + adds_before(n - SLOTS + 1))
                nc.vector.tensor_tensor(soft[:, n % SLOTS, c0:], z[:, n % SLOTS, c0:], low[:, n % SLOTS, c0:], ALU.max).then_inc(soft_set, 1)

            def copy_out(i, k):
                n = LAST[k]
                h, t, j, c0 = step[n]
                dve.wait_ge(wts_used, NSTEP * i + n + 1)
                dve.wait_ge(o_stored[k % 2], 32 * i + 16 * (k // 2))
                nc.vector.tensor_copy(out[:, k % 2, :], o[:, h, :]).then_inc(o_copied, 1)

            def turn(i):
                for n in range(AHEAD):
                    limit(i, n)
                softplus(i, 0)
                for n in range(NSTEP):
                    if n + 1 < NSTEP:
                        softplus(i, n + 1)
                    if n + AHEAD < NSTEP:
                        limit(i, n + AHEAD)
                    if n - 2 in LAST:
                        copy_out(i, LAST.index(n - 2))
                for k, n in enumerate(LAST):
                    if n + 2 >= NSTEP:
                        copy_out(i, k)

            turn(0)
            with dve.Fori(1, PAIRS) as i:
                turn(i)

def chunk_attention(nc, qkT_dram, v_dram, ident, bias_dram, oT_dram):
    SLOTS = 2
    step = [(h, qb, min(qb, 4) + 1) for qb in range(NB) for h in range(2)]
    NSTEP = len(step)
    PAIRS = HEADS // 2
    with ExitStack() as ctx:
        def sb(name, shape, dt=F32):
            return ctx.enter_context(nc.sbuf_tensor(name, shape, dt))

        def sem(name):
            return ctx.enter_context(nc.semaphore(name))

        qk = sb("ca_qk", [HD, 2, 2, S])
        v = sb("ca_v", [P, 2, NB, HD])
        bias = sb("ca_bias", [P, 2, BAND])
        prob = sb("ca_prob", [P, 4, BAND])
        probT = sb("ca_probT", [P, 2, 5, P])
        neg_top = sb("ca_neg_top", [P, 4])
        mass = sb("ca_mass", [P, 4])
        inv = sb("ca_inv", [P, 4])
        out = sb("ca_out", [HD, 2, HALF])
        s = ctx.enter_context(nc.psum_tensor("ca_s", [P, SLOTS, 2 * HALF], F32))
        turned = ctx.enter_context(nc.psum_tensor("ca_turned", [P, 2 * HALF], F32))
        o = ctx.enter_context(nc.psum_tensor("ca_o", [HD, 2, HALF], F32))

        head_in = [sem("ca_head_in0"), sem("ca_head_in1")]
        s_set, biased_set, neg_set = sem("ca_s_set"), sem("ca_biased"), sem("ca_neg")
        exp_set, inv_set, prob_set = sem("ca_exp"), sem("ca_inv"), sem("ca_prob")
        turned_set, probT_set, o_set, o_copied = sem("ca_turned"), sem("ca_probT"), sem("ca_o"), sem("ca_copied")
        o_stored = [sem("ca_stored0"), sem("ca_stored1")]

        block = ctx.enter_context(nc.Block())

        @block.sync
        def _(sp):
            def turn(i):
                for h in range(2):
                    sp.wait_ge(o_set, NSTEP * i)
                    row = i * P + h * HD
                    for n in range(2):
                        sp.dma_start(qk[:, h, n, :], qkT_dram[1, n, bass.ds(row, HD), :]).then_inc(head_in[h], 16)
                    sp.dma_start(v[:, h, :, :], v_dram[1, :, bass.ds(row, HD)].rearrange("(b p) d -> p b d", p=P)).then_inc(head_in[h], 16)
                    sp.dma_start(bias[:, h, :], bass.AP(tensor=bias_dram.tensor, offset=(2 * i + h) * (P * EXT) + P - 1,
                                                        ap=[[EXT - 1, P], [1, BAND]])).then_inc(head_in[h], 16)

            turn(0)
            with sp.Fori(1, PAIRS) as i:
                turn(i)

        @block.gpsimd
        def _(pool):
            def send(i, quad, h):
                pool.wait_ge(o_copied, 4 * i + 2 * quad + h + 1)
                pool.dma_start(oT_dram[1, bass.ds(i * P + h * HD, HD), quad * HALF:(quad + 1) * HALF],
                               out[:, h, :]).then_inc(o_stored[h], 16)

            def turn(i):
                for n in range(NSTEP):
                    h, qb, nk = step[n]
                    pool.wait_ge(inv_set, NSTEP * i + n + 1)
                    row = prob[:, n % 4, 0:nk * P]
                    nc.gpsimd.tensor_tensor(row, row, inv[:, n % 4:n % 4 + 1].to_broadcast([P, nk * P]), ALU.mult).then_inc(prob_set, 1)
                    if n in (12, 13):
                        send(i, 0, n - 12)
                send(i, 1, 0)
                send(i, 1, 1)

            turn(0)
            with pool.Fori(1, PAIRS) as i:
                turn(i)
            for h in range(2):
                pool.wait_ge(o_stored[h], 16 * 2 * PAIRS)

        @block.tensor
        def _(pe):
            def scores(i, n):
                h, qb, nk = step[n]
                if n < 2:
                    pe.wait_ge(head_in[h], 64 * i + 64)
                pe.wait_ge(biased_set, NSTEP * i + n - SLOTS + 1 if n >= SLOTS else NSTEP * i)
                k0, w = (qb - nk + 1) * P, nk * P
                for a in range(0, w, HALF):
                    b = min(w, a + HALF)
                    mm = nc.tensor.matmul(s[:, n % SLOTS, a:b], qk[:, h, 0, qb * P:(qb + 1) * P], qk[:, h, 1, k0 + a:k0 + b],
                                          start=True, stop=True)
                mm.then_inc(s_set, 1)

            def transpose_probs(i, n):
                h, qb, nk = step[n]
                pe.wait_ge(prob_set, NSTEP * i + n + 1)
                pe.wait_ge(probT_set, NSTEP * i + n)
                for b in range(nk):
                    mm = nc.tensor.transpose(turned[:, b * P:(b + 1) * P], prob[:, n % 4, b * P:(b + 1) * P], ident[:, :])
                mm.then_inc(turned_set, 1)

            def values(i, n):
                h, qb, nk = step[n]
                pe.wait_ge(probT_set, NSTEP * i + n + 1)
                if qb % 4 == 0:
                    pe.wait_ge(o_copied, 4 * i + (2 if qb else 0))
                for b in range(nk):
                    mm = nc.tensor.matmul(o[:, h, (qb % 4) * P:(qb % 4 + 1) * P], v[:, h, qb - nk + 1 + b, :], probT[:, n % 2, b, :],
                                          start=(b == 0), stop=(b == nk - 1))
                mm.then_inc(o_set, 1)

            def turn(i):
                for n in range(NSTEP + 3):
                    if n < NSTEP:
                        scores(i, n)
                    if 2 <= n < NSTEP + 2:
                        transpose_probs(i, n - 2)
                    if n >= 3:
                        values(i, n - 3)

            turn(0)
            with pe.Fori(1, PAIRS) as i:
                turn(i)

        @block.scalar
        def _(act):
            def turn(i):
                for n in range(NSTEP + 1):
                    if n < NSTEP:
                        h, qb, nk = step[n]
                        act.wait_ge(neg_set, NSTEP * i + n + 1)
                        nc.scalar.activation(prob[:, n % 4, 0:nk * P], prob[:, n % 4, 0:nk * P], ACT.Exp, bias=neg_top[:, n % 4:n % 4 + 1],
                                             accum_out=mass[:, n % 4:n % 4 + 1]).then_inc(exp_set, 1)
                    if n >= 1:
                        m = n - 1
                        h, qb, nk = step[m]
                        act.wait_ge(turned_set, NSTEP * i + m + 1)
                        act.wait_ge(o_set, NSTEP * i + m - 1 if m >= 2 else NSTEP * i)
                        nc.scalar.activation(probT[:, m % 2, 0:nk, :], turned[:, 0:nk * P].rearrange("p (b q) -> p b q", q=P),
                                             ACT.Copy).then_inc(probT_set, 1)

            turn(0)
            with act.Fori(1, PAIRS) as i:
                turn(i)

        @block.vector
        def _(dve):
            def biased(i, n):
                h, qb, nk = step[n]
                if n < 2:
                    dve.wait_ge(head_in[h], 64 * i + 64)
                dve.wait_ge(s_set, NSTEP * i + n + 1)
                dve.wait_ge(turned_set, NSTEP * i + n - 3 if n >= 4 else NSTEP * i)
                row = prob[:, n % 4, 0:nk * P]
                nc.vector.tensor_tensor(row, s[:, n % SLOTS, 0:nk * P], bias[:, h, BAND - nk * P:], ALU.add).then_inc(biased_set, 1)
                dve.wait_ge(biased_set, NSTEP * i + n + 1)
                nc.vector.tensor_reduce(neg_top[:, n % 4:n % 4 + 1], row, AX_X, ALU.max, negate=True).then_inc(neg_set, 1)

            def scaled(i, n):
                h, qb, nk = step[n]
                dve.wait_ge(exp_set, NSTEP * i + n + 1)
                nc.vector.reciprocal(inv[:, n % 4:n % 4 + 1], mass[:, n % 4:n % 4 + 1]).then_inc(inv_set, 1)

            def copy_out(i, k):
                quad, h = k // 2, k % 2
                dve.wait_ge(o_set, NSTEP * i + 8 * quad + 6 + h + 1)
                dve.wait_ge(o_stored[h], 32 * i + 16 * quad)
                nc.vector.tensor_copy(out[:, h, :], o[:, h, :]).then_inc(o_copied, 1)

            def turn(i):
                biased(i, 0)
                for n in range(NSTEP):
                    if n + 1 < NSTEP:
                        biased(i, n + 1)
                    scaled(i, n)
                    if n == 10:
                        copy_out(i, 0)
                        copy_out(i, 1)
                copy_out(i, 2)
                copy_out(i, 3)

            turn(0)
            with dve.Fori(1, PAIRS) as i:
                turn(i)

def gate_and_merge(nc, w_in, w_sb_proj, w_ca_proj, hT, oT_dram, mT_dram):
    GATES = 6 * WIDTH
    with ExitStack() as ctx:
        def sb(name, shape, dt=F32):
            return ctx.enter_context(nc.sbuf_tensor(name, shape, dt))

        def sem(name):
            return ctx.enter_context(nc.semaphore(name))

        oT = sb("oT", [P, 2, NCT, S])
        wg = sb("w_gate", [P, 2, 2, NC, P])
        wp = sb("w_branch", [P, 2, 2, NCT, P])
        gate = sb("gate", [P, 2, 2, HALF])
        part = sb("part", [P, 2, 2, HALF])
        merged = sb("merged", [P, 2, HALF])
        acc = ctx.enter_context(nc.psum_tensor("merge_acc", [P, 2, 4, HALF], F32))

        o_in = sem("o_in")
        w_loaded = [sem("gate_w0"), sem("gate_w1")]
        gates_full, branches_full = sem("gates_full"), sem("branches_full")
        gate_set, part_set, merged_set = sem("gate_set"), sem("part_set"), sem("merged_set")
        stored = [sem("merge_stored0"), sem("merge_stored1")]
        PAIRS = NC // 2

        w_cols = w_in[0].rearrange("(c p) n -> p c n", p=P)
        sb_cols = w_sb_proj[0].rearrange("(c p) n -> p c n", p=P)
        ca_cols = w_ca_proj[0].rearrange("(c p) n -> p c n", p=P)

        block = ctx.enter_context(nc.Block())

        @block.sync
        def _(sp):
            def turn(i):
                for j in range(2):
                    if not isinstance(i, int):
                        sp.wait_ge(branches_full, 4 * i - 2 + 2 * j)
                    col = (2 * i + j) * P
                    for a in range(2):
                        sp.dma_start(wg[:, j, a, :, :], w_cols[:, :, bass.ds(col + (GATES + a * D), P)]).then_inc(w_loaded[j], 16)
                    sp.dma_start(wp[:, j, 0, :, :], sb_cols[:, :, bass.ds(col, P)]).then_inc(w_loaded[j], 16)
                    sp.dma_start(wp[:, j, 1, :, :], ca_cols[:, :, bass.ds(col, P)]).then_inc(w_loaded[j], 16)

            turn(0)
            with sp.Fori(1, PAIRS) as i:
                turn(i)

        @block.gpsimd
        def _(pool):
            for a in range(2):
                pool.dma_start(oT[:, a, :, :], oT_dram[a].rearrange("(c p) t -> p c t", p=P)).then_inc(o_in, 16)
            def turn(i):
                for j in range(2):
                    for u in range(2):
                        pool.wait_ge(merged_set, 4 * i + 2 * j + u + 1)
                        pool.dma_start(mT_dram[bass.ds((2 * i + j) * P, P), u * HALF:(u + 1) * HALF], merged[:, u, :]).then_inc(stored[u], 16)

            turn(0)
            with pool.Fori(1, PAIRS) as i:
                turn(i)
            for u in range(2):
                pool.wait_ge(stored[u], 16 * NC)

        @block.tensor
        def _(pe):
            def turn(i):
                for j in range(2):
                    pe.wait_ge(w_loaded[j], 64 * i + 64)
                    for u in range(2):
                        cols = slice(u * HALF, (u + 1) * HALF)
                        n = 2 * j + u
                        pe.wait_ge(merged_set, 4 * i + n - 1 if n >= 2 else 4 * i)
                        for a in range(2):
                            for c in range(NC):
                                mm = nc.tensor.matmul(acc[:, u, a, :], wg[:, j, a, c, :], hT[:, c, cols], start=(c == 0), stop=(c == NC - 1))
                        mm.then_inc(gates_full, 1)
                        pe.wait_ge(o_in, 32)
                        for a in range(2):
                            for c in range(NCT):
                                mm = nc.tensor.matmul(acc[:, u, 2 + a, :], wp[:, j, a, c, :], oT[:, a, c, cols], start=(c == 0), stop=(c == NCT - 1))
                        mm.then_inc(branches_full, 1)

            turn(0)
            with pe.Fori(1, PAIRS) as i:
                turn(i)

        @block.scalar
        def _(act):
            def turn(i):
                for n in range(4):
                    u = n % 2
                    act.wait_ge(gates_full, 4 * i + n + 1)
                    act.wait_ge(merged_set, 4 * i + n - 1 if n >= 2 else 4 * i)
                    nc.scalar.activation(gate[:, u, :, :], acc[:, u, 0:2, :], ACT.Sigmoid).then_inc(gate_set, 1)

            turn(0)
            with act.Fori(1, PAIRS) as i:
                turn(i)

        @block.vector
        def _(dve):
            def turn(i):
                for n in range(4):
                    u = n % 2
                    dve.wait_ge(gate_set, 4 * i + n + 1)
                    dve.wait_ge(branches_full, 4 * i + n + 1)
                    dve.wait_ge(merged_set, 4 * i + n - 1 if n >= 2 else 4 * i)
                    nc.vector.tensor_tensor(part[:, u, :, :], gate[:, u, :, :], acc[:, u, 2:4, :], ALU.mult).then_inc(part_set, 1)
                    dve.wait_ge(part_set, 4 * i + n + 1)
                    dve.wait_ge(stored[u], 16 * (2 * i + n // 2))
                    nc.vector.tensor_tensor(merged[:, u, :], part[:, u, 0, :], part[:, u, 1, :], ALU.add).then_inc(merged_set, 1)

            turn(0)
            with dve.Fori(1, PAIRS) as i:
                turn(i)

def route_and_retrieve(nc, x, w_out, norm_ffn, w_query, keysT, expert_u, expert_v, norm_final, ident, mT_dram, out):
    RU = 4
    RV = 4
    SLOTS = NSEL
    QG = PH * 2 * NK // HALF
    with ExitStack() as ctx:
        def sb(name, shape, dt=F32):
            return ctx.enter_context(nc.sbuf_tensor(name, shape, dt))

        def sem(name):
            return ctx.enter_context(nc.semaphore(name))

        wo = sb("w_out_sb", [P, NC, D])
        wq = sb("w_query_sb", [P, NC, QG * HALF])
        keys = sb("keys", [P, NS, NK])
        g2 = sb("g2", [P, D])
        gf = sb("gf", [P, D])
        u_rows = sb("u_rows", [P, RU, D])
        v_rows = sb("v_rows", [P, RV, D])
        x1n, x1c = sb("x1_next", [P, D]), sb("x1_now", [P, D])
        h2n, h2c = sb("h2_next", [P, D]), sb("h2_now", [P, D])
        q = sb("query", [P, NS * NK])
        qT = sb("queryT", [P, NS, NK])
        scores = sb("scores", [P, NS, NK])
        scores2 = sb("scores2", [P, NS, NK])
        mblk = q[:, 0:D].rearrange("p (c t) -> p c t", t=P)
        h2T = qT[:, 0:NC, :]
        junk = scores2[:, 0:NC, :].rearrange("p a n -> p (a n)")
        cand = q[:, :].rearrange("p (h n) -> p h n", h=PH)
        cand2 = qT[:, :, :].rearrange("p (h a) n -> p h (a n)", a=2)
        hot = scores2[:, :, :].rearrange("p a (b i) -> p (a b) i", i=TOPK)
        diag = sb("diag", [P, RV, P])
        tv = sb("top_values", [P, NS, TOPK])
        ti = sb("top_index", [P, NS, TOPK], U32)
        bv = sb("best_values", [P, PH, TOPK])
        bp = sb("best_pos", [P, PH, TOPK], U32)
        bij = sb("best_ij", [P, 2, NSEL], U32)
        eij = sb("expert_ij", [P, 2, NSEL])
        iota = sb("iota", [P, TOPK])
        shifted = sb("shifted", [P, PH, TOPK])
        mass = sb("gate_mass", [P, PH])
        minv = sb("gate_inv", [P, PH])
        gate_n, gate_c = sb("gate_next", [P, NSEL]), sb("gate_now", [P, NSEL])
        idx_n, idx_c = sb("index_next", [P, NSEL], I32), sb("index_now", [P, NSEL], I32)
        dots = sb("dots", [P, NSEL])
        gel = sb("gelu", [P, NSEL])
        wts = sb("expert_wts", [P, NSEL])
        eps = sb("eps2", [P, 1])
        ss, root, rstd = sb("ss2", [P, 1]), sb("root2", [P, 1]), sb("rstd2", [P, 1])
        ssy, rooty, rstdy = sb("ssy", [P, 1]), sb("rooty", [P, 1]), sb("rstdy", [P, 1])
        front = ctx.enter_context(nc.psum_tensor("front", [P, 4, HALF], F32))
        sums = ctx.enter_context(nc.psum_tensor("sums", [P, 2, HALF], F32))

        wo_in = [sem("wo_in0"), sem("wo_in1")]
        g2_in, keys_in, gf_in, eps_set, iota_set = sem("g2_in"), sem("keys_in"), sem("gf_in"), sem("eps2_set"), sem("iota_set")
        m_in, x_in = sem("m_in"), sem("xb_in")
        wq_in = [sem(f"wq_in{i}") for i in range(QG)]
        unit_full, unit_taken = sem("unit_full"), sem("unit_taken")
        x1_set, sq_set, root_set, rstd_set, h2_set = sem("x1_set"), sem("sq2_set"), sem("root2_set"), sem("rstd2_set"), sem("h2_set")
        search = sem("search")
        shift_set, gexp_set, gate_set = sem("shift_set"), sem("gexp_set"), sem("gate_n_set")
        idx_set, idx_moved, now_set = sem("idx_set"), sem("idx_moved"), sem("now_set")
        u_in = [sem(f"u_in{i}") for i in range(RU)]
        v_in = [sem(f"v_in{i}") for i in range(RV)]
        dot_set, gel_set, wts_set, diag_set = sem("dot_set"), sem("gel_set"), sem("expert_wts_set"), sem("diag_set")
        v_free, y_set, ysq_set, yroot_set, yrstd_set, yout_set = (sem("v_free"), sem("y_set"), sem("ysq_set"), sem("yroot_set"),
                                                                  sem("yrstd_set"), sem("yout_set"))
        y_stored, search_passed, pool_passed = sem("y_stored"), sem("search_passed"), sem("pool_passed")

        x_rows = x.rearrange("a (b p) d -> (a b) p d", p=P)
        out_rows = out.rearrange("a (b p) d -> (a b) p d", p=P)
        wq_rows = w_query[0].rearrange("(c p) n -> p c n", p=P)

        def unit(u, b):
            bank = front[:, u % 4, :]
            if u < 2:
                if u == 0:
                    nc.tensor.wait_ge(m_in, 16 * b + 16)
                nc.tensor.wait_ge(unit_taken, 14 * b)
                nc.tensor.wait_ge(wo_in[u], 16)
                for c in range(NC):
                    mm = nc.tensor.matmul(bank, mblk[:, c, :], wo[:, c, u * HALF:(u + 1) * HALF], start=(c == 0), stop=(c == NC - 1))
            elif u < 4:
                nc.tensor.wait_ge(h2_set, b + 1)
                for c in range(4):
                    k = 4 * (u - 2) + c
                    mm = nc.tensor.transpose(bank[:, c * P:(c + 1) * P], h2n[:, k * P:(k + 1) * P], ident[:, :])
            elif u < 8:
                nc.tensor.wait_ge(unit_taken, 14 * b + 2)
                g = u - 4
                nc.tensor.wait_ge(wq_in[g], 16)
                for c in range(NC):
                    mm = nc.tensor.matmul(bank, h2T[:, c, :], wq[:, c, g * HALF:(g + 1) * HALF], start=(c == 0), stop=(c == NC - 1))
            elif u < 12:
                nc.tensor.wait_ge(unit_taken, 14 * b + 2 + (u - 8) + 1)
                for c in range(4):
                    k = 4 * (u - 8) + c
                    mm = nc.tensor.transpose(bank[:, c * P:(c + 1) * P], q[:, k * P:(k + 1) * P], ident[:, :])
            else:
                nc.tensor.wait_ge(unit_taken, 14 * b + 6 + (u - 12) + 1)
                nc.tensor.wait_ge(keys_in, 16)
                for c in range(4):
                    k = 4 * (u - 12) + c
                    mm = nc.tensor.matmul(bank[:, c * P:(c + 1) * P], qT[:, k, :], keys[:, k, :], start=True, stop=True)
            mm.then_inc(unit_full, 1)

        def take(u, b):
            nc.scalar.wait_ge(unit_full, 16 * b + u + 1)
            if u < 8:
                nc.scalar.wait_ge(idx_set, b)
            if u < 4:
                dst = h2T[:, 4 * (u - 2):4 * (u - 1), :]
            elif u < 8:
                dst = q[:, (u - 4) * HALF:(u - 3) * HALF]
            elif u < 12:
                dst = qT[:, 4 * (u - 8):4 * (u - 7), :]
            else:
                dst = scores[:, 4 * (u - 12):4 * (u - 11), :]
            nc.scalar.activation(dst, front[:, u % 4, :], ACT.Copy).then_inc(unit_taken, 1)

        def search_norm_act(b):
            nc.scalar.wait_ge(x1_set, 2 * b + 2)
            nc.scalar.wait_ge(idx_set, b)
            nc.scalar.activation(junk, x1n[:, :], ACT.Square, accum_out=ss[:, :]).then_inc(sq_set, 1)
            nc.scalar.wait_ge(sq_set, b + 1)
            nc.scalar.activation(root[:, :], ss[:, :], ACT.Sqrt, scale=1.0 / D, bias=eps[:, 0:1]).then_inc(root_set, 1)

        def search_x1(b, u):
            nc.vector.wait_ge(unit_full, 16 * b + u + 1)
            nc.vector.wait_ge(x_in, 16 * b + 16)
            cols = slice(u * HALF, (u + 1) * HALF)
            nc.vector.tensor_tensor(x1n[:, cols], front[:, u, :], x1n[:, cols], ALU.add).then_inc(x1_set, 1)

        def search_h2(b):
            nc.vector.wait_ge(root_set, b + 1)
            nc.vector.reciprocal(rstd[:, :], root[:, :]).then_inc(rstd_set, 1)
            nc.vector.wait_ge(rstd_set, b + 1)
            nc.vector.scalar_tensor_tensor(h2n[:, :], x1n[:, :], rstd[:, 0:1], g2[:, :], op0=ALU.mult, op1=ALU.mult).then_inc(h2_set, 1)

        LISTS, SUMS, PICK = 5 * NS, 5 * NS + 1, 5 * NS + 1 + 5 * PH
        NSEARCH = PICK + 10

        def after_step(b, n):
            nc.vector.wait_ge(search, NSEARCH * b + n)
            nc.vector.sem_inc(search_passed, 1)

        def search_lists(b, r):
            rnd = r // 4
            if r == 0:
                nc.vector.wait_ge(unit_taken, 14 * b + 14)
            if r % 4 == 0:
                after_step(b, rnd * NS)
            for l in range(4 * (r % 4), 4 * (r % 4) + 4):
                if rnd == 0:
                    step = nc.vector.max(tv[:, l, 0:8], scores[:, l, :])
                elif rnd == 1:
                    step = nc.vector.max_index(ti[:, l, 0:8], tv[:, l, 0:8], scores[:, l, :])
                elif rnd == 2:
                    step = nc.vector.match_replace(scores2[:, l, :], tv[:, l, 0:8], scores[:, l, :], LOWEST)
                elif rnd == 3:
                    step = nc.vector.max(tv[:, l, 8:16], scores2[:, l, :])
                else:
                    step = nc.vector.max_index(ti[:, l, 8:16], tv[:, l, 8:16], scores2[:, l, :])
                step.then_inc(search, 1)

        def search_sums(b):
            after_step(b, LISTS)
            first = tv[:, 0::2, :].unsqueeze(3).to_broadcast([P, PH, TOPK, TOPK])
            second = tv[:, 1::2, :].unsqueeze(2).to_broadcast([P, PH, TOPK, TOPK])
            nc.vector.tensor_tensor(cand.rearrange("p h (i j) -> p h i j", j=TOPK), first, second, ALU.add).then_inc(search, 1)

        def search_best(b, r):
            rnd = r // 2
            if r % 2 == 0:
                after_step(b, SUMS + rnd * PH)
            for h in range(4 * (r % 2), 4 * (r % 2) + 4):
                if rnd == 0:
                    step = nc.vector.max(bv[:, h, 0:8], cand[:, h, :])
                elif rnd == 1:
                    step = nc.vector.max_index(bp[:, h, 0:8], bv[:, h, 0:8], cand[:, h, :])
                elif rnd == 2:
                    step = nc.vector.match_replace(cand2[:, h, :], bv[:, h, 0:8], cand[:, h, :], LOWEST)
                elif rnd == 3:
                    step = nc.vector.max(bv[:, h, 8:16], cand2[:, h, :])
                else:
                    step = nc.vector.max_index(bp[:, h, 8:16], bv[:, h, 8:16], cand2[:, h, :])
                step.then_inc(search, 1)

        def search_pick(b, r):
            flat = bp[:, :, :].rearrange("p h k -> p (h k)")
            if r == 0:
                after_step(b, PICK)
                nc.vector.tensor_single_scalar(bij[:, 0, :], flat, 4, ALU.logical_shift_right).then_inc(search, 1)
                nc.vector.tensor_single_scalar(bij[:, 1, :], flat, TOPK - 1, ALU.bitwise_and).then_inc(search, 1)
                after_step(b, PICK + 2)
                nc.vector.tensor_tensor(shifted[:, :, :], bv[:, :, :], bv[:, :, 0:1].to_broadcast([P, PH, TOPK]), ALU.subtract).then_inc(shift_set, 1)
            elif r < 7:
                side, part = (r - 1) // 3, (r - 1) % 3
                after_step(b, PICK + 2 + r - 1)
                if part == 0:
                    pos = bij[:, side, :].unsqueeze(2).to_broadcast([P, NSEL, TOPK])
                    row = iota[:, :].unsqueeze(1).to_broadcast([P, NSEL, TOPK])
                    nc.vector.tensor_tensor(hot, pos, row, ALU.is_equal).then_inc(search, 1)
                elif part == 1:
                    hot4 = hot.rearrange("p (h k) i -> p h k i", h=PH)
                    key = ti[:, side::2, :].unsqueeze(2).to_broadcast([P, PH, TOPK, TOPK])
                    nc.vector.tensor_tensor(hot4, hot4, key, ALU.mult).then_inc(search, 1)
                else:
                    nc.vector.tensor_reduce(eij[:, side, :], hot, AX_X, ALU.add).then_inc(search, 1)
            elif r == 7:
                after_step(b, PICK + 8)
                nc.vector.wait_ge(idx_moved, b)
                nc.vector.scalar_tensor_tensor(idx_n[:, :], eij[:, 0, :], float(NK), eij[:, 1, :], op0=ALU.mult, op1=ALU.add).then_inc(idx_set, 1)
                nc.vector.wait_ge(gexp_set, b + 1)
                nc.vector.tensor_reduce(mass[:, :], shifted[:, :, :], AX_X, ALU.add).then_inc(search, 1)
                after_step(b, PICK + 9)
                nc.vector.reciprocal(minv[:, :], mass[:, :]).then_inc(search, 1)
            else:
                after_step(b, PICK + 10)
                nc.vector.tensor_tensor(gate_n[:, :].rearrange("p (h k) -> p h k", h=PH), shifted[:, :, :],
                                        minv[:, :].unsqueeze(2).to_broadcast([P, PH, TOPK]), ALU.mult).then_inc(gate_set, 1)

        def search_exp(b):
            nc.scalar.wait_ge(shift_set, b + 1)
            nc.scalar.activation(shifted[:, :, :], shifted[:, :, :], ACT.Exp).then_inc(gexp_set, 1)

        def unit_at(s):
            return s // 4 - 1 if 4 <= s < 68 and s % 4 == 0 else None

        LISTS_AT, SUMS_AT = 68, 88
        BEST_AT, PICK_AT = 89, 99

        def search_dve(s, b):
            if s in (6, 10):
                search_x1(b, s // 4 - 1)
            if s == 11:
                search_h2(b)
            if LISTS_AT <= s < SUMS_AT:
                search_lists(b, s - LISTS_AT)
            if s == SUMS_AT:
                search_sums(b)
            if BEST_AT <= s < PICK_AT:
                search_best(b, s - BEST_AT)
            if PICK_AT <= s < PICK_AT + 9:
                search_pick(b, s - PICK_AT)

        def search_act(s, b):
            if s == 10:
                search_norm_act(b)
            u = unit_at(s - 2) if s >= 2 else None
            if u is not None and u >= 2:
                take(u, b)
            if s == PICK_AT + 2:
                search_exp(b)

        block = ctx.enter_context(nc.Block())

        @block.sync
        def _(sp):
            def search_block(b):
                sp.wait_ge(unit_full, 16 * b)
                sp.wait_ge(idx_set, b)
                sp.dma_start(mblk, mT_dram.rearrange("(c p) t -> p c t", p=P)[:, :, bass.ds(b * P, P)]).then_inc(m_in, 16)
                sp.wait_ge(now_set, 3 * b)
                sp.dma_start(x1n[:, :], x_rows[bass.ds(b, 1)][0]).then_inc(x_in, 16)

            for a in range(2):
                sp.dma_start(wo[:, :, a * HALF:(a + 1) * HALF], w_out[0].rearrange("(c p) n -> p c n", p=P)[:, :, a * HALF:(a + 1) * HALF]).then_inc(wo_in[a], 16)
                if a == 0:
                    search_block(0)
            sp.dma_start(g2[:, :], norm_ffn.to_broadcast([P, D])).then_inc(g2_in, 16)
            for g in range(QG):
                sp.dma_start(wq[:, :, g * HALF:(g + 1) * HALF], wq_rows[:, :, g * HALF:(g + 1) * HALF]).then_inc(wq_in[g], 16)
            sp.dma_start(keys[:, :, :], keysT).then_inc(keys_in, 16)
            sp.dma_start(gf[:, :], norm_final.rearrange("(a d) -> a d", a=1).to_broadcast([P, D])).then_inc(gf_in, 16)

            with sp.Fori(1, NB) as b:
                search_block(b)

        @block.gpsimd
        def _(pool):
            nc.gpsimd.iota(iota[:, :], [[1, TOPK]], base=0, channel_multiplier=0,
                           allow_small_or_imprecise_dtypes=True).then_inc(iota_set, 1)

            def gather_u(index, col, n, b):
                if b is not None:
                    pool.wait_ge(dot_set, SLOTS * b + n - RU + 1)
                    pool.sem_inc(pool_passed, 1)
                elif n >= RU:
                    pool.wait_ge(dot_set, n - RU + 1)
                pool.indirect_dma_start(u_rows[:, n % RU, :], None, expert_u[0], bass.IndirectOffsetOnAxis(index[:, col:col + 1], 0)).then_inc(u_in[n % RU], 16)

            def gather_v(n, b):
                pool.wait_ge(v_free, SLOTS * b + n + 1)
                pool.sem_inc(pool_passed, 1)
                pool.indirect_dma_start(v_rows[:, n % RV, :], None, expert_v[0], bass.IndirectOffsetOnAxis(idx_c[:, n:n + 1], 0)).then_inc(v_in[n % RV], 16)

            def retrieve(b, last):
                for n in range(RU):
                    pool.wait_ge(u_in[n], 16 * (SLOTS // RU) * b + 16 * (TOPK // RU))
                for n in range(RV):
                    pool.wait_ge(v_in[n], 16 * (SLOTS // RV) * b)
                pool.wait_ge(idx_set, b + 1)
                pool.sem_inc(pool_passed, 1)
                nc.gpsimd.tensor_copy(idx_c[:, :], idx_n[:, :]).then_inc(idx_moved, 1)
                pool.wait_ge(idx_moved, b + 1)
                for s in range(SLOTS):
                    if s + TOPK < SLOTS:
                        gather_u(idx_c, s + TOPK, s + TOPK, b)
                    elif not last:
                        if s + TOPK == SLOTS:
                            pool.wait_ge(idx_set, b + 2)
                        gather_u(idx_n, s + TOPK - SLOTS, s + TOPK, b)
                    gather_v(s, b)

            pool.wait_ge(idx_set, 1)
            for n in range(TOPK):
                gather_u(idx_n, n, n, None)
            retrieve(0, False)
            with pool.Fori(1, NB - 1) as b:
                retrieve(b, False)
            retrieve(NB - 1, True)

        @block.tensor
        def _(pe):
            pe.sem_inc(v_free, RV)
            for u in range(16):
                unit(u, 0)

            def retrieve(b, last):
                for s in range(SLOTS):
                    if s == 0:
                        pe.wait_ge(y_set, b)
                    pe.wait_ge(diag_set, SLOTS * b + s + 1)
                    pe.wait_ge(v_in[s % RV], 16 * (SLOTS // RV) * b + 16 * (s // RV + 1))
                    for a in range(2):
                        mm = nc.tensor.matmul(sums[:, a, :], diag[:, s % RV, :], v_rows[:, s % RV, a * HALF:(a + 1) * HALF],
                                              start=(s == 0), stop=(s == SLOTS - 1))
                    mm.then_inc(v_free, 1)
                    if not last and unit_at(s) is not None:
                        unit(unit_at(s), b + 1)

            retrieve(0, False)
            with pe.Fori(1, NB - 1) as b:
                retrieve(b, False)
            retrieve(NB - 1, True)

        @block.scalar
        def _(act):
            act.wait_ge(eps_set, 1)
            for s in range(SLOTS):
                search_act(s, 0)

            def gelu(h, b):
                act.wait_ge(dot_set, SLOTS * b + TOPK * h + TOPK)
                hs = slice((h % PH) * TOPK, (h % PH) * TOPK + TOPK)
                nc.scalar.activation(gel[:, hs], dots[:, hs], ACT.Gelu).then_inc(gel_set, 1)

            def finish(b):
                act.wait_ge(y_set, b + 1)
                act.wait_ge(idx_set, min(b + 2, NB) if isinstance(b, int) else b + 2)
                nc.scalar.activation(junk, x1c[:, :], ACT.Square, accum_out=ssy[:, :]).then_inc(ysq_set, 1)
                act.wait_ge(ysq_set, b + 1)
                nc.scalar.activation(rooty[:, :], ssy[:, :], ACT.Sqrt, scale=1.0 / D, bias=eps[:, 0:1]).then_inc(yroot_set, 1)
                act.wait_ge(yout_set, b + 1)
                act.dma_start(out_rows[bass.ds(b, 1)][0] if not isinstance(b, int) else out_rows[b], x1c[:, :]).then_inc(y_stored, 16)

            def retrieve(b, last):
                for s in range(SLOTS):
                    if s % TOPK == 0:
                        act.wait_ge(wts_set, PH * b + s // TOPK + 1)
                    act.wait_ge(v_free, SLOTS * b + s + 1)
                    nc.scalar.activation(diag[:, s % RV, :], ident[:, :], ACT.Copy, scale=wts[:, s:s + 1]).then_inc(diag_set, 1)
                    if s % TOPK == TOPK - 1 and not (last and s == SLOTS - 1):
                        gelu(s // TOPK + 1, b)
                    if not last:
                        search_act(s, b + 1)
                finish(b)

            gelu(0, 0)
            retrieve(0, False)
            with act.Fori(1, NB - 1) as b:
                retrieve(b, False)
            retrieve(NB - 1, True)
            act.wait_ge(y_stored, 16 * NB)

        @block.vector
        def _(dve):
            nc.vector.memset(eps[:, :], EPS).then_inc(eps_set, 1)
            dve.wait_ge(g2_in, 16)
            dve.wait_ge(iota_set, 1)
            for s in range(SLOTS):
                search_dve(s, 0)

            def dot(n, h2, b):
                row = u_rows[:, n % RU, :]
                dve.wait_ge(u_in[n % RU], 16 * (SLOTS // RU) * b + 16 * (n // RU + 1))
                nc.vector.tensor_tensor_reduce(row, row, h2, 1.0, 0.0, ALU.mult, ALU.add,
                                               dots[:, n % SLOTS:n % SLOTS + 1]).then_inc(dot_set, 1)

            def weigh(h, gate, b):
                dve.wait_ge(gel_set, PH * b + h + 1)
                hs = slice((h % PH) * TOPK, (h % PH) * TOPK + TOPK)
                if h:
                    dve.wait_ge(diag_set, SLOTS * b + TOPK * (h - PH + 1) if h >= PH else SLOTS * b)
                nc.vector.tensor_tensor(wts[:, hs], gel[:, hs], gate[:, hs], ALU.mult).then_inc(wts_set, 1)

            def retrieve(b, last):
                dve.wait_ge(dot_set, SLOTS * b + TOPK)
                nc.vector.tensor_copy(h2c[:, :], h2n[:, :]).then_inc(now_set, 1)
                dve.wait_ge(wts_set, PH * b + 1)
                nc.vector.tensor_copy(gate_c[:, :], gate_n[:, :]).then_inc(now_set, 1)
                dve.wait_ge(now_set, 3 * b + 2)
                for s in range(SLOTS):
                    if s == 1:
                        dve.wait_ge(y_stored, 16 * b)
                        nc.vector.tensor_copy(x1c[:, :], x1n[:, :]).then_inc(now_set, 1)
                    n = s + TOPK
                    if n < SLOTS:
                        dot(n, h2c[:, :], b)
                    elif not last:
                        dot(n, h2n[:, :], b)
                    if not last:
                        search_dve(s, b + 1)
                    if n % TOPK == TOPK - 1:
                        if n < SLOTS:
                            weigh(n // TOPK, gate_c, b)
                        elif not last:
                            dve.wait_ge(gate_set, b + 2)
                            weigh(n // TOPK, gate_n, b)
                dve.wait_ge(now_set, 3 * b + 3)
                dve.wait_ge(v_free, SLOTS * b + SLOTS + RV)
                nc.vector.tensor_tensor(x1c[:, :], sums[:, :, :].rearrange("p a n -> p (a n)"), x1c[:, :], ALU.add).then_inc(y_set, 1)
                dve.wait_ge(yroot_set, b + 1)
                nc.vector.reciprocal(rstdy[:, :], rooty[:, :]).then_inc(yrstd_set, 1)
                dve.wait_ge(yrstd_set, b + 1)
                dve.wait_ge(gf_in, 16)
                nc.vector.scalar_tensor_tensor(x1c[:, :], x1c[:, :], rstdy[:, 0:1], gf[:, :], op0=ALU.mult, op1=ALU.mult).then_inc(yout_set, 1)

            for n in range(TOPK):
                dot(n, h2n[:, :], 0)
            dve.wait_ge(gate_set, 1)
            weigh(0, gate_n, 0)
            retrieve(0, False)
            with dve.Fori(1, NB - 1) as b:
                retrieve(b, False)
            retrieve(NB - 1, True)


def constants(nc, ident, neg_suffix, neg_ones, masked):
    with ExitStack() as ctx:
        filled = ctx.enter_context(nc.semaphore("filled"))
        block = ctx.enter_context(nc.Block())

        @block.gpsimd
        def _(pool):
            nc.gpsimd.memset(ident[:, :], 0.0).then_inc(filled, 1)
            nc.gpsimd.memset(neg_ones[:, :], -1.0).then_inc(filled, 1)
            nc.gpsimd.memset(neg_suffix[:, :], -1.0).then_inc(filled, 1)
            nc.gpsimd.memset(masked[:, :], MASKED).then_inc(filled, 1)
            pool.wait_ge(filled, 4)
            nc.gpsimd.affine_select(out=ident[:, :], in_=ident[:, :], compare_op=ALU.not_equal, fill=1.0,
                                    base=0, pattern=[[-1, P]], channel_multiplier=1)
            nc.gpsimd.affine_select(out=neg_suffix[:, :], in_=neg_suffix[:, :], compare_op=ALU.is_ge, fill=0.0,
                                    base=0, pattern=[[-1, P]], channel_multiplier=1)
            nc.gpsimd.affine_select(out=masked[:, :], in_=masked[:, :], compare_op=ALU.is_ge, fill=0.0,
                                    base=0, pattern=[[-1, P]], channel_multiplier=1)


def program(nc, x, norm_mix, w_in, w_sb_proj, w_ca_proj, rel_reversed, w_out, norm_ffn, w_query, keysT,
            expert_u, expert_v, norm_final, out):
    def dram(name, shape):
        return nc.dram_tensor(name, shape, F32, kind="Internal").ap()

    qkT_dram = dram("qkT_dram", [2, 2, WIDTH, S])
    v_dram = dram("v_dram", [2, S, WIDTH])
    oT_dram = dram("oT_dram", [2, WIDTH, S])
    mT_dram = dram("mT_dram", [D, S])
    ext_dram = dram("ext_dram", [HEADS, EXT])
    bias_dram = dram("bias_dram", [HEADS, P, EXT])
    with ExitStack() as ctx:
        ident, neg_suffix, neg_ones, masked = (ctx.enter_context(nc.sbuf_tensor(n, [P, P], F32))
                                               for n in ("ident", "neg_suffix", "neg_ones", "masked"))
        constants(nc, ident, neg_suffix, neg_ones, masked)
        with nc.sbuf_tensor("hT", [P, NC, S], F32) as hT:
            normalise_and_project(nc, x, norm_mix, w_in, rel_reversed, ident, hT, qkT_dram, v_dram, ext_dram, bias_dram)
            stick_breaking(nc, qkT_dram, v_dram, neg_suffix, neg_ones, ident, masked, oT_dram)
            chunk_attention(nc, qkT_dram, v_dram, ident, bias_dram, oT_dram)
            gate_and_merge(nc, w_in, w_sb_proj, w_ca_proj, hT, oT_dram, mT_dram)
        route_and_retrieve(nc, x, w_out, norm_ffn, w_query, keysT, expert_u, expert_v, norm_final, ident, mT_dram, out)


_INS = ["x", "norm_mix", "w_in", "w_sb_proj", "w_ca_proj", "ca_rel_bias", "w_out", "norm_ffn", "peer_w_query",
        "peer_sub_keys", "peer_u", "peer_v", "norm_final"]


def kernel(**inputs):
    import numpy as np
    import concourse.bacc as bacc
    from concourse.bass_utils import run_bass_kernel_spmd

    nc = bacc.Bacc("TRN2", target_bir_lowering=False, num_devices=1)
    arrays, args = {}, []
    for name in _INS:
        a = np.asarray(inputs[name])
        if name == "ca_rel_bias":
            a = a[0, :, ::-1]
        if name == "peer_sub_keys":
            a = a[0].transpose(3, 0, 1, 2).reshape(P, NS, NK)
        a = np.ascontiguousarray(a)
        arrays[f"in_{name}"] = a
        args.append(nc.dram_tensor(f"in_{name}", a.shape, mybir.dt.from_np(a.dtype), kind="ExternalInput").ap())
    args.append(nc.dram_tensor("out_y", (1, S, D), F32, kind="ExternalOutput").ap())
    program(nc, *args)
    return run_bass_kernel_spmd(nc, [arrays], core_ids=[0]).results[0]["out_y"]
```

```python
from contextlib import ExitStack

import concourse.bass as bass
from concourse import mybir

ALU = mybir.AluOpType
ACT = mybir.ActivationFunctionType
F32 = mybir.dt.float32
I32 = mybir.dt.int32
U32 = mybir.dt.uint32
AX_X = mybir.AxisListType.X

P = 128
D = 1024
S = 1024
NB = S // P
NC = D // P
HD = 64
HEADS = 8
WIDTH = HEADS * HD
NCT = WIDTH // P
HALF = 512
EPS = 1e-6
MASKED = -1e30
CHUNK = 64
LOWEST = -3.0e38
BAND = 5 * P
REL = 128
NREL = 2 * REL + 1
EXT = BAND + P
PH = 8
NK = 128
NS = 2 * PH
TOPK = 16
NEXP = NK * NK
EXP_AND_LN = 6
NSEL = PH * TOPK


def normalise_and_project(nc, x, norm_mix, w_in, rel_reversed, ident, hT, qkT_dram, v_dram, ext_dram, bias_dram):
    XR = 4
    NW = 3
    with ExitStack() as ctx:
        def sb(name, shape, dt=F32):
            return ctx.enter_context(nc.sbuf_tensor(name, shape, dt))

        def sem(name):
            return ctx.enter_context(nc.semaphore(name))

        xt = sb("xt", [P, XR, D])
        xs = sb("xs", [P, XR, D])
        sq = sb("sq", [P, XR, D])
        ss = sb("ss", [P, XR])
        root = sb("root", [P, XR])
        rstd = sb("rstd", [P, XR])
        eps = sb("eps", [P, 1])
        g1 = sb("g1", [P, NC])
        w = sb("w_qkv", [P, NW, NC, HALF])
        rel = sb("ca_rel", [HEADS, NREL])
        ext = sb("ca_ext", [HEADS, EXT])
        hidden = sb("ca_hidden", [CHUNK, HEADS, CHUNK])
        stage = sb("proj_stage", [P, 4, HALF])
        turned = ctx.enter_context(nc.psum_tensor("turned", [P, 2, NC, P], F32))
        acc = ctx.enter_context(nc.psum_tensor("proj_acc", [P, 4, HALF], F32))

        x_in = [sem(f"x_in{i}") for i in range(XR)]
        g1_in, eps_set = sem("g1_in"), sem("eps_set")
        squared, rooted, rstd_set, x_scaled = sem("squared"), sem("rooted"), sem("rstd_set"), sem("x_scaled")
        x_turned, h_set = sem("x_turned"), sem("h_set")
        w_loaded = [sem(f"w_loaded{i}") for i in range(NW)]
        acc_full, staged = sem("acc_full"), sem("staged")
        stored = [sem(f"stored{i}") for i in range(4)]
        rel_in, ext_set, ext_out, window_out, hidden_set = sem("rel_in"), sem("ext_set"), sem("ext_out"), sem("window_out"), sem("hidden_set")

        x_rows = x.rearrange("a (b p) d -> (a b) p d", p=P)
        w_rows = w_in[0].rearrange("(c p) n -> p c n", p=P)
        UNITS = 8

        def window(row, column):
            return bass.AP(tensor=bias_dram.tensor, offset=row * (EXT - 1) + column + P - 1,
                           ap=[[EXT - 1, CHUNK], [P * EXT, HEADS], [1, CHUNK]])

        block = ctx.enter_context(nc.Block())

        @block.sync
        def _(sp):
            sp.dma_start(g1[:, :], norm_mix[0].rearrange("(c p) -> p c", p=P), allow_slow_non_contiguous=True).then_inc(g1_in, 16)
            for j in range(XR):
                sp.dma_start(xt[:, j, :], x_rows[j]).then_inc(x_in[j], 16)
            for n in range(NW):
                sp.dma_start(w[:, n, :, :], w_rows[:, :, n * WIDTH:(n + 1) * WIDTH]).then_inc(w_loaded[n], 16)
            with sp.Fori(1, NB // XR) as i:
                for j in range(XR):
                    sp.wait_ge(x_scaled, (i - 1) * XR + j + 1)
                    sp.dma_start(xt[:, j, :], x_rows[bass.ds(i * XR + j, 1)][0]).then_inc(x_in[j], 16)
            sp.dma_start(rel[:, :], rel_reversed).then_inc(rel_in, 16)
            sp.wait_ge(ext_set, 3)
            sp.dma_start(ext_dram, ext[:, :]).then_inc(ext_out, 16)
            sp.wait_ge(ext_out, 16)
            for h in range(HEADS):
                sp.dma_start(bias_dram[h], ext_dram[h:h + 1, :].to_broadcast([P, EXT])).then_inc(window_out, 16)
            sp.wait_ge(window_out, 16 * HEADS)
            sp.wait_ge(hidden_set, 1)
            sp.dma_start(window(0, BAND - CHUNK), hidden[:, :, :]).then_inc(window_out, 16)
            sp.dma_start(window(CHUNK, 0), hidden[:, :, :]).then_inc(window_out, 16)
            sp.wait_ge(window_out, 16 * (HEADS + 2))
            for n in range(NW):
                sp.wait_ge(acc_full, (n + 1) * UNITS)
                sp.dma_start(w[:, n, :, :], w_rows[:, :, (NW + n) * WIDTH:(NW + n + 1) * WIDTH]).then_inc(w_loaded[n], 16)

        @block.gpsimd
        def _(pool):
            nc.gpsimd.memset(hidden[:, :, :], MASKED).then_inc(hidden_set, 1)
            for a in range(2):
                for n in range(NW):
                    for u in range(UNITS):
                        pool.wait_ge(staged, a * NW * UNITS + n * UNITS + u + 1)
                        if n < 2:
                            dst = qkT_dram[bass.ds(a, 1), n, (u % 4) * P:(u % 4 + 1) * P, (u // 4) * HALF:(u // 4 + 1) * HALF][0]
                        else:
                            dst = v_dram[bass.ds(a, 1), u * P:(u + 1) * P, :][0]
                        pool.dma_start(dst, stage[:, u % 4, :]).then_inc(stored[u % 4], 16)
            for j in range(4):
                pool.wait_ge(stored[j], 16 * 2 * NW * UNITS // 4)

        @block.scalar
        def _(act):
            act.wait_ge(eps_set, 1)
            def turn(i):
                for j in range(XR):
                    act.wait_ge(x_in[j], 16 * i + 16)
                    act.wait_ge(x_scaled, XR * i)
                    nc.scalar.activation(sq[:, j, :], xt[:, j, :], ACT.Square, accum_out=ss[:, j:j + 1]).then_inc(squared, 1)
                act.wait_ge(squared, XR * i + XR)
                nc.scalar.activation(root[:, :], ss[:, :], ACT.Sqrt, scale=1.0 / D, bias=eps[:, 0:1]).then_inc(rooted, 1)

            turn(0)
            with act.Fori(1, NB // XR) as i:
                turn(i)
            for a in range(2):
                for n in range(NW):
                    for u in range(UNITS):
                        act.wait_ge(acc_full, a * NW * UNITS + n * UNITS + u + 1)
                        act.wait_ge(stored[u % 4], a * (16 * NW * 2) + 16 * (n * 2 + u // 4))
                        nc.scalar.activation(stage[:, u % 4, :], acc[:, u % 4, :], ACT.Copy,
                                             scale=float(HD) ** -0.5 if n == 0 else 1.0).then_inc(staged, 1)

        @block.vector
        def _(dve):
            nc.vector.memset(eps[:, :], EPS).then_inc(eps_set, 1)
            dve.wait_ge(g1_in, 16)
            def turn(i):
                dve.wait_ge(rooted, i + 1)
                nc.vector.reciprocal(rstd[:, :], root[:, :]).then_inc(rstd_set, 1)
                dve.wait_ge(rstd_set, i + 1)
                dve.wait_ge(x_turned, XR * i)
                for j in range(XR):
                    nc.vector.tensor_scalar(xs[:, j, :], xt[:, j, :], rstd[:, j:j + 1], None, ALU.mult).then_inc(x_scaled, 1)
                for j in range(XR):
                    dve.wait_ge(x_turned, XR * i + j + 1)
                    nc.vector.tensor_tensor(hT[:, :, bass.ds((i * XR + j) * P, P)], turned[:, j % 2, :, :],
                                            g1[:, :].unsqueeze(2).to_broadcast([P, NC, P]), ALU.mult).then_inc(h_set, 1)

            turn(0)
            with dve.Fori(1, NB // XR) as i:
                turn(i)

            dve.wait_ge(rel_in, 16)
            nc.vector.memset(ext[:, 0:EXT - NREL], 0.0).then_inc(ext_set, 1)
            nc.vector.tensor_copy(ext[:, EXT - NREL:], rel[:, :]).then_inc(ext_set, 1)
            dve.wait_ge(ext_set, 2)
            nc.vector.tensor_scalar(ext[:, 0:EXT - NREL], ext[:, 0:EXT - NREL], rel[:, 0:1], None, ALU.add).then_inc(ext_set, 1)

        @block.tensor
        def _(pe):
            def turn(i):
                for j in range(XR):
                    pe.wait_ge(x_scaled, XR * i + j + 1)
                    pe.wait_ge(h_set, XR * i + j - 1 if j >= 2 or not isinstance(i, int) else 0)
                    for c in range(NC):
                        mm = nc.tensor.transpose(turned[:, j % 2, c, :], xs[:, j, c * P:(c + 1) * P], ident[:, :])
                    mm.then_inc(x_turned, 1)

            turn(0)
            with pe.Fori(1, NB // XR) as i:
                turn(i)
            for a in range(2):
                for n in range(NW):
                    for u in range(UNITS):
                        if u == 0:
                            pe.wait_ge(w_loaded[n], 16 * a + 16)
                        pe.wait_ge(h_set, NB // 2 if u < 4 and n < 2 else NB)
                        back = n * UNITS + u - 4
                        pe.wait_ge(staged, a * NW * UNITS + back + 1 if back >= 0 else a * (NW * UNITS + back + 1))
                        for c in range(NC):
                            if n < 2:
                                lhs = w[:, n, c, (u % 4) * P:(u % 4 + 1) * P]
                                rhs = hT[:, c, (u // 4) * HALF:(u // 4 + 1) * HALF]
                            else:
                                lhs = hT[:, c, u * P:(u + 1) * P]
                                rhs = w[:, n, c, :]
                            mm = nc.tensor.matmul(acc[:, u % 4, :], lhs, rhs, start=(c == 0), stop=(c == NC - 1))
                        mm.then_inc(acc_full, 1)

def stick_breaking(nc, qkT_dram, v_dram, neg_suffix, neg_ones, ident, masked, oT_dram):
    LARGE = 30.0
    SLOTS = 6
    AHEAD = 4
    STEPS = [(t, j, max(0, j - 4 * t) * P) for t in range(2) for j in range(4 * t + 3, -1, -1)]
    NSTEP = 2 * len(STEPS)
    step = [(h, *STEPS[i]) for i in range(len(STEPS)) for h in range(2)]
    LAST = [n for n, (h, t, j, c0) in enumerate(step) if j == 0]
    with ExitStack() as ctx:
        def sb(name, shape, dt=F32):
            return ctx.enter_context(nc.sbuf_tensor(name, shape, dt))

        def sem(name):
            return ctx.enter_context(nc.semaphore(name))

        qk = sb("sb_qk", [HD, 2, 2, S])
        v = sb("sb_v", [P, 2, NB, HD])
        low = sb("sb_low", [P, SLOTS, HALF])
        soft = sb("sb_soft", [P, SLOTS, HALF])
        wts = sb("sb_wts", [P, SLOTS, HALF])
        total = sb("sb_total", [P, 2, HALF])
        out = sb("sb_out", [HD, 2, HALF])
        zeros = sb("sb_zeros", [P, P])
        z = ctx.enter_context(nc.psum_tensor("sb_z", [P, SLOTS, HALF], F32))
        o = ctx.enter_context(nc.psum_tensor("sb_o", [HD, 2, HALF], F32))

        head_in = [sem("sb_head_in0"), sem("sb_head_in1")]
        z_set, low_set, exp_set, log_set = sem("sb_z_set"), sem("sb_low_set"), sem("sb_exp"), sem("sb_log")
        soft_set, total_set, after_set = sem("sb_soft"), sem("sb_total"), sem("sb_after")
        wts_set, wts_used, o_set, o_copied = sem("sb_wts"), sem("sb_wts_used"), sem("sb_o"), sem("sb_copied")
        o_stored = [sem("sb_stored0"), sem("sb_stored1")]
        zeros_set = sem("sb_zeros_set")
        PAIRS = HEADS // 2

        block = ctx.enter_context(nc.Block())

        @block.sync
        def _(sp):
            def turn(i):
                for h in range(2):
                    sp.wait_ge(wts_used, NSTEP * i)
                    row = i * P + h * HD
                    for n in range(2):
                        sp.dma_start(qk[:, h, n, :], qkT_dram[0, n, bass.ds(row, HD), :]).then_inc(head_in[h], 16)
                    sp.dma_start(v[:, h, :, :], v_dram[0, :, bass.ds(row, HD)].rearrange("(b p) d -> p b d", p=P)).then_inc(head_in[h], 16)

            turn(0)
            with sp.Fori(1, PAIRS) as i:
                turn(i)

        @block.gpsimd
        def _(pool):
            nc.gpsimd.memset(zeros[:, :], 0.0).then_inc(zeros_set, 1)
            pool.wait_ge(zeros_set, 1)
            def turn(i):
                for n, (h, t, j, c0) in enumerate(step):
                    first = j == 4 * t + 3
                    if j > 0:
                        old = HALF if first else max(0, j + 1 - 4 * t) * P
                        pool.wait_ge(soft_set, NSTEP * i + n + 1)
                        pool.wait_ge(after_set, NSTEP * i + n + 1)
                        s = soft[:, n % SLOTS, :]
                        if old < HALF:
                            last = nc.gpsimd.tensor_tensor(total[:, h, old:], total[:, h, old:], s[:, old:], ALU.add)
                        if old > c0:
                            last = nc.gpsimd.tensor_tensor(total[:, h, c0:old], s[:, c0:old], zeros[:, :], ALU.add)
                        last.then_inc(total_set, 1)
                    if j == 0:
                        k = LAST.index(n)
                        pool.wait_ge(o_copied, 4 * i + k + 1)
                        pool.dma_start(oT_dram[0, bass.ds(i * P + h * HD, HD), t * HALF:(t + 1) * HALF],
                                       out[:, k % 2, :]).then_inc(o_stored[k % 2], 16)

            turn(0)
            with pool.Fori(1, PAIRS) as i:
                turn(i)
            for k in range(2):
                pool.wait_ge(o_stored[k], 16 * 2 * PAIRS)

        def adds_before(n):
            return sum(1 for (h, t, j, c0) in step[:n] if j > 0)

        TOTALS = adds_before(NSTEP)

        @block.tensor
        def _(pe):
            def scores(i, n):
                h, t, j, c0 = step[n]
                if n < 2:
                    pe.wait_ge(head_in[h], 48 * i + 48)
                pe.wait_ge(wts_set, NSTEP * i + n - SLOTS + 1 if n >= SLOTS else NSTEP * i)
                diag = j >= 4 * t
                mm = nc.tensor.matmul(z[:, n % SLOTS, c0:], qk[:, h, 1, j * P:(j + 1) * P],
                                      qk[:, h, 0, t * HALF + c0:(t + 1) * HALF], start=True, stop=True)
                if diag:
                    mm = nc.tensor.matmul(z[:, n % SLOTS, c0:c0 + P], ident[:, :], masked[:, :], start=False, stop=True,
                                          skip_group_check=True)
                mm.then_inc(z_set, 1)

            def after(i, n):
                h, t, j, c0 = step[n]
                pe.wait_ge(soft_set, NSTEP * i + n + 1)
                mm = nc.tensor.matmul(z[:, n % SLOTS, c0:], neg_suffix[:, :], soft[:, n % SLOTS, c0:],
                                      start=False, stop=True, skip_group_check=True)
                if j < 4 * t + 3:
                    old = max(0, j + 1 - 4 * t) * P
                    pe.wait_ge(total_set, TOTALS * i + adds_before(n - 1))
                    mm = nc.tensor.matmul(z[:, n % SLOTS, old:], neg_ones[:, :], total[:, h, old:],
                                          start=False, stop=True, skip_group_check=True)
                mm.then_inc(after_set, 1)

            def values(i, n):
                h, t, j, c0 = step[n]
                pe.wait_ge(wts_set, NSTEP * i + n + 1)
                if j == 4 * t + 3:
                    pe.wait_ge(o_copied, 4 * i + (h + 1 if t else 0))
                mm = nc.tensor.matmul(o[:, h, c0:], v[:, h, j, :], wts[:, n % SLOTS, c0:],
                                      start=(j == 4 * t + 3), stop=(j == 0), skip_group_check=True)
                mm.then_inc(wts_used, 1)

            def turn(i):
                for n in range(AHEAD):
                    scores(i, n)
                for n in range(NSTEP):
                    if n + AHEAD < NSTEP:
                        scores(i, n + AHEAD)
                    after(i, n)
                    if n >= 2:
                        values(i, n - 2)
                values(i, NSTEP - 2)
                values(i, NSTEP - 1)

            turn(0)
            with pe.Fori(1, PAIRS) as i:
                turn(i)

        @block.scalar
        def _(act):
            def log_part(i, n):
                h, t, j, c0 = step[n]
                act.wait_ge(low_set, NSTEP * i + n + 1)
                s = low[:, n % SLOTS, c0:]
                nc.scalar.activation(s, s, ACT.Exp).then_inc(exp_set, 1)
                act.wait_ge(exp_set, NSTEP * i + n + 1)
                nc.scalar.activation(s, s, ACT.Ln, bias=1.0).then_inc(log_set, 1)

            def weights(i, n):
                h, t, j, c0 = step[n]
                act.wait_ge(after_set, NSTEP * i + n + 1)
                if n >= SLOTS:
                    act.wait_ge(wts_used, NSTEP * i + n - SLOTS + 1)
                nc.scalar.activation(wts[:, n % SLOTS, c0:], z[:, n % SLOTS, c0:], ACT.Exp).then_inc(wts_set, 1)

            act.add_instruction(mybir.InstLoadActFuncSet(name=nc.get_next_instruction_name(), act_func_set_id=EXP_AND_LN))
            def turn(i):
                for n in range(3):
                    log_part(i, n)
                for n in range(NSTEP):
                    if n + 3 < NSTEP:
                        log_part(i, n + 3)
                    weights(i, n)

            turn(0)
            with act.Fori(1, PAIRS) as i:
                turn(i)

        @block.vector
        def _(dve):
            def limit(i, n):
                h, t, j, c0 = step[n]
                dve.wait_ge(z_set, NSTEP * i + n + 1)
                nc.vector.tensor_single_scalar(low[:, n % SLOTS, c0:], z[:, n % SLOTS, c0:], LARGE, ALU.min).then_inc(low_set, 1)

            def softplus(i, n):
                h, t, j, c0 = step[n]
                dve.wait_ge(log_set, NSTEP * i + n + 1)
                if n >= SLOTS:
                    dve.wait_ge(total_set, TOTALS * i + adds_before(n - SLOTS + 1))
                nc.vector.tensor_tensor(soft[:, n % SLOTS, c0:], z[:, n % SLOTS, c0:], low[:, n % SLOTS, c0:], ALU.max).then_inc(soft_set, 1)

            def copy_out(i, k):
                n = LAST[k]
                h, t, j, c0 = step[n]
                dve.wait_ge(wts_used, NSTEP * i + n + 1)
                dve.wait_ge(o_stored[k % 2], 32 * i + 16 * (k // 2))
                nc.vector.tensor_copy(out[:, k % 2, :], o[:, h, :]).then_inc(o_copied, 1)

            def turn(i):
                for n in range(AHEAD):
                    limit(i, n)
                softplus(i, 0)
                for n in range(NSTEP):
                    if n + 1 < NSTEP:
                        softplus(i, n + 1)
                    if n + AHEAD < NSTEP:
                        limit(i, n + AHEAD)
                    if n - 2 in LAST:
                        copy_out(i, LAST.index(n - 2))
                for k, n in enumerate(LAST):
                    if n + 2 >= NSTEP:
                        copy_out(i, k)

            turn(0)
            with dve.Fori(1, PAIRS) as i:
                turn(i)

def chunk_attention(nc, qkT_dram, v_dram, ident, bias_dram, oT_dram):
    SLOTS = 2
    step = [(h, qb, min(qb, 4) + 1) for qb in range(NB) for h in range(2)]
    NSTEP = len(step)
    PAIRS = HEADS // 2
    with ExitStack() as ctx:
        def sb(name, shape, dt=F32):
            return ctx.enter_context(nc.sbuf_tensor(name, shape, dt))

        def sem(name):
            return ctx.enter_context(nc.semaphore(name))

        qk = sb("ca_qk", [HD, 2, 2, S])
        v = sb("ca_v", [P, 2, NB, HD])
        bias = sb("ca_bias", [P, 2, BAND])
        prob = sb("ca_prob", [P, 4, BAND])
        probT = sb("ca_probT", [P, 2, 5, P])
        neg_top = sb("ca_neg_top", [P, 4])
        mass = sb("ca_mass", [P, 4])
        inv = sb("ca_inv", [P, 4])
        out = sb("ca_out", [HD, 2, HALF])
        s = ctx.enter_context(nc.psum_tensor("ca_s", [P, SLOTS, 2 * HALF], F32))
        turned = ctx.enter_context(nc.psum_tensor("ca_turned", [P, 2 * HALF], F32))
        o = ctx.enter_context(nc.psum_tensor("ca_o", [HD, 2, HALF], F32))

        head_in = [sem("ca_head_in0"), sem("ca_head_in1")]
        s_set, biased_set, neg_set = sem("ca_s_set"), sem("ca_biased"), sem("ca_neg")
        exp_set, inv_set, prob_set = sem("ca_exp"), sem("ca_inv"), sem("ca_prob")
        turned_set, probT_set, o_set, o_copied = sem("ca_turned"), sem("ca_probT"), sem("ca_o"), sem("ca_copied")
        o_stored = [sem("ca_stored0"), sem("ca_stored1")]

        block = ctx.enter_context(nc.Block())

        @block.sync
        def _(sp):
            def turn(i):
                for h in range(2):
                    sp.wait_ge(o_set, NSTEP * i)
                    row = i * P + h * HD
                    for n in range(2):
                        sp.dma_start(qk[:, h, n, :], qkT_dram[1, n, bass.ds(row, HD), :]).then_inc(head_in[h], 16)
                    sp.dma_start(v[:, h, :, :], v_dram[1, :, bass.ds(row, HD)].rearrange("(b p) d -> p b d", p=P)).then_inc(head_in[h], 16)
                    sp.dma_start(bias[:, h, :], bass.AP(tensor=bias_dram.tensor, offset=(2 * i + h) * (P * EXT) + P - 1,
                                                        ap=[[EXT - 1, P], [1, BAND]])).then_inc(head_in[h], 16)

            turn(0)
            with sp.Fori(1, PAIRS) as i:
                turn(i)

        @block.gpsimd
        def _(pool):
            def send(i, quad, h):
                pool.wait_ge(o_copied, 4 * i + 2 * quad + h + 1)
                pool.dma_start(oT_dram[1, bass.ds(i * P + h * HD, HD), quad * HALF:(quad + 1) * HALF],
                               out[:, h, :]).then_inc(o_stored[h], 16)

            def turn(i):
                for n in range(NSTEP):
                    h, qb, nk = step[n]
                    pool.wait_ge(inv_set, NSTEP * i + n + 1)
                    row = prob[:, n % 4, 0:nk * P]
                    nc.gpsimd.tensor_tensor(row, row, inv[:, n % 4:n % 4 + 1].to_broadcast([P, nk * P]), ALU.mult).then_inc(prob_set, 1)
                    if n in (12, 13):
                        send(i, 0, n - 12)
                send(i, 1, 0)
                send(i, 1, 1)

            turn(0)
            with pool.Fori(1, PAIRS) as i:
                turn(i)
            for h in range(2):
                pool.wait_ge(o_stored[h], 16 * 2 * PAIRS)

        @block.tensor
        def _(pe):
            def scores(i, n):
                h, qb, nk = step[n]
                if n < 2:
                    pe.wait_ge(head_in[h], 64 * i + 64)
                pe.wait_ge(biased_set, NSTEP * i + n - SLOTS + 1 if n >= SLOTS else NSTEP * i)
                k0, w = (qb - nk + 1) * P, nk * P
                for a in range(0, w, HALF):
                    b = min(w, a + HALF)
                    mm = nc.tensor.matmul(s[:, n % SLOTS, a:b], qk[:, h, 0, qb * P:(qb + 1) * P], qk[:, h, 1, k0 + a:k0 + b],
                                          start=True, stop=True)
                mm.then_inc(s_set, 1)

            def transpose_probs(i, n):
                h, qb, nk = step[n]
                pe.wait_ge(prob_set, NSTEP * i + n + 1)
                pe.wait_ge(probT_set, NSTEP * i + n)
                for b in range(nk):
                    mm = nc.tensor.transpose(turned[:, b * P:(b + 1) * P], prob[:, n % 4, b * P:(b + 1) * P], ident[:, :])
                mm.then_inc(turned_set, 1)

            def values(i, n):
                h, qb, nk = step[n]
                pe.wait_ge(probT_set, NSTEP * i + n + 1)
                if qb % 4 == 0:
                    pe.wait_ge(o_copied, 4 * i + (2 if qb else 0))
                for b in range(nk):
                    mm = nc.tensor.matmul(o[:, h, (qb % 4) * P:(qb % 4 + 1) * P], v[:, h, qb - nk + 1 + b, :], probT[:, n % 2, b, :],
                                          start=(b == 0), stop=(b == nk - 1))
                mm.then_inc(o_set, 1)

            def turn(i):
                for n in range(NSTEP + 3):
                    if n < NSTEP:
                        scores(i, n)
                    if 2 <= n < NSTEP + 2:
                        transpose_probs(i, n - 2)
                    if n >= 3:
                        values(i, n - 3)

            turn(0)
            with pe.Fori(1, PAIRS) as i:
                turn(i)

        @block.scalar
        def _(act):
            def turn(i):
                for n in range(NSTEP + 1):
                    if n < NSTEP:
                        h, qb, nk = step[n]
                        act.wait_ge(neg_set, NSTEP * i + n + 1)
                        nc.scalar.activation(prob[:, n % 4, 0:nk * P], prob[:, n % 4, 0:nk * P], ACT.Exp, bias=neg_top[:, n % 4:n % 4 + 1],
                                             accum_out=mass[:, n % 4:n % 4 + 1]).then_inc(exp_set, 1)
                    if n >= 1:
                        m = n - 1
                        h, qb, nk = step[m]
                        act.wait_ge(turned_set, NSTEP * i + m + 1)
                        act.wait_ge(o_set, NSTEP * i + m - 1 if m >= 2 else NSTEP * i)
                        nc.scalar.activation(probT[:, m % 2, 0:nk, :], turned[:, 0:nk * P].rearrange("p (b q) -> p b q", q=P),
                                             ACT.Copy).then_inc(probT_set, 1)

            turn(0)
            with act.Fori(1, PAIRS) as i:
                turn(i)

        @block.vector
        def _(dve):
            def biased(i, n):
                h, qb, nk = step[n]
                if n < 2:
                    dve.wait_ge(head_in[h], 64 * i + 64)
                dve.wait_ge(s_set, NSTEP * i + n + 1)
                dve.wait_ge(turned_set, NSTEP * i + n - 3 if n >= 4 else NSTEP * i)
                row = prob[:, n % 4, 0:nk * P]
                nc.vector.tensor_tensor(row, s[:, n % SLOTS, 0:nk * P], bias[:, h, BAND - nk * P:], ALU.add).then_inc(biased_set, 1)
                dve.wait_ge(biased_set, NSTEP * i + n + 1)
                nc.vector.tensor_reduce(neg_top[:, n % 4:n % 4 + 1], row, AX_X, ALU.max, negate=True).then_inc(neg_set, 1)

            def scaled(i, n):
                h, qb, nk = step[n]
                dve.wait_ge(exp_set, NSTEP * i + n + 1)
                nc.vector.reciprocal(inv[:, n % 4:n % 4 + 1], mass[:, n % 4:n % 4 + 1]).then_inc(inv_set, 1)

            def copy_out(i, k):
                quad, h = k // 2, k % 2
                dve.wait_ge(o_set, NSTEP * i + 8 * quad + 6 + h + 1)
                dve.wait_ge(o_stored[h], 32 * i + 16 * quad)
                nc.vector.tensor_copy(out[:, h, :], o[:, h, :]).then_inc(o_copied, 1)

            def turn(i):
                biased(i, 0)
                for n in range(NSTEP):
                    if n + 1 < NSTEP:
                        biased(i, n + 1)
                    scaled(i, n)
                    if n == 10:
                        copy_out(i, 0)
                        copy_out(i, 1)
                copy_out(i, 2)
                copy_out(i, 3)

            turn(0)
            with dve.Fori(1, PAIRS) as i:
                turn(i)

def gate_and_merge(nc, w_in, w_sb_proj, w_ca_proj, hT, oT_dram, mT_dram):
    GATES = 6 * WIDTH
    with ExitStack() as ctx:
        def sb(name, shape, dt=F32):
            return ctx.enter_context(nc.sbuf_tensor(name, shape, dt))

        def sem(name):
            return ctx.enter_context(nc.semaphore(name))

        oT = sb("oT", [P, 2, NCT, S])
        wg = sb("w_gate", [P, 2, 2, NC, P])
        wp = sb("w_branch", [P, 2, 2, NCT, P])
        gate = sb("gate", [P, 2, 2, HALF])
        part = sb("part", [P, 2, 2, HALF])
        merged = sb("merged", [P, 2, HALF])
        acc = ctx.enter_context(nc.psum_tensor("merge_acc", [P, 2, 4, HALF], F32))

        o_in = sem("o_in")
        w_loaded = [sem("gate_w0"), sem("gate_w1")]
        gates_full, branches_full = sem("gates_full"), sem("branches_full")
        gate_set, part_set, merged_set = sem("gate_set"), sem("part_set"), sem("merged_set")
        stored = [sem("merge_stored0"), sem("merge_stored1")]
        PAIRS = NC // 2

        w_cols = w_in[0].rearrange("(c p) n -> p c n", p=P)
        sb_cols = w_sb_proj[0].rearrange("(c p) n -> p c n", p=P)
        ca_cols = w_ca_proj[0].rearrange("(c p) n -> p c n", p=P)

        block = ctx.enter_context(nc.Block())

        @block.sync
        def _(sp):
            def turn(i):
                for j in range(2):
                    if not isinstance(i, int):
                        sp.wait_ge(branches_full, 4 * i - 2 + 2 * j)
                    col = (2 * i + j) * P
                    for a in range(2):
                        sp.dma_start(wg[:, j, a, :, :], w_cols[:, :, bass.ds(col + (GATES + a * D), P)]).then_inc(w_loaded[j], 16)
                    sp.dma_start(wp[:, j, 0, :, :], sb_cols[:, :, bass.ds(col, P)]).then_inc(w_loaded[j], 16)
                    sp.dma_start(wp[:, j, 1, :, :], ca_cols[:, :, bass.ds(col, P)]).then_inc(w_loaded[j], 16)

            turn(0)
            with sp.Fori(1, PAIRS) as i:
                turn(i)

        @block.gpsimd
        def _(pool):
            for a in range(2):
                pool.dma_start(oT[:, a, :, :], oT_dram[a].rearrange("(c p) t -> p c t", p=P)).then_inc(o_in, 16)
            def turn(i):
                for j in range(2):
                    for u in range(2):
                        pool.wait_ge(merged_set, 4 * i + 2 * j + u + 1)
                        pool.dma_start(mT_dram[bass.ds((2 * i + j) * P, P), u * HALF:(u + 1) * HALF], merged[:, u, :]).then_inc(stored[u], 16)

            turn(0)
            with pool.Fori(1, PAIRS) as i:
                turn(i)
            for u in range(2):
                pool.wait_ge(stored[u], 16 * NC)

        @block.tensor
        def _(pe):
            def turn(i):
                for j in range(2):
                    pe.wait_ge(w_loaded[j], 64 * i + 64)
                    for u in range(2):
                        cols = slice(u * HALF, (u + 1) * HALF)
                        n = 2 * j + u
                        pe.wait_ge(merged_set, 4 * i + n - 1 if n >= 2 else 4 * i)
                        for a in range(2):
                            for c in range(NC):
                                mm = nc.tensor.matmul(acc[:, u, a, :], wg[:, j, a, c, :], hT[:, c, cols], start=(c == 0), stop=(c == NC - 1))
                        mm.then_inc(gates_full, 1)
                        pe.wait_ge(o_in, 32)
                        for a in range(2):
                            for c in range(NCT):
                                mm = nc.tensor.matmul(acc[:, u, 2 + a, :], wp[:, j, a, c, :], oT[:, a, c, cols], start=(c == 0), stop=(c == NCT - 1))
                        mm.then_inc(branches_full, 1)

            turn(0)
            with pe.Fori(1, PAIRS) as i:
                turn(i)

        @block.scalar
        def _(act):
            def turn(i):
                for n in range(4):
                    u = n % 2
                    act.wait_ge(gates_full, 4 * i + n + 1)
                    act.wait_ge(merged_set, 4 * i + n - 1 if n >= 2 else 4 * i)
                    nc.scalar.activation(gate[:, u, :, :], acc[:, u, 0:2, :], ACT.Sigmoid).then_inc(gate_set, 1)

            turn(0)
            with act.Fori(1, PAIRS) as i:
                turn(i)

        @block.vector
        def _(dve):
            def turn(i):
                for n in range(4):
                    u = n % 2
                    dve.wait_ge(gate_set, 4 * i + n + 1)
                    dve.wait_ge(branches_full, 4 * i + n + 1)
                    dve.wait_ge(merged_set, 4 * i + n - 1 if n >= 2 else 4 * i)
                    nc.vector.tensor_tensor(part[:, u, :, :], gate[:, u, :, :], acc[:, u, 2:4, :], ALU.mult).then_inc(part_set, 1)
                    dve.wait_ge(part_set, 4 * i + n + 1)
                    dve.wait_ge(stored[u], 16 * (2 * i + n // 2))
                    nc.vector.tensor_tensor(merged[:, u, :], part[:, u, 0, :], part[:, u, 1, :], ALU.add).then_inc(merged_set, 1)

            turn(0)
            with dve.Fori(1, PAIRS) as i:
                turn(i)

def route_and_retrieve(nc, x, w_out, norm_ffn, w_query, keysT, expert_u, expert_v, norm_final, ident, mT_dram, out):
    RU = 4
    RV = 4
    SLOTS = NSEL
    QG = NS * NK // HALF
    GH = PH // QG
    GL = NS // QG
    GE = GH * TOPK
    with ExitStack() as ctx:
        def sb(name, shape, dt=F32):
            return ctx.enter_context(nc.sbuf_tensor(name, shape, dt))

        def sem(name):
            return ctx.enter_context(nc.semaphore(name))

        wo = sb("w_out_sb", [P, NC, D])
        wq = sb("w_query_sb", [P, NC, QG * HALF])
        keys = sb("keys", [P, NS, NK])
        g2 = sb("g2", [P, D])
        gf = sb("gf", [P, D])
        u_rows = sb("u_rows", [P, RU, D])
        v_rows = sb("v_rows", [P, RV, D])
        x1n, x1c = sb("x1_next", [P, D]), sb("x1_now", [P, D])
        h2n, h2c = sb("h2_next", [P, D]), sb("h2_now", [P, D])
        q = sb("query", [P, NS * NK])
        qT = sb("queryT", [P, NS, NK])
        scores = sb("scores", [P, NS, NK])
        scores2 = sb("scores2", [P, NS, NK])
        mblk = q[:, 0:D].rearrange("p (c t) -> p c t", t=P)
        h2T = scores2[:, NS - NC:, :]
        junk = scores2[:, 0:NC, :].rearrange("p a n -> p (a n)")
        cand = q[:, :].rearrange("p (h n) -> p h n", h=PH)
        cand2 = qT[:, :, :].rearrange("p (h a) n -> p h (a n)", a=2)
        hot = scores2[:, :, :].rearrange("p a (b i) -> p (a b) i", i=TOPK)
        diag = sb("diag", [P, RV, P])
        tv = sb("top_values", [P, NS, TOPK])
        ti = sb("top_index", [P, NS, TOPK], U32)
        bv = sb("best_values", [P, PH, TOPK])
        bp = sb("best_pos", [P, PH, TOPK], U32)
        bij = sb("best_ij", [P, 2, NSEL], U32)
        eij = sb("expert_ij", [P, 2, NSEL])
        iota = sb("iota", [P, TOPK])
        shifted = sb("shifted", [P, PH, TOPK])
        mass = sb("gate_mass", [P, PH])
        minv = sb("gate_inv", [P, PH])
        gate_n, gate_c = sb("gate_next", [P, NSEL]), sb("gate_now", [P, NSEL])
        idx_n, idx_c = sb("index_next", [P, NSEL], I32), sb("index_now", [P, NSEL], I32)
        dots = sb("dots", [P, NSEL])
        gel = sb("gelu", [P, NSEL])
        wts = sb("expert_wts", [P, NSEL])
        eps = sb("eps2", [P, 1])
        ss, root, rstd = sb("ss2", [P, 1]), sb("root2", [P, 1]), sb("rstd2", [P, 1])
        ssy, rooty, rstdy = sb("ssy", [P, 1]), sb("rooty", [P, 1]), sb("rstdy", [P, 1])
        front = ctx.enter_context(nc.psum_tensor("front", [P, 4, HALF], F32))
        sums = ctx.enter_context(nc.psum_tensor("sums", [P, 2, HALF], F32))

        wo_in = [sem("wo_in0"), sem("wo_in1")]
        g2_in, keys_in, gf_in, eps_set, iota_set = sem("g2_in"), sem("keys_in"), sem("gf_in"), sem("eps2_set"), sem("iota_set")
        m_in, x_in = sem("m_in"), sem("xb_in")
        wq_in = [sem(f"wq_in{i}") for i in range(QG)]
        unit_full, unit_taken = sem("unit_full"), sem("unit_taken")
        x1_set, sq_set, root_set, rstd_set, h2_set = sem("x1_set"), sem("sq2_set"), sem("root2_set"), sem("rstd2_set"), sem("h2_set")
        search = sem("search")
        shift_set, gexp_set, gate_set = sem("shift_set"), sem("gexp_set"), sem("gate_n_set")
        idx_set, idx_moved, gate_moved, now_set = sem("idx_set"), sem("idx_moved"), sem("gate_moved"), sem("now_set")
        u_in = [sem(f"u_in{i}") for i in range(RU)]
        v_in = [sem(f"v_in{i}") for i in range(RV)]
        dot_set, gel_set, wts_set, diag_set = sem("dot_set"), sem("gel_set"), sem("expert_wts_set"), sem("diag_set")
        v_free, y_set, ysq_set, yroot_set, yrstd_set, yout_set = (sem("v_free"), sem("y_set"), sem("ysq_set"), sem("yroot_set"),
                                                                  sem("yrstd_set"), sem("yout_set"))
        y_stored, search_passed, pool_passed = sem("y_stored"), sem("search_passed"), sem("pool_passed")

        x_rows = x.rearrange("a (b p) d -> (a b) p d", p=P)
        out_rows = out.rearrange("a (b p) d -> (a b) p d", p=P)
        wq_rows = w_query[0].rearrange("(c p) n -> p c n", p=P)

        def unit(u, b):
            bank = front[:, u % 4, :]
            if u < 2:
                if u == 0:
                    nc.tensor.wait_ge(m_in, 16 * b + 16)
                nc.tensor.wait_ge(unit_taken, 14 * b)
                nc.tensor.wait_ge(wo_in[u], 16)
                for c in range(NC):
                    mm = nc.tensor.matmul(bank, mblk[:, c, :], wo[:, c, u * HALF:(u + 1) * HALF], start=(c == 0), stop=(c == NC - 1))
            elif u < 4:
                nc.tensor.wait_ge(h2_set, b + 1)
                for c in range(4):
                    k = 4 * (u - 2) + c
                    mm = nc.tensor.transpose(bank[:, c * P:(c + 1) * P], h2n[:, k * P:(k + 1) * P], ident[:, :])
            elif (u - 4) % 3 == 0:
                nc.tensor.wait_ge(unit_taken, 14 * b + max(2, u - 5))
                g = (u - 4) // 3
                nc.tensor.wait_ge(wq_in[g], 16)
                for c in range(NC):
                    mm = nc.tensor.matmul(bank, h2T[:, c, :], wq[:, c, g * HALF:(g + 1) * HALF], start=(c == 0), stop=(c == NC - 1))
            else:
                nc.tensor.wait_ge(unit_taken, 14 * b + u - 2)
                for c in range(GL):
                    k = GL * ((u - 4) // 3) + c
                    if (u - 4) % 3 == 1:
                        mm = nc.tensor.transpose(bank[:, c * P:(c + 1) * P], q[:, k * P:(k + 1) * P], ident[:, :])
                    else:
                        nc.tensor.wait_ge(keys_in, 16)
                        mm = nc.tensor.matmul(bank[:, c * P:(c + 1) * P], qT[:, k, :], keys[:, k, :], start=True, stop=True)
            mm.then_inc(unit_full, 1)

        def take(u, b):
            nc.scalar.wait_ge(unit_full, 16 * b + u + 1)
            nc.scalar.wait_ge(idx_set, QG * b)
            g = (u - 4) // 3
            if u < 4:
                dst = h2T[:, 4 * (u - 2):4 * (u - 1), :]
            elif (u - 4) % 3 == 0:
                dst = q[:, g * HALF:(g + 1) * HALF]
            elif (u - 4) % 3 == 1:
                dst = qT[:, GL * g:GL * (g + 1), :]
            else:
                dst = scores[:, GL * g:GL * (g + 1), :]
            nc.scalar.activation(dst, front[:, u % 4, :], ACT.Copy).then_inc(unit_taken, 1)

        def search_norm_act(b):
            nc.scalar.wait_ge(x1_set, 2 * b + 2)
            nc.scalar.wait_ge(idx_set, QG * b - 2 if not isinstance(b, int) or b else 0)
            nc.scalar.activation(junk, x1n[:, :], ACT.Square, accum_out=ss[:, :]).then_inc(sq_set, 1)
            nc.scalar.wait_ge(sq_set, b + 1)
            nc.scalar.activation(root[:, :], ss[:, :], ACT.Sqrt, scale=1.0 / D, bias=eps[:, 0:1]).then_inc(root_set, 1)

        def search_x1(b, u):
            nc.vector.wait_ge(unit_full, 16 * b + u + 1)
            nc.vector.wait_ge(x_in, 16 * b + 16)
            cols = slice(u * HALF, (u + 1) * HALF)
            nc.vector.tensor_tensor(x1n[:, cols], front[:, u, :], x1n[:, cols], ALU.add).then_inc(x1_set, 1)

        def search_h2(b):
            nc.vector.wait_ge(root_set, b + 1)
            nc.vector.reciprocal(rstd[:, :], root[:, :]).then_inc(rstd_set, 1)
            nc.vector.wait_ge(rstd_set, b + 1)
            nc.vector.scalar_tensor_tensor(h2n[:, :], x1n[:, :], rstd[:, 0:1], g2[:, :], op0=ALU.mult, op1=ALU.mult).then_inc(h2_set, 1)

        LISTS, SUMS, PICK = 5 * GL, 5 * GL + 1, 5 * GL + 1 + 5 * GH
        NSEARCH = PICK + 10
        PIECES = 20

        def search_piece(b, g, piece):
            def after_step(n):
                nc.vector.wait_ge(search, QG * NSEARCH * b + NSEARCH * g + n)
                nc.vector.sem_inc(search_passed, 1)

            lists, heads, experts = slice(GL * g, GL * g + GL), slice(GH * g, GH * g + GH), slice(GE * g, GE * g + GE)
            if piece < 5:
                if piece == 0:
                    nc.vector.wait_ge(unit_taken, 14 * b + 5 + 3 * g)
                if piece == 2 and GL * g + GL > NS - NC:
                    nc.vector.wait_ge(unit_full, 16 * b + 14)
                if piece or g or not isinstance(b, int) or b:
                    after_step(piece * GL)
                for l in range(GL * g, GL * g + GL):
                    if piece == 0:
                        step = nc.vector.max(tv[:, l, 0:8], scores[:, l, :])
                    elif piece == 1:
                        step = nc.vector.max_index(ti[:, l, 0:8], tv[:, l, 0:8], scores[:, l, :])
                    elif piece == 2:
                        step = nc.vector.match_replace(scores2[:, l, :], tv[:, l, 0:8], scores[:, l, :], LOWEST)
                    elif piece == 3:
                        step = nc.vector.max(tv[:, l, 8:16], scores2[:, l, :])
                    else:
                        step = nc.vector.max_index(ti[:, l, 8:16], tv[:, l, 8:16], scores2[:, l, :])
                    step.then_inc(search, 1)
            elif piece == 5:
                after_step(LISTS)
                first = tv[:, lists, :][:, 0::2, :].unsqueeze(3).to_broadcast([P, GH, TOPK, TOPK])
                second = tv[:, lists, :][:, 1::2, :].unsqueeze(2).to_broadcast([P, GH, TOPK, TOPK])
                nc.vector.tensor_tensor(cand[:, heads, :].rearrange("p h (i j) -> p h i j", j=TOPK), first, second, ALU.add).then_inc(search, 1)
            elif piece < 11:
                rnd = piece - 6
                after_step(SUMS + rnd * GH)
                for h in range(GH * g, GH * g + GH):
                    if rnd == 0:
                        step = nc.vector.max(bv[:, h, 0:8], cand[:, h, :])
                    elif rnd == 1:
                        step = nc.vector.max_index(bp[:, h, 0:8], bv[:, h, 0:8], cand[:, h, :])
                    elif rnd == 2:
                        step = nc.vector.match_replace(cand2[:, h, :], bv[:, h, 0:8], cand[:, h, :], LOWEST)
                    elif rnd == 3:
                        step = nc.vector.max(bv[:, h, 8:16], cand2[:, h, :])
                    else:
                        step = nc.vector.max_index(bp[:, h, 8:16], bv[:, h, 8:16], cand2[:, h, :])
                    step.then_inc(search, 1)
            elif piece == 11:
                after_step(PICK)
                flat = bp[:, heads, :].rearrange("p h k -> p (h k)")
                nc.vector.tensor_single_scalar(bij[:, 0, experts], flat, 4, ALU.logical_shift_right).then_inc(search, 1)
                nc.vector.tensor_single_scalar(bij[:, 1, experts], flat, TOPK - 1, ALU.bitwise_and).then_inc(search, 1)
                nc.vector.tensor_tensor(shifted[:, heads, :], bv[:, heads, :], bv[:, heads, 0:1].to_broadcast([P, GH, TOPK]), ALU.subtract).then_inc(shift_set, 1)
            elif piece < 18:
                side, part = (piece - 12) // 3, (piece - 12) % 3
                after_step(PICK + 2 + piece - 12)
                rows = hot[:, experts, :]
                if part == 0:
                    pos = bij[:, side, experts].unsqueeze(2).to_broadcast([P, GE, TOPK])
                    nc.vector.tensor_tensor(rows, pos, iota[:, :].unsqueeze(1).to_broadcast([P, GE, TOPK]), ALU.is_equal).then_inc(search, 1)
                elif part == 1:
                    rows4 = rows.rearrange("p (h k) i -> p h k i", h=GH)
                    key = ti[:, lists, :][:, side::2, :].unsqueeze(2).to_broadcast([P, GH, TOPK, TOPK])
                    nc.vector.tensor_tensor(rows4, rows4, key, ALU.mult).then_inc(search, 1)
                else:
                    nc.vector.tensor_reduce(eij[:, side, experts], rows, AX_X, ALU.add).then_inc(search, 1)
            elif piece == 18:
                after_step(PICK + 8)
                nc.vector.wait_ge(idx_moved, QG * (b - 1) + g + 1 if not isinstance(b, int) or b else 0)
                nc.vector.scalar_tensor_tensor(idx_n[:, experts], eij[:, 0, experts], float(NK), eij[:, 1, experts],
                                               op0=ALU.mult, op1=ALU.add).then_inc(idx_set, 1)
                nc.vector.wait_ge(gexp_set, QG * b + g + 1)
                nc.vector.tensor_reduce(mass[:, heads], shifted[:, heads, :], AX_X, ALU.add).then_inc(search, 1)
                after_step(PICK + 9)
                nc.vector.reciprocal(minv[:, heads], mass[:, heads]).then_inc(search, 1)
            else:
                after_step(PICK + 10)
                nc.vector.tensor_tensor(gate_n[:, experts].rearrange("p (h k) -> p h k", h=GH), shifted[:, heads, :],
                                        minv[:, heads].unsqueeze(2).to_broadcast([P, GH, TOPK]), ALU.mult).then_inc(gate_set, 1)

        def search_exp(b, g):
            heads = slice(GH * g, GH * g + GH)
            nc.scalar.wait_ge(shift_set, QG * b + g + 1)
            nc.scalar.activation(shifted[:, heads, :], shifted[:, heads, :], ACT.Exp).then_inc(gexp_set, 1)

        UNIT_AT = [4, 12, 20, 22, 24, 30, 32, 36, 42, 44, 48, 54, 56, 60, 66, 68]
        GROUP_AT = [34, 55, 76, 97]

        def unit_at(s):
            return UNIT_AT.index(s) if s in UNIT_AT else None

        def search_dve(s, b):
            if s in (UNIT_AT[0] + 2, UNIT_AT[1] + 2):
                search_x1(b, 0 if s < UNIT_AT[1] else 1)
            if s == UNIT_AT[1] + 3:
                search_h2(b)
            for g in range(QG):
                if GROUP_AT[g] <= s < GROUP_AT[g] + PIECES:
                    search_piece(b, g, s - GROUP_AT[g])

        def search_act(s, b):
            if s == UNIT_AT[1] + 2:
                search_norm_act(b)
            u = unit_at(s - 1) if s else None
            if u is not None and u >= 2:
                take(u, b)
            for g in range(QG):
                if s == GROUP_AT[g] + 14:
                    search_exp(b, g)

        def late_dve(s):
            for k in (2 * s, 2 * s + 1):
                if k < 2 * PIECES:
                    search_piece(0, 2 + k // PIECES, k % PIECES)

        def late_act(s):
            for g in range(2):
                if s == (g * PIECES + 12) // 2:
                    search_exp(0, 2 + g)

        block = ctx.enter_context(nc.Block())

        @block.sync
        def _(sp):
            def search_block(b):
                sp.wait_ge(unit_full, 16 * b)
                sp.wait_ge(idx_set, QG * b - 2 if not isinstance(b, int) else 0)
                sp.dma_start(mblk, mT_dram.rearrange("(c p) t -> p c t", p=P)[:, :, bass.ds(b * P, P)]).then_inc(m_in, 16)
                sp.wait_ge(now_set, 2 * b)
                sp.dma_start(x1n[:, :], x_rows[bass.ds(b, 1)][0]).then_inc(x_in, 16)

            for a in range(2):
                sp.dma_start(wo[:, :, a * HALF:(a + 1) * HALF], w_out[0].rearrange("(c p) n -> p c n", p=P)[:, :, a * HALF:(a + 1) * HALF]).then_inc(wo_in[a], 16)
                if a == 0:
                    search_block(0)
            sp.dma_start(g2[:, :], norm_ffn.to_broadcast([P, D])).then_inc(g2_in, 16)
            for g in range(QG):
                sp.dma_start(wq[:, :, g * HALF:(g + 1) * HALF], wq_rows[:, :, g * HALF:(g + 1) * HALF]).then_inc(wq_in[g], 16)
            sp.dma_start(keys[:, :, :], keysT).then_inc(keys_in, 16)
            sp.dma_start(gf[:, :], norm_final.rearrange("(a d) -> a d", a=1).to_broadcast([P, D])).then_inc(gf_in, 16)

            with sp.Fori(1, NB) as b:
                search_block(b)

        @block.gpsimd
        def _(pool):
            nc.gpsimd.iota(iota[:, :], [[1, TOPK]], base=0, channel_multiplier=0,
                           allow_small_or_imprecise_dtypes=True).then_inc(iota_set, 1)

            def gather_u(index, col, n, b):
                if b is not None:
                    pool.wait_ge(dot_set, SLOTS * b + n - RU + 1)
                    pool.sem_inc(pool_passed, 1)
                elif n >= RU:
                    pool.wait_ge(dot_set, n - RU + 1)
                pool.indirect_dma_start(u_rows[:, n % RU, :], None, expert_u[0], bass.IndirectOffsetOnAxis(index[:, col:col + 1], 0)).then_inc(u_in[n % RU], 16)

            def gather_v(n, b):
                pool.wait_ge(v_free, SLOTS * b + n + 1)
                pool.sem_inc(pool_passed, 1)
                pool.indirect_dma_start(v_rows[:, n % RV, :], None, expert_v[0], bass.IndirectOffsetOnAxis(idx_c[:, n:n + 1], 0)).then_inc(v_in[n % RV], 16)

            def retrieve(b, last):
                def move_indices(g):
                    if not isinstance(b, int) or b:
                        for n in range(RU):
                            pool.wait_ge(u_in[n], 16 * (SLOTS // RU) * (b - 1) + 16 * (GE // RU) * (g + 1))
                        for n in range(RV):
                            pool.wait_ge(v_in[n], 16 * (SLOTS // RV) * (b - 1) + 16 * (GE // RV) * (g + 1))
                    pool.wait_ge(idx_set, QG * b + g + 1)
                    pool.sem_inc(pool_passed, 1)
                    experts = slice(GE * g, GE * g + GE)
                    nc.gpsimd.tensor_copy(idx_c[:, experts], idx_n[:, experts]).then_inc(idx_moved, 1)
                    pool.wait_ge(idx_moved, QG * b + g + 1)
                    pool.sem_inc(pool_passed, 1)

                for s in range(SLOTS):
                    for g in range(QG):
                        if s == max(0, GE * g - TOPK):
                            move_indices(g)
                    if s + TOPK < SLOTS:
                        gather_u(idx_c, s + TOPK, s + TOPK, b)
                    elif not last:
                        if s + TOPK == SLOTS:
                            pool.wait_ge(idx_set, QG * (b + 1) + 1)
                        gather_u(idx_n, s + TOPK - SLOTS, s + TOPK, b)
                    gather_v(s, b)

            pool.wait_ge(idx_set, 1)
            for n in range(TOPK):
                gather_u(idx_n, n, n, None)
            retrieve(0, False)
            with pool.Fori(1, NB - 1) as b:
                retrieve(b, False)
            retrieve(NB - 1, True)

        @block.tensor
        def _(pe):
            pe.sem_inc(v_free, RV)
            for u in range(16):
                unit(u, 0)

            def retrieve(b, last):
                for s in range(SLOTS):
                    if s == 0:
                        pe.wait_ge(y_set, b)
                    pe.wait_ge(diag_set, SLOTS * b + s + 1)
                    pe.wait_ge(v_in[s % RV], 16 * (SLOTS // RV) * b + 16 * (s // RV + 1))
                    for a in range(2):
                        mm = nc.tensor.matmul(sums[:, a, :], diag[:, s % RV, :], v_rows[:, s % RV, a * HALF:(a + 1) * HALF],
                                              start=(s == 0), stop=(s == SLOTS - 1))
                    mm.then_inc(v_free, 1)
                    if not last and unit_at(s) is not None:
                        unit(unit_at(s), b + 1)

            retrieve(0, False)
            with pe.Fori(1, NB - 1) as b:
                retrieve(b, False)
            retrieve(NB - 1, True)

        @block.scalar
        def _(act):
            act.wait_ge(eps_set, 1)
            search_norm_act(0)
            for u in range(2, 16):
                take(u, 0)
                if u == 9:
                    search_exp(0, 0)

            def gelu(h, b):
                act.wait_ge(dot_set, SLOTS * b + TOPK * h + TOPK)
                hs = slice((h % PH) * TOPK, (h % PH) * TOPK + TOPK)
                nc.scalar.activation(gel[:, hs], dots[:, hs], ACT.Gelu).then_inc(gel_set, 1)

            def finish(b):
                act.wait_ge(y_set, b + 1)
                act.wait_ge(idx_set, min(QG * (b + 2), QG * NB) if isinstance(b, int) else QG * (b + 2))
                nc.scalar.activation(junk, x1c[:, :], ACT.Square, accum_out=ssy[:, :]).then_inc(ysq_set, 1)
                act.wait_ge(ysq_set, b + 1)
                nc.scalar.activation(rooty[:, :], ssy[:, :], ACT.Sqrt, scale=1.0 / D, bias=eps[:, 0:1]).then_inc(yroot_set, 1)
                act.wait_ge(yout_set, b + 1)
                act.dma_start(out_rows[bass.ds(b, 1)][0] if not isinstance(b, int) else out_rows[b], x1c[:, :]).then_inc(y_stored, 16)

            def retrieve(b, last):
                for s in range(SLOTS):
                    if s % TOPK == 0:
                        act.wait_ge(wts_set, PH * b + s // TOPK + 1)
                    act.wait_ge(v_free, SLOTS * b + s + 1)
                    nc.scalar.activation(diag[:, s % RV, :], ident[:, :], ACT.Copy, scale=wts[:, s:s + 1]).then_inc(diag_set, 1)
                    if s % TOPK == TOPK - 1 and not (last and s == SLOTS - 1):
                        gelu(s // TOPK + 1, b)
                    if isinstance(b, int) and b == 0:
                        late_act(s)
                    if not last:
                        search_act(s, b + 1)
                finish(b)

            search_exp(0, 1)
            gelu(0, 0)
            retrieve(0, False)
            with act.Fori(1, NB - 1) as b:
                retrieve(b, False)
            retrieve(NB - 1, True)
            act.wait_ge(y_stored, 16 * NB)

        @block.vector
        def _(dve):
            nc.vector.memset(eps[:, :], EPS).then_inc(eps_set, 1)
            dve.wait_ge(g2_in, 16)
            dve.wait_ge(iota_set, 1)
            for u in range(2):
                search_x1(0, u)
            search_h2(0)
            for piece in range(PIECES):
                search_piece(0, 0, piece)

            def dot(n, h2, b):
                row = u_rows[:, n % RU, :]
                dve.wait_ge(u_in[n % RU], 16 * (SLOTS // RU) * b + 16 * (n // RU + 1))
                nc.vector.tensor_tensor_reduce(row, row, h2, 1.0, 0.0, ALU.mult, ALU.add,
                                               dots[:, n % SLOTS:n % SLOTS + 1]).then_inc(dot_set, 1)

            def weigh(h, gate, b):
                dve.wait_ge(gel_set, PH * b + h + 1)
                hs = slice((h % PH) * TOPK, (h % PH) * TOPK + TOPK)
                if h:
                    dve.wait_ge(diag_set, SLOTS * b + TOPK * (h - PH + 1) if h >= PH else SLOTS * b)
                nc.vector.tensor_tensor(wts[:, hs], gel[:, hs], gate[:, hs], ALU.mult).then_inc(wts_set, 1)

            def retrieve(b, last):
                dve.wait_ge(dot_set, SLOTS * b + TOPK)
                nc.vector.tensor_copy(h2c[:, :], h2n[:, :]).then_inc(now_set, 1)
                dve.wait_ge(now_set, 2 * b + 1)
                for s in range(SLOTS):
                    for g in range(QG):
                        if s == max(0, GE * g - 2):
                            dve.wait_ge(wts_set, PH * b + max(1, 2 * g))
                            dve.wait_ge(gate_set, QG * b + g + 1)
                            experts = slice(GE * g, GE * g + GE)
                            nc.vector.tensor_copy(gate_c[:, experts], gate_n[:, experts]).then_inc(gate_moved, 1)
                    if s == 1:
                        dve.wait_ge(y_stored, 16 * b)
                        nc.vector.tensor_copy(x1c[:, :], x1n[:, :]).then_inc(now_set, 1)
                    n = s + TOPK
                    if n < SLOTS:
                        dot(n, h2c[:, :], b)
                    elif not last:
                        dot(n, h2n[:, :], b)
                    if isinstance(b, int) and b == 0:
                        late_dve(s)
                    if not last:
                        search_dve(s, b + 1)
                    if n % TOPK == TOPK - 1:
                        if n < SLOTS:
                            dve.wait_ge(gate_moved, QG * b + n // GE + 1)
                            weigh(n // TOPK, gate_c, b)
                        elif not last:
                            dve.wait_ge(gate_set, QG * (b + 1) + 1)
                            weigh(n // TOPK, gate_n, b)
                dve.wait_ge(now_set, 2 * b + 2)
                dve.wait_ge(v_free, SLOTS * b + SLOTS + RV)
                nc.vector.tensor_tensor(x1c[:, :], sums[:, :, :].rearrange("p a n -> p (a n)"), x1c[:, :], ALU.add).then_inc(y_set, 1)
                dve.wait_ge(yroot_set, b + 1)
                nc.vector.reciprocal(rstdy[:, :], rooty[:, :]).then_inc(yrstd_set, 1)
                dve.wait_ge(yrstd_set, b + 1)
                dve.wait_ge(gf_in, 16)
                nc.vector.scalar_tensor_tensor(x1c[:, :], x1c[:, :], rstdy[:, 0:1], gf[:, :], op0=ALU.mult, op1=ALU.mult).then_inc(yout_set, 1)

            for piece in range(PIECES):
                if piece < TOPK:
                    dot(piece, h2n[:, :], 0)
                search_piece(0, 1, piece)
            dve.wait_ge(gate_set, 1)
            weigh(0, gate_n, 0)
            retrieve(0, False)
            with dve.Fori(1, NB - 1) as b:
                retrieve(b, False)
            retrieve(NB - 1, True)


def constants(nc, ident, neg_suffix, neg_ones, masked):
    with ExitStack() as ctx:
        filled = ctx.enter_context(nc.semaphore("filled"))
        block = ctx.enter_context(nc.Block())

        @block.gpsimd
        def _(pool):
            nc.gpsimd.memset(ident[:, :], 0.0).then_inc(filled, 1)
            nc.gpsimd.memset(neg_ones[:, :], -1.0).then_inc(filled, 1)
            nc.gpsimd.memset(neg_suffix[:, :], -1.0).then_inc(filled, 1)
            nc.gpsimd.memset(masked[:, :], MASKED).then_inc(filled, 1)
            pool.wait_ge(filled, 4)
            nc.gpsimd.affine_select(out=ident[:, :], in_=ident[:, :], compare_op=ALU.not_equal, fill=1.0,
                                    base=0, pattern=[[-1, P]], channel_multiplier=1)
            nc.gpsimd.affine_select(out=neg_suffix[:, :], in_=neg_suffix[:, :], compare_op=ALU.is_ge, fill=0.0,
                                    base=0, pattern=[[-1, P]], channel_multiplier=1)
            nc.gpsimd.affine_select(out=masked[:, :], in_=masked[:, :], compare_op=ALU.is_ge, fill=0.0,
                                    base=0, pattern=[[-1, P]], channel_multiplier=1)


def program(nc, x, norm_mix, w_in, w_sb_proj, w_ca_proj, rel_reversed, w_out, norm_ffn, w_query, keysT,
            expert_u, expert_v, norm_final, out):
    def dram(name, shape):
        return nc.dram_tensor(name, shape, F32, kind="Internal").ap()

    qkT_dram = dram("qkT_dram", [2, 2, WIDTH, S])
    v_dram = dram("v_dram", [2, S, WIDTH])
    oT_dram = dram("oT_dram", [2, WIDTH, S])
    mT_dram = dram("mT_dram", [D, S])
    ext_dram = dram("ext_dram", [HEADS, EXT])
    bias_dram = dram("bias_dram", [HEADS, P, EXT])
    with ExitStack() as ctx:
        ident, neg_suffix, neg_ones, masked = (ctx.enter_context(nc.sbuf_tensor(n, [P, P], F32))
                                               for n in ("ident", "neg_suffix", "neg_ones", "masked"))
        constants(nc, ident, neg_suffix, neg_ones, masked)
        with nc.sbuf_tensor("hT", [P, NC, S], F32) as hT:
            normalise_and_project(nc, x, norm_mix, w_in, rel_reversed, ident, hT, qkT_dram, v_dram, ext_dram, bias_dram)
            stick_breaking(nc, qkT_dram, v_dram, neg_suffix, neg_ones, ident, masked, oT_dram)
            chunk_attention(nc, qkT_dram, v_dram, ident, bias_dram, oT_dram)
            gate_and_merge(nc, w_in, w_sb_proj, w_ca_proj, hT, oT_dram, mT_dram)
        route_and_retrieve(nc, x, w_out, norm_ffn, w_query, keysT, expert_u, expert_v, norm_final, ident, mT_dram, out)


_INS = ["x", "norm_mix", "w_in", "w_sb_proj", "w_ca_proj", "ca_rel_bias", "w_out", "norm_ffn", "peer_w_query",
        "peer_sub_keys", "peer_u", "peer_v", "norm_final"]


def kernel(**inputs):
    import numpy as np
    import concourse.bacc as bacc
    from concourse.bass_utils import run_bass_kernel_spmd

    nc = bacc.Bacc("TRN2", target_bir_lowering=False, num_devices=1)
    arrays, args = {}, []
    for name in _INS:
        a = np.asarray(inputs[name])
        if name == "ca_rel_bias":
            a = a[0, :, ::-1]
        if name == "peer_sub_keys":
            a = a[0].transpose(3, 0, 1, 2).reshape(P, NS, NK)
        a = np.ascontiguousarray(a)
        arrays[f"in_{name}"] = a
        args.append(nc.dram_tensor(f"in_{name}", a.shape, mybir.dt.from_np(a.dtype), kind="ExternalInput").ap())
    args.append(nc.dram_tensor("out_y", (1, S, D), F32, kind="ExternalOutput").ap())
    program(nc, *args)
    return run_bass_kernel_spmd(nc, [arrays], core_ids=[0]).results[0]["out_y"]
```

```python
from contextlib import ExitStack

import concourse.bass as bass
from concourse import mybir

ALU = mybir.AluOpType
ACT = mybir.ActivationFunctionType
F32 = mybir.dt.float32
F32R = mybir.dt.float32r
I32 = mybir.dt.int32
U32 = mybir.dt.uint32
AX_X = mybir.AxisListType.X

P = 128
D = 1024
S = 1024
NB = S // P
NC = D // P
HD = 64
HEADS = 8
WIDTH = HEADS * HD
NCT = WIDTH // P
HALF = 512
EPS = 1e-6
MASKED = -1e30
CHUNK = 64
LOWEST = -3.0e38
BAND = 5 * P
REL = 128
NREL = 2 * REL + 1
EXT = BAND + P
PH = 8
NK = 128
NS = 2 * PH
TOPK = 16
EXP_AND_LN = 6
NSEL = PH * TOPK


def split_matmul(nc, acc, hi, lo, rhs_hi, rhs_lo, first, last):
    nc.tensor.matmul(acc, hi, rhs_hi, start=first, stop=False)
    nc.tensor.matmul(acc, hi, rhs_lo, start=False, stop=False)
    return nc.tensor.matmul(acc, lo, rhs_hi, start=False, stop=last)


def normalise_and_project(nc, x, norm_mix, w_in, rel_reversed, ident, h_hi, h_lo, qkT_dram, v_dram, ext_dram, bias_dram):
    XR = 4
    COLS = HALF // 2
    RAW = 3
    PER_ATT = 3 * WIDTH // COLS
    CHUNKS = 2 * PER_ATT
    UNITS = 4
    with ExitStack() as ctx:
        def sb(name, shape, dt=F32):
            return ctx.enter_context(nc.sbuf_tensor(name, shape, dt))

        def sem(name):
            return ctx.enter_context(nc.semaphore(name))

        xt = sb("xt", [P, XR, D])
        xs = sb("xs", [P, XR, D])
        sq = sb("sq", [P, XR, D])
        ss = sb("ss", [P, XR])
        root = sb("root", [P, XR])
        rstd = sb("rstd", [P, XR])
        eps = sb("eps", [P, 1])
        g1 = sb("g1", [P, NC])
        h = sb("h_whole", [P, 2, NC, P])
        w = sb("w_qkv", [P, RAW, NC, COLS])
        w_hi = sb("w_qkv_hi", [P, 2, NC, COLS], F32R)
        w_lo = sb("w_qkv_lo", [P, 2, NC, COLS], F32R)
        rel = sb("ca_rel", [HEADS, NREL])
        ext = sb("ca_ext", [HEADS, EXT])
        hidden = sb("ca_hidden", [CHUNK, HEADS, CHUNK])
        stage = sb("proj_stage", [P, UNITS, HALF])
        stage_lo = sq[:, :, 0:HALF]
        turned = ctx.enter_context(nc.psum_tensor("turned", [P, 2, NC, P], F32))
        acc = ctx.enter_context(nc.psum_tensor("proj_acc", [P, UNITS, HALF], F32))

        x_in = [sem(f"x_in{i}") for i in range(XR)]
        g1_in, eps_set = sem("g1_in"), sem("eps_set")
        squared, rooted, rstd_set, x_scaled = sem("squared"), sem("rooted"), sem("rstd_set"), sem("x_scaled")
        x_turned, h_set, h_hi_set, h_lo_set = sem("x_turned"), sem("h_set"), sem("h_hi_set"), sem("h_lo_set")
        w_loaded = [sem(f"w_loaded{i}") for i in range(RAW)]
        w_hi_set, w_lo_set = sem("w_hi_set"), sem("w_lo_set")
        acc_full, staged, rest_staged = sem("acc_full"), sem("staged"), sem("rest_staged")
        stored = [sem(f"stored{i}") for i in range(UNITS)]
        rest_stored = [sem(f"rest_stored{i}") for i in range(UNITS)]
        rel_in, ext_set, ext_out, window_out, hidden_set = sem("rel_in"), sem("ext_set"), sem("ext_out"), sem("window_out"), sem("hidden_set")

        x_rows = x.rearrange("a (b p) d -> (a b) p d", p=P)
        w_rows = w_in[0].rearrange("(c p) n -> p c n", p=P)

        def window(row, column):
            return bass.AP(tensor=bias_dram.tensor, offset=row * (EXT - 1) + column + P - 1,
                           ap=[[EXT - 1, CHUNK], [P * EXT, HEADS], [1, CHUNK]])

        def is_v(k):
            return k % PER_ATT >= 4

        def scale(k):
            return float(HD) ** -0.5 if k % PER_ATT < 2 else 1.0

        def rests(k):
            return sum(not is_v(m) for m in range(k))

        block = ctx.enter_context(nc.Block())

        @block.sync
        def _(sp):
            def load_w(k):
                if k >= RAW:
                    sp.wait_ge(w_lo_set, k - RAW + 1)
                sp.dma_start(w[:, k % RAW, :, :], w_rows[:, :, k * COLS:(k + 1) * COLS]).then_inc(w_loaded[k % RAW], 16)

            for j in range(XR):
                sp.dma_start(xt[:, j, :], x_rows[j]).then_inc(x_in[j], 16)
            sp.dma_start(g1[:, :], norm_mix[0].rearrange("(c p) -> p c", p=P), allow_slow_non_contiguous=True).then_inc(g1_in, 16)
            for k in range(2):
                load_w(k)
            for j in range(XR):
                sp.wait_ge(x_scaled, j + 1)
                sp.dma_start(xt[:, j, :], x_rows[XR + j]).then_inc(x_in[j], 16)
            for k in range(2, 5):
                load_w(k)
            sp.dma_start(rel[:, :], rel_reversed).then_inc(rel_in, 16)
            sp.wait_ge(ext_set, 3)
            sp.dma_start(ext_dram, ext[:, :]).then_inc(ext_out, 16)
            sp.wait_ge(ext_out, 16)
            for head in range(HEADS):
                sp.dma_start(bias_dram[head], ext_dram[head:head + 1, :].to_broadcast([P, EXT])).then_inc(window_out, 16)
            sp.wait_ge(window_out, 16 * HEADS)
            sp.wait_ge(hidden_set, 1)
            sp.dma_start(window(0, BAND - CHUNK), hidden[:, :, :]).then_inc(window_out, 16)
            sp.dma_start(window(CHUNK, 0), hidden[:, :, :]).then_inc(window_out, 16)
            sp.wait_ge(window_out, 16 * (HEADS + 2))
            for k in range(5, CHUNKS):
                load_w(k)

        @block.gpsimd
        def _(pool):
            nc.gpsimd.memset(hidden[:, :, :], MASKED).then_inc(hidden_set, 1)
            for k in range(CHUNKS):
                a, n, part = k // PER_ATT, k % PER_ATT // 2, k % 2
                for u in range(UNITS):
                    pool.wait_ge(staged, k * UNITS + u + 1)
                    if n < 2:
                        row = part * COLS + u % 2 * P
                        dst = qkT_dram[a, n, :, row:row + P, (u // 2) * HALF:(u // 2 + 1) * HALF]
                        pool.dma_start(dst[0], stage[:, u, :]).then_inc(stored[u], 16)
                        pool.wait_ge(rest_staged, rests(k) * UNITS + u + 1)
                        pool.dma_start(dst[1], stage_lo[:, u, :]).then_inc(rest_stored[u], 16)
                    else:
                        pool.dma_start(v_dram[a, 2 * u * P:2 * (u + 1) * P, part * COLS:(part + 1) * COLS].rearrange("(t p) d -> p t d", p=P),
                                       stage[:, u, :].rearrange("p (t d) -> p t d", t=2)).then_inc(stored[u], 16)
            for u in range(UNITS):
                pool.wait_ge(stored[u], 16 * CHUNKS)
                pool.wait_ge(rest_stored[u], 16 * rests(CHUNKS))

        @block.scalar
        def _(act):
            act.wait_ge(eps_set, 1)

            def split_w(k):
                act.wait_ge(w_loaded[k % RAW], 16 * (k // RAW + 1))
                if k >= 2:
                    act.wait_ge(acc_full, (k - 1) * UNITS)
                nc.scalar.activation(w_hi[:, k % 2, :, :], w[:, k % RAW, :, :], ACT.Copy).then_inc(w_hi_set, 1)

            def mean_square(i):
                for j in range(XR):
                    act.wait_ge(x_in[j], 16 * i + 16)
                    act.wait_ge(x_scaled, XR * i)
                    nc.scalar.activation(sq[:, j, :], xt[:, j, :], ACT.Square, accum_out=ss[:, j:j + 1]).then_inc(squared, 1)
                act.wait_ge(squared, XR * i + XR)
                nc.scalar.activation(root[:, :], ss[:, :], ACT.Sqrt, scale=1.0 / D, bias=eps[:, 0:1]).then_inc(rooted, 1)

            def hi_of_h(b):
                act.wait_ge(h_set, b + 1)
                nc.scalar.activation(h_hi[:, :, b * P:(b + 1) * P], h[:, b % 2, :, :], ACT.Copy).then_inc(h_hi_set, 1)

            mean_square(0)
            hi_of_h(0)
            hi_of_h(1)
            mean_square(1)
            hi_of_h(2)
            hi_of_h(3)
            split_w(0)
            for b in range(4, NB):
                hi_of_h(b)
            split_w(1)
            for k in range(CHUNKS):
                for u in range(UNITS):
                    act.wait_ge(acc_full, k * UNITS + u + 1)
                    act.wait_ge(stored[u], 16 * k)
                    dst = stage[:, u, :] if is_v(k) else stage[:, u, :].bitcast(F32R)
                    if not is_v(k) and k:
                        act.wait_ge(rest_staged, (rests(k) - 1) * UNITS + u + 1)
                    nc.scalar.activation(dst, acc[:, u, :], ACT.Copy, scale=scale(k)).then_inc(staged, 1)
                    if u == 0 and 1 <= k < CHUNKS - 1:
                        split_w(k + 1)

        @block.vector
        def _(dve):
            nc.vector.memset(eps[:, :], EPS).then_inc(eps_set, 1)

            def rest_of_w(k):
                dve.wait_ge(w_hi_set, k + 1)
                nc.vector.tensor_tensor(w_lo[:, k % 2, :, :], w[:, k % RAW, :, :], w_hi[:, k % 2, :, :].bitcast(F32),
                                        ALU.subtract).then_inc(w_lo_set, 1)

            def scale_x(i):
                dve.wait_ge(rooted, i + 1)
                nc.vector.reciprocal(rstd[:, :], root[:, :]).then_inc(rstd_set, 1)
                dve.wait_ge(rstd_set, i + 1)
                dve.wait_ge(x_turned, XR * i)
                for j in range(XR):
                    nc.vector.tensor_scalar(xs[:, j, :], xt[:, j, :], rstd[:, j:j + 1], None, ALU.mult).then_inc(x_scaled, 1)

            def whole_h(b):
                dve.wait_ge(x_turned, b + 1)
                if b >= 2:
                    dve.wait_ge(h_lo_set, b - 1)
                nc.vector.tensor_tensor(h[:, b % 2, :, :], turned[:, b % 2, :, :],
                                        g1[:, :].unsqueeze(2).to_broadcast([P, NC, P]), ALU.mult).then_inc(h_set, 1)

            def rest_of_h(b):
                tokens = slice(b * P, (b + 1) * P)
                dve.wait_ge(h_hi_set, b + 1)
                nc.vector.tensor_tensor(h_lo[:, :, tokens], h[:, b % 2, :, :], h_hi[:, :, tokens].bitcast(F32), ALU.subtract).then_inc(h_lo_set, 1)

            scale_x(0)
            dve.wait_ge(g1_in, 16)
            whole_h(0)
            for b in range(1, 4):
                whole_h(b)
                rest_of_h(b - 1)
            scale_x(1)
            rest_of_h(3)
            whole_h(4)
            rest_of_w(0)
            for b in range(5, NB):
                whole_h(b)
                rest_of_h(b - 1)
            rest_of_h(NB - 1)
            rest_of_w(1)

            dve.wait_ge(rel_in, 16)
            nc.vector.memset(ext[:, 0:EXT - NREL], 0.0).then_inc(ext_set, 1)
            nc.vector.tensor_copy(ext[:, EXT - NREL:], rel[:, :]).then_inc(ext_set, 1)
            dve.wait_ge(ext_set, 2)
            nc.vector.tensor_scalar(ext[:, 0:EXT - NREL], ext[:, 0:EXT - NREL], rel[:, 0:1], None, ALU.add).then_inc(ext_set, 1)
            for k in range(CHUNKS):
                for u in range(UNITS):
                    if u == 1 and 1 <= k < CHUNKS - 1:
                        rest_of_w(k + 1)
                    if not is_v(k):
                        dve.wait_ge(staged, k * UNITS + u + 1)
                        dve.wait_ge(rest_stored[u], 16 * rests(k))
                        nc.vector.scalar_tensor_tensor(stage_lo[:, u, :].bitcast(F32R), acc[:, u, :], scale(k), stage[:, u, :],
                                                       op0=ALU.mult, op1=ALU.subtract).then_inc(rest_staged, 1)

        @block.tensor
        def _(pe):
            def turn_x(b):
                pe.wait_ge(x_scaled, b + 1)
                if b >= 2:
                    pe.wait_ge(h_set, b - 1)
                for c in range(NC):
                    mm = nc.tensor.transpose(turned[:, b % 2, c, :], xs[:, b % XR, c * P:(c + 1) * P], ident[:, :])
                mm.then_inc(x_turned, 1)

            def unit(k, u):
                if u == 0:
                    pe.wait_ge(w_lo_set, k + 1)
                n, slot = k % PER_ATT // 2, k % 2
                pe.wait_ge(h_lo_set, NB // 2 if u < 2 else NB)
                if k:
                    pe.wait_ge(staged, (k - 1) * UNITS + u + 1)
                    if not is_v(k - 1):
                        pe.wait_ge(rest_staged, rests(k - 1) * UNITS + u + 1)
                if n < 2:
                    cols, tokens = slice(u % 2 * P, (u % 2 + 1) * P), slice((u // 2) * HALF, (u // 2 + 1) * HALF)
                    for c in range(NC):
                        mm = split_matmul(nc, acc[:, u, :], w_hi[:, slot, c, cols], w_lo[:, slot, c, cols],
                                          h_hi[:, c, tokens], h_lo[:, c, tokens], c == 0, c == NC - 1)
                else:
                    for t in range(2):
                        tokens = slice((2 * u + t) * P, (2 * u + t + 1) * P)
                        for c in range(NC):
                            mm = split_matmul(nc, acc[:, u, t * COLS:(t + 1) * COLS], h_hi[:, c, tokens], h_lo[:, c, tokens],
                                              w_hi[:, slot, c, :], w_lo[:, slot, c, :], c == 0, c == NC - 1)
                mm.then_inc(acc_full, 1)

            for b in range(NB):
                turn_x(b)
            for k in range(CHUNKS):
                for u in range(UNITS):
                    unit(k, u)


def load_queries_and_keys(sp, qk, qk_in, qkT_dram, attention, i):
    for h in range(2):
        for n in range(2):
            sp.dma_start(qk[:, h, n, :, :].bitcast(F32),
                         qkT_dram[attention, n, :, bass.ds(i * P + h * HD, HD), :].rearrange("s c t -> c s t")).then_inc(qk_in[h], 16)


def stick_breaking(nc, qkT_dram, v_dram, neg_suffix_r, neg_ones, ident_r, masked_r, oT_dram, ca_qk, ca_qk_in):
    LARGE = 30.0
    SLOTS = 6
    PARTS = 3
    WSLOTS = 3
    AHEAD = 4
    STEPS = [(t, j, max(0, j - 4 * t) * P) for t in range(2) for j in range(4 * t + 3, -1, -1)]
    NSTEP = 2 * len(STEPS)
    step = [(h, *STEPS[i]) for i in range(len(STEPS)) for h in range(2)]
    LAST = [n for n, (h, t, j, c0) in enumerate(step) if j == 0]
    with ExitStack() as ctx:
        def sb(name, shape, dt=F32):
            return ctx.enter_context(nc.sbuf_tensor(name, shape, dt))

        def sem(name):
            return ctx.enter_context(nc.semaphore(name))

        qk = sb("sb_qk", [HD, 2, 2, 2, S], F32R)
        v = sb("sb_v", [P, 2, NB, HD])
        low = sb("sb_low", [P, SLOTS, HALF])
        soft = sb("sb_soft", [P, SLOTS, HALF])
        soft_hi = sb("sb_soft_hi", [P, PARTS, HALF], F32R)
        soft_lo = sb("sb_soft_lo", [P, PARTS, HALF], F32R)
        wts = sb("sb_wts", [P, WSLOTS, HALF])
        total = sb("sb_total", [P, 2, HALF])
        out = sb("sb_out", [HD, 2, HALF])
        zeros = sb("sb_zeros", [P, P])
        z = ctx.enter_context(nc.psum_tensor("sb_z", [P, SLOTS, HALF], F32))
        o = ctx.enter_context(nc.psum_tensor("sb_o", [HD, 2, HALF], F32))

        qk_in = [sem("sb_qk_in0"), sem("sb_qk_in1")]
        v_in = [sem("sb_v_in0"), sem("sb_v_in1")]
        passed = sem("sb_passed")
        z_set, low_set, exp_set, log_set = sem("sb_z_set"), sem("sb_low_set"), sem("sb_exp"), sem("sb_log")
        soft_set, total_set, after_set = sem("sb_soft"), sem("sb_total"), sem("sb_after")
        hi_set, lo_set = sem("sb_soft_hi_set"), sem("sb_soft_lo_set")
        wts_set, wts_used, o_copied = sem("sb_wts"), sem("sb_wts_used"), sem("sb_copied")
        o_stored = [sem("sb_stored0"), sem("sb_stored1")]
        zeros_set = sem("sb_zeros_set")
        PAIRS = HEADS // 2

        block = ctx.enter_context(nc.Block())

        @block.sync
        def _(sp):
            def turn(i):
                sp.wait_ge(z_set, NSTEP * i)
                load_queries_and_keys(sp, qk, qk_in, qkT_dram, 0, i)
                for h in range(2):
                    sp.wait_ge(wts_used, NSTEP * i)
                    sp.sem_inc(passed, 1)
                    sp.dma_start(v[:, h, :, :], v_dram[0, :, bass.ds(i * P + h * HD, HD)].rearrange("(b p) d -> p b d", p=P)).then_inc(v_in[h], 16)

            turn(0)
            load_queries_and_keys(sp, ca_qk, ca_qk_in, qkT_dram, 1, 0)
            with sp.Fori(1, PAIRS) as i:
                turn(i)

        @block.gpsimd
        def _(pool):
            nc.gpsimd.memset(zeros[:, :], 0.0).then_inc(zeros_set, 1)
            pool.wait_ge(zeros_set, 1)
            def turn(i):
                for n, (h, t, j, c0) in enumerate(step):
                    first = j == 4 * t + 3
                    if j > 0:
                        old = HALF if first else max(0, j + 1 - 4 * t) * P
                        pool.wait_ge(soft_set, NSTEP * i + n + 1)
                        pool.wait_ge(after_set, NSTEP * i + n + 1)
                        s = soft[:, n % SLOTS, :]
                        if old < HALF:
                            last = nc.gpsimd.tensor_tensor(total[:, h, old:], total[:, h, old:], s[:, old:], ALU.add)
                        if old > c0:
                            last = nc.gpsimd.tensor_tensor(total[:, h, c0:old], s[:, c0:old], zeros[:, :], ALU.add)
                        last.then_inc(total_set, 1)
                    if j == 0:
                        k = LAST.index(n)
                        pool.wait_ge(o_copied, 4 * i + k + 1)
                        pool.dma_start(oT_dram[0, bass.ds(i * P + h * HD, HD), t * HALF:(t + 1) * HALF],
                                       out[:, k % 2, :]).then_inc(o_stored[k % 2], 16)

            turn(0)
            with pool.Fori(1, PAIRS) as i:
                turn(i)
            for k in range(2):
                pool.wait_ge(o_stored[k], 16 * 2 * PAIRS)

        def adds_before(n):
            return sum(1 for (h, t, j, c0) in step[:n] if j > 0)

        TOTALS = adds_before(NSTEP)

        @block.tensor
        def _(pe):
            def scores(i, n):
                h, t, j, c0 = step[n]
                if n < 2:
                    pe.wait_ge(qk_in[h], 32 * i + 32)
                pe.wait_ge(wts_set, NSTEP * i + n - SLOTS + 1 if n >= SLOTS else NSTEP * i)
                diag = j >= 4 * t
                keys, queries = slice(j * P, (j + 1) * P), slice(t * HALF + c0, (t + 1) * HALF)
                mm = split_matmul(nc, z[:, n % SLOTS, c0:], qk[:, h, 1, 0, keys], qk[:, h, 1, 1, keys],
                                  qk[:, h, 0, 0, queries], qk[:, h, 0, 1, queries], True, True)
                if diag:
                    mm = nc.tensor.matmul(z[:, n % SLOTS, c0:c0 + P], ident_r[:, :], masked_r[:, :], start=False, stop=True,
                                          skip_group_check=True)
                mm.then_inc(z_set, 1)

            def after(i, n):
                h, t, j, c0 = step[n]
                pe.wait_ge(lo_set, NSTEP * i + n + 1)
                for part in (soft_hi, soft_lo):
                    mm = nc.tensor.matmul(z[:, n % SLOTS, c0:], neg_suffix_r[:, :], part[:, n % PARTS, c0:],
                                          start=False, stop=True, skip_group_check=True)
                if j < 4 * t + 3:
                    old = max(0, j + 1 - 4 * t) * P
                    pe.wait_ge(total_set, TOTALS * i + adds_before(n - 1))
                    mm = nc.tensor.matmul(z[:, n % SLOTS, old:], neg_ones[:, :], total[:, h, old:],
                                          start=False, stop=True, skip_group_check=True)
                mm.then_inc(after_set, 1)

            def values(i, n):
                h, t, j, c0 = step[n]
                pe.wait_ge(wts_set, NSTEP * i + n + 1)
                if j == 4 * t + 3:
                    pe.wait_ge(o_copied, 4 * i + (h + 1 if t else 0))
                    pe.wait_ge(v_in[h], 16 * i + 16)
                mm = nc.tensor.matmul(o[:, h, c0:], v[:, h, j, :], wts[:, n % WSLOTS, c0:],
                                      start=(j == 4 * t + 3), stop=(j == 0), skip_group_check=True)
                mm.then_inc(wts_used, 1)

            def turn(i):
                for n in range(AHEAD):
                    scores(i, n)
                for n in range(NSTEP):
                    if n + AHEAD < NSTEP:
                        scores(i, n + AHEAD)
                    after(i, n)
                    if n >= 2:
                        values(i, n - 2)
                values(i, NSTEP - 2)
                values(i, NSTEP - 1)

            turn(0)
            with pe.Fori(1, PAIRS) as i:
                turn(i)

        @block.scalar
        def _(act):
            def log_part(i, n):
                h, t, j, c0 = step[n]
                act.wait_ge(low_set, NSTEP * i + n + 1)
                s = low[:, n % SLOTS, c0:]
                nc.scalar.activation(s, s, ACT.Exp).then_inc(exp_set, 1)
                act.wait_ge(exp_set, NSTEP * i + n + 1)
                nc.scalar.activation(s, s, ACT.Ln, bias=1.0).then_inc(log_set, 1)

            def weights(i, n):
                h, t, j, c0 = step[n]
                act.wait_ge(after_set, NSTEP * i + n + 1)
                if n >= WSLOTS:
                    act.wait_ge(wts_used, NSTEP * i + n - WSLOTS + 1)
                nc.scalar.activation(wts[:, n % WSLOTS, c0:], z[:, n % SLOTS, c0:], ACT.Exp).then_inc(wts_set, 1)

            act.add_instruction(mybir.InstLoadActFuncSet(name=nc.get_next_instruction_name(), act_func_set_id=EXP_AND_LN))
            def hi_part(i, n):
                h, t, j, c0 = step[n]
                act.wait_ge(soft_set, NSTEP * i + n + 1)
                if n >= PARTS:
                    act.wait_ge(after_set, NSTEP * i + n - PARTS + 1)
                nc.scalar.activation(soft_hi[:, n % PARTS, c0:], soft[:, n % SLOTS, c0:], ACT.Copy).then_inc(hi_set, 1)

            def turn(i):
                for n in range(3):
                    log_part(i, n)
                for n in range(2):
                    hi_part(i, n)
                for n in range(NSTEP):
                    if n + 3 < NSTEP:
                        log_part(i, n + 3)
                    if n + 2 < NSTEP:
                        hi_part(i, n + 2)
                    weights(i, n)

            turn(0)
            with act.Fori(1, PAIRS) as i:
                turn(i)

        @block.vector
        def _(dve):
            def limit(i, n):
                h, t, j, c0 = step[n]
                dve.wait_ge(z_set, NSTEP * i + n + 1)
                nc.vector.tensor_single_scalar(low[:, n % SLOTS, c0:], z[:, n % SLOTS, c0:], LARGE, ALU.min).then_inc(low_set, 1)

            def softplus(i, n):
                h, t, j, c0 = step[n]
                dve.wait_ge(log_set, NSTEP * i + n + 1)
                if n >= SLOTS:
                    dve.wait_ge(total_set, TOTALS * i + adds_before(n - SLOTS + 1))
                nc.vector.tensor_tensor(soft[:, n % SLOTS, c0:], z[:, n % SLOTS, c0:], low[:, n % SLOTS, c0:], ALU.max).then_inc(soft_set, 1)

            def lo_part(i, n):
                h, t, j, c0 = step[n]
                dve.wait_ge(hi_set, NSTEP * i + n + 1)
                nc.vector.tensor_tensor(soft_lo[:, n % PARTS, c0:], soft[:, n % SLOTS, c0:], soft_hi[:, n % PARTS, c0:].bitcast(F32),
                                        ALU.subtract).then_inc(lo_set, 1)

            def copy_out(i, k):
                n = LAST[k]
                h, t, j, c0 = step[n]
                dve.wait_ge(wts_used, NSTEP * i + n + 1)
                dve.wait_ge(o_stored[k % 2], 32 * i + 16 * (k // 2))
                nc.vector.tensor_copy(out[:, k % 2, :], o[:, h, :]).then_inc(o_copied, 1)

            def turn(i):
                for n in range(AHEAD):
                    limit(i, n)
                softplus(i, 0)
                softplus(i, 1)
                lo_part(i, 0)
                for n in range(NSTEP):
                    if n + 2 < NSTEP:
                        softplus(i, n + 2)
                    if n + AHEAD < NSTEP:
                        limit(i, n + AHEAD)
                    if n + 1 < NSTEP:
                        lo_part(i, n + 1)
                    if n - 2 in LAST:
                        copy_out(i, LAST.index(n - 2))
                for k, n in enumerate(LAST):
                    if n + 2 >= NSTEP:
                        copy_out(i, k)

            turn(0)
            with dve.Fori(1, PAIRS) as i:
                turn(i)


def load_gate_weights(sp, wg, wg_in, w_in, i):
    for a in range(2):
        sp.dma_start(wg[:, a, :, :], w_in[0].rearrange("(c p) n -> p c n", p=P)[:, :, bass.ds(i * P + (6 * WIDTH + a * D), P)]
                     ).then_inc(wg_in, 16)


def chunk_attention(nc, qkT_dram, v_dram, ident, bias_dram, oT_dram, qk, qk_in, w_in, wg, wg_in):
    SLOTS = 2
    ROWS = 8
    LAG = 4
    step = [(h, qb, min(qb, 4) + 1) for qb in range(NB) for h in range(2)]
    NSTEP = len(step)
    PAIRS = HEADS // 2
    with ExitStack() as ctx:
        def sb(name, shape, dt=F32):
            return ctx.enter_context(nc.sbuf_tensor(name, shape, dt))

        def sem(name):
            return ctx.enter_context(nc.semaphore(name))

        v = sb("ca_v", [P, 2, NB, HD])
        bias = sb("ca_bias", [P, 2, BAND])
        prob = sb("ca_prob", [P, ROWS, BAND])
        probT = sb("ca_probT", [P, 2, 5, P])
        neg_top = sb("ca_neg_top", [P, ROWS])
        mass = sb("ca_mass", [P, ROWS])
        inv = sb("ca_inv", [P, ROWS])
        out = sb("ca_out", [HD, 2, HALF])
        s = ctx.enter_context(nc.psum_tensor("ca_s", [P, SLOTS, 2, HALF], F32))
        turned = ctx.enter_context(nc.psum_tensor("ca_turned", [P, 2 * HALF], F32))
        o = ctx.enter_context(nc.psum_tensor("ca_o", [HD, 2, HALF], F32))

        bias_in = [sem("ca_bias_in0"), sem("ca_bias_in1")]
        v_in = [sem("ca_v_in0"), sem("ca_v_in1")]
        passed = sem("ca_passed")
        s_set, biased_set, neg_set = sem("ca_s_set"), sem("ca_biased"), sem("ca_neg")
        exp_set, inv_set, prob_set = sem("ca_exp"), sem("ca_inv"), sem("ca_prob")
        turned_set, probT_set, o_set, o_copied = sem("ca_turned"), sem("ca_probT"), sem("ca_o"), sem("ca_copied")
        o_stored = [sem("ca_stored0"), sem("ca_stored1")]

        block = ctx.enter_context(nc.Block())

        def parts(nk):
            return [(0, BAND // 2), (BAND // 2, BAND)] if nk == 5 else [(0, nk * P)]

        @block.sync
        def _(sp):
            def turn(i):
                sp.wait_ge(s_set, NSTEP * i)
                if not isinstance(i, int):
                    load_queries_and_keys(sp, qk, qk_in, qkT_dram, 1, i)
                for h in range(2):
                    sp.wait_ge(biased_set, NSTEP * i)
                    sp.sem_inc(passed, 1)
                    sp.dma_start(bias[:, h, :], bass.AP(tensor=bias_dram.tensor, offset=(2 * i + h) * (P * EXT) + P - 1,
                                                        ap=[[EXT - 1, P], [1, BAND]])).then_inc(bias_in[h], 16)
                for h in range(2):
                    sp.wait_ge(o_set, NSTEP * i)
                    sp.sem_inc(passed, 1)
                    sp.dma_start(v[:, h, :, :], v_dram[1, :, bass.ds(i * P + h * HD, HD)].rearrange("(b p) d -> p b d", p=P)).then_inc(v_in[h], 16)

            turn(0)
            load_gate_weights(sp, wg, wg_in, w_in, 0)
            with sp.Fori(1, PAIRS) as i:
                turn(i)

        @block.gpsimd
        def _(pool):
            def send(i, quad, h):
                pool.wait_ge(o_copied, 4 * i + 2 * quad + h + 1)
                pool.dma_start(oT_dram[1, bass.ds(i * P + h * HD, HD), quad * HALF:(quad + 1) * HALF],
                               out[:, h, :]).then_inc(o_stored[h], 16)

            def turn(i):
                for n in range(NSTEP):
                    h, qb, nk = step[n]
                    pool.wait_ge(inv_set, NSTEP * i + n + 1)
                    row = prob[:, n % ROWS, 0:nk * P]
                    nc.gpsimd.tensor_tensor(row, row, inv[:, n % ROWS:n % ROWS + 1].to_broadcast([P, nk * P]), ALU.mult).then_inc(prob_set, 1)
                    if n in (12, 13):
                        send(i, 0, n - 12)
                send(i, 1, 0)
                send(i, 1, 1)

            turn(0)
            with pool.Fori(1, PAIRS) as i:
                turn(i)
            for h in range(2):
                pool.wait_ge(o_stored[h], 16 * 2 * PAIRS)

        @block.tensor
        def _(pe):
            def scores(i, n):
                h, qb, nk = step[n]
                if n < 2:
                    pe.wait_ge(qk_in[h], 32 * i + 32)
                pe.wait_ge(biased_set, NSTEP * i + n - SLOTS + 1 if n >= SLOTS else NSTEP * i)
                for part, (a, b) in enumerate(parts(nk)):
                    k0 = (qb - nk + 1) * P
                    queries, keys = slice(qb * P, (qb + 1) * P), slice(k0 + a, k0 + b)
                    mm = split_matmul(nc, s[:, n % SLOTS, part, 0:b - a], qk[:, h, 0, 0, queries], qk[:, h, 0, 1, queries],
                                      qk[:, h, 1, 0, keys], qk[:, h, 1, 1, keys], True, True)
                mm.then_inc(s_set, 1)

            def transpose_probs(i, n):
                h, qb, nk = step[n]
                pe.wait_ge(prob_set, NSTEP * i + n + 1)
                pe.wait_ge(probT_set, NSTEP * i + n)
                for b in range(nk):
                    mm = nc.tensor.transpose(turned[:, b * P:(b + 1) * P], prob[:, n % ROWS, b * P:(b + 1) * P], ident[:, :])
                mm.then_inc(turned_set, 1)

            def values(i, n):
                h, qb, nk = step[n]
                pe.wait_ge(probT_set, NSTEP * i + n + 1)
                if qb % 4 == 0:
                    pe.wait_ge(o_copied, 4 * i + (2 if qb else 0))
                    pe.wait_ge(v_in[h], 16 * i + 16)
                for b in range(nk):
                    mm = nc.tensor.matmul(o[:, h, (qb % 4) * P:(qb % 4 + 1) * P], v[:, h, qb - nk + 1 + b, :], probT[:, n % 2, b, :],
                                          start=(b == 0), stop=(b == nk - 1))
                mm.then_inc(o_set, 1)

            def turn(i):
                for n in range(NSTEP + LAG + 1):
                    if n < NSTEP:
                        scores(i, n)
                    if LAG <= n < NSTEP + LAG:
                        transpose_probs(i, n - LAG)
                    if n >= LAG + 1:
                        values(i, n - LAG - 1)

            turn(0)
            with pe.Fori(1, PAIRS) as i:
                turn(i)

        @block.scalar
        def _(act):
            def turn(i):
                for n in range(NSTEP + 2):
                    if n < NSTEP:
                        h, qb, nk = step[n]
                        act.wait_ge(neg_set, NSTEP * i + n + 1)
                        nc.scalar.activation(prob[:, n % ROWS, 0:nk * P], prob[:, n % ROWS, 0:nk * P], ACT.Exp, bias=neg_top[:, n % ROWS:n % ROWS + 1],
                                             accum_out=mass[:, n % ROWS:n % ROWS + 1]).then_inc(exp_set, 1)
                    if n >= 2:
                        m = n - 2
                        h, qb, nk = step[m]
                        act.wait_ge(turned_set, NSTEP * i + m + 1)
                        act.wait_ge(o_set, NSTEP * i + m - 1 if m >= 2 else NSTEP * i)
                        nc.scalar.activation(probT[:, m % 2, 0:nk, :], turned[:, 0:nk * P].rearrange("p (b q) -> p b q", q=P),
                                             ACT.Copy).then_inc(probT_set, 1)

            turn(0)
            with act.Fori(1, PAIRS) as i:
                turn(i)

        @block.vector
        def _(dve):
            def biased(i, n):
                h, qb, nk = step[n]
                if n < 2:
                    dve.wait_ge(bias_in[h], 16 * i + 16)
                dve.wait_ge(s_set, NSTEP * i + n + 1)
                dve.wait_ge(turned_set, NSTEP * i + n - ROWS + 1 if n >= ROWS else NSTEP * i)
                row = prob[:, n % ROWS, 0:nk * P]
                split = dict(a=len(parts(nk)))
                nc.vector.tensor_tensor(row.rearrange("p (a n) -> p a n", **split), s[:, n % SLOTS, 0:split["a"], 0:parts(nk)[0][1]],
                                        bias[:, h, BAND - nk * P:].rearrange("p (a n) -> p a n", **split), ALU.add).then_inc(biased_set, 1)
                dve.wait_ge(biased_set, NSTEP * i + n + 1)
                nc.vector.tensor_reduce(neg_top[:, n % ROWS:n % ROWS + 1], row, AX_X, ALU.max, negate=True).then_inc(neg_set, 1)

            def scaled(i, n):
                h, qb, nk = step[n]
                dve.wait_ge(exp_set, NSTEP * i + n + 1)
                nc.vector.reciprocal(inv[:, n % ROWS:n % ROWS + 1], mass[:, n % ROWS:n % ROWS + 1]).then_inc(inv_set, 1)

            def copy_out(i, k):
                quad, h = k // 2, k % 2
                dve.wait_ge(o_set, NSTEP * i + 8 * quad + 6 + h + 1)
                dve.wait_ge(o_stored[h], 32 * i + 16 * quad)
                nc.vector.tensor_copy(out[:, h, :], o[:, h, :]).then_inc(o_copied, 1)

            def turn(i):
                biased(i, 0)
                for n in range(NSTEP):
                    if n + 1 < NSTEP:
                        biased(i, n + 1)
                    scaled(i, n)
                    if n == 10:
                        copy_out(i, 0)
                        copy_out(i, 1)
                copy_out(i, 2)
                copy_out(i, 3)

            turn(0)
            with dve.Fori(1, PAIRS) as i:
                turn(i)


def gate_and_merge(nc, w_in, w_sb_proj, w_ca_proj, h_hi, h_lo, oT_dram, mT_dram, wg, wg_in):
    with ExitStack() as ctx:
        def sb(name, shape, dt=F32):
            return ctx.enter_context(nc.sbuf_tensor(name, shape, dt))

        def sem(name):
            return ctx.enter_context(nc.semaphore(name))

        oT_hi = sb("oT_hi", [P, 2, NCT, S], F32R)
        oT_lo = sb("oT_lo", [P, 2, NCT, S], F32R)
        wg_hi = sb("w_gate_hi", [P, 2, 2, NC, P], F32R)
        wg_lo = sb("w_gate_lo", [P, 2, 2, NC, P], F32R)
        wp = sb("w_branch", [P, 2, NCT, P])
        wp_hi = sb("w_branch_hi", [P, 2, 2, NCT, P], F32R)
        wp_lo = sb("w_branch_lo", [P, 2, 2, NCT, P], F32R)
        gate = sb("gate", [P, 2, 2, HALF])
        merged = sb("merged", [P, 2, HALF])
        acc = ctx.enter_context(nc.psum_tensor("merge_acc", [P, 2, 4, HALF], F32))

        o_stage = [gate[:, 0, :, :], gate[:, 1, :, :], merged[:, :, :]]
        o_in = [sem(f"o_in{k}") for k in range(3)]
        o_hi_set, o_lo_set, wp_in = sem("o_hi_set"), sem("o_lo_set"), sem("branch_w_in")
        w_hi_set, w_lo_set = sem("merge_w_hi"), sem("merge_w_lo")
        gates_full, branches_full = sem("gates_full"), sem("branches_full")
        gate_set, part_set, merged_set = sem("gate_set"), sem("part_set"), sem("merged_set")
        stored = [sem("merge_stored0"), sem("merge_stored1")]
        PAIRS = NC // 2

        sb_cols = w_sb_proj[0].rearrange("(c p) n -> p c n", p=P)
        ca_cols = w_ca_proj[0].rearrange("(c p) n -> p c n", p=P)

        block = ctx.enter_context(nc.Block())

        @block.sync
        def _(sp):
            def load_branch_weights(i):
                sp.dma_start(wp[:, 0, :, :], sb_cols[:, :, bass.ds(i * P, P)]).then_inc(wp_in, 16)
                sp.dma_start(wp[:, 1, :, :], ca_cols[:, :, bass.ds(i * P, P)]).then_inc(wp_in, 16)

            load_branch_weights(0)
            for k in range(2 * NCT):
                if k >= 3:
                    sp.wait_ge(o_lo_set, k - 2)
                sp.dma_start(o_stage[k % 3].rearrange("p a n -> p (a n)"),
                             oT_dram[k // NCT, k % NCT * P:(k % NCT + 1) * P, :]).then_inc(o_in[k % 3], 16)
            with sp.Fori(1, NC) as i:
                sp.wait_ge(w_lo_set, 2 * i)
                load_gate_weights(sp, wg, wg_in, w_in, i)
                load_branch_weights(i)

        @block.gpsimd
        def _(pool):
            def turn(i):
                for j in range(2):
                    for u in range(2):
                        pool.wait_ge(merged_set, 4 * i + 2 * j + u + 1)
                        pool.dma_start(mT_dram[bass.ds((2 * i + j) * P, P), u * HALF:(u + 1) * HALF], merged[:, u, :]).then_inc(stored[u], 16)

            turn(0)
            with pool.Fori(1, PAIRS) as i:
                turn(i)
            for u in range(2):
                pool.wait_ge(stored[u], 16 * NC)

        @block.tensor
        def _(pe):
            def turn(i):
                for j in range(2):
                    pe.wait_ge(w_lo_set, 4 * i + 2 * j + 1)
                    for u in range(2):
                        cols = slice(u * HALF, (u + 1) * HALF)
                        n = 2 * j + u
                        pe.wait_ge(merged_set, 4 * i + n - 1 if n >= 2 else 4 * i)
                        for a in range(2):
                            for c in range(NC):
                                mm = split_matmul(nc, acc[:, u, a, :], wg_hi[:, j, a, c, :], wg_lo[:, j, a, c, :],
                                                  h_hi[:, c, cols], h_lo[:, c, cols], c == 0, c == NC - 1)
                        mm.then_inc(gates_full, 1)
                        pe.wait_ge(w_lo_set, 4 * i + 2 * j + 2)
                        for a in range(2):
                            for c in range(NCT):
                                if isinstance(i, int) and i == 0 and n == 0:
                                    pe.wait_ge(o_lo_set, a * NCT + c + 1)
                                mm = split_matmul(nc, acc[:, u, 2 + a, :], wp_hi[:, j, a, c, :], wp_lo[:, j, a, c, :],
                                                  oT_hi[:, a, c, cols], oT_lo[:, a, c, cols], c == 0, c == NCT - 1)
                        mm.then_inc(branches_full, 1)

            turn(0)
            with pe.Fori(1, PAIRS) as i:
                turn(i)

        @block.scalar
        def _(act):
            def split_w(i, j):
                act.wait_ge(wg_in, 64 * i + 32 * j + 32)
                if not isinstance(i, int) or i:
                    act.wait_ge(branches_full, 4 * i - 2 + 2 * j)
                nc.scalar.activation(wg_hi[:, j, :, :, :], wg[:, :, :, :], ACT.Copy).then_inc(w_hi_set, 1)
                act.wait_ge(wp_in, 64 * i + 32 * j + 32)
                nc.scalar.activation(wp_hi[:, j, :, :, :], wp[:, :, :, :], ACT.Copy).then_inc(w_hi_set, 1)

            def turn(i, last):
                for n in range(4):
                    u = n % 2
                    act.wait_ge(gates_full, 4 * i + n + 1)
                    if isinstance(i, int) and i == 0 and n == 0:
                        act.wait_ge(o_lo_set, 2 * NCT)
                    act.wait_ge(merged_set, 4 * i + n - 1 if n >= 2 else 4 * i)
                    nc.scalar.activation(gate[:, u, :, :], acc[:, u, 0:2, :], ACT.Sigmoid).then_inc(gate_set, 1)
                    if n == 0 and (not isinstance(i, int) or i):
                        split_w(i, 1)
                    if n == 2 and not last:
                        split_w(i + 1, 0)

            split_w(0, 0)
            for k in range(2 * NCT):
                act.wait_ge(o_in[k % 3], 16 * (k // 3 + 1))
                nc.scalar.activation(oT_hi[:, k // NCT, k % NCT, :], o_stage[k % 3].rearrange("p a n -> p (a n)"), ACT.Copy).then_inc(o_hi_set, 1)
            split_w(0, 1)
            turn(0, False)
            with act.Fori(1, PAIRS - 1) as i:
                turn(i, False)
            turn(PAIRS - 1, True)

        @block.vector
        def _(dve):
            def rest_of_w(i, j):
                dve.wait_ge(w_hi_set, 4 * i + 2 * j + 1)
                nc.vector.tensor_tensor(wg_lo[:, j, :, :, :], wg[:, :, :, :], wg_hi[:, j, :, :, :].bitcast(F32), ALU.subtract).then_inc(w_lo_set, 1)
                dve.wait_ge(w_hi_set, 4 * i + 2 * j + 2)
                nc.vector.tensor_tensor(wp_lo[:, j, :, :, :], wp[:, :, :, :], wp_hi[:, j, :, :, :].bitcast(F32), ALU.subtract).then_inc(w_lo_set, 1)

            def turn(i, last):
                for n in range(4):
                    u = n % 2
                    if n == 0 and (not isinstance(i, int) or i):
                        rest_of_w(i, 1)
                    if n == 2 and not last:
                        rest_of_w(i + 1, 0)
                    dve.wait_ge(gate_set, 4 * i + n + 1)
                    dve.wait_ge(branches_full, 4 * i + n + 1)
                    nc.vector.tensor_tensor(gate[:, u, :, :], gate[:, u, :, :], acc[:, u, 2:4, :], ALU.mult).then_inc(part_set, 1)
                    dve.wait_ge(part_set, 4 * i + n + 1)
                    dve.wait_ge(stored[u], 16 * (2 * i + n // 2))
                    nc.vector.tensor_tensor(merged[:, u, :], gate[:, u, 0, :], gate[:, u, 1, :], ALU.add).then_inc(merged_set, 1)

            rest_of_w(0, 0)
            for k in range(2 * NCT):
                o_hi = oT_hi[:, k // NCT, k % NCT, :].bitcast(F32)
                dve.wait_ge(o_hi_set, k + 1)
                nc.vector.tensor_tensor(oT_lo[:, k // NCT, k % NCT, :], o_stage[k % 3].rearrange("p a n -> p (a n)"), o_hi,
                                        ALU.subtract).then_inc(o_lo_set, 1)
            rest_of_w(0, 1)
            turn(0, False)
            with dve.Fori(1, PAIRS - 1) as i:
                turn(i, False)
            turn(PAIRS - 1, True)


def route_and_retrieve(nc, x, w_out, norm_ffn, w_query, keysT, expert_u, expert_v, norm_final, ident, mT_dram, out):
    RU = 4
    RV = 4
    SLOTS = NSEL
    QG = NS * NK // HALF
    GH = PH // QG
    GL = NS // QG
    GE = GH * TOPK
    with ExitStack() as ctx:
        def sb(name, shape, dt=F32):
            return ctx.enter_context(nc.sbuf_tensor(name, shape, dt))

        def sem(name):
            return ctx.enter_context(nc.semaphore(name))

        wo = sb("w_out_sb", [P, NC, D])
        wq = sb("w_query_sb", [P, NC, QG * HALF])
        keys = sb("keys", [P, NS, NK])
        g2 = sb("g2", [P, D])
        gf = sb("gf", [P, D])
        u_rows = sb("u_rows", [P, RU, D])
        v_rows = sb("v_rows", [P, RV, D])
        x1n, x1c = sb("x1_next", [P, D]), sb("x1_now", [P, D])
        h2n, h2c = sb("h2_next", [P, D]), sb("h2_now", [P, D])
        q = sb("query", [P, NS * NK])
        qT = sb("queryT", [P, NS, NK])
        scores = sb("scores", [P, NS, NK])
        scores2 = sb("scores2", [P, NS, NK])
        mblk = q[:, 0:D].rearrange("p (c t) -> p c t", t=P)
        h2T = scores2[:, NS - NC:, :]
        junk = scores2[:, 0:NC, :].rearrange("p a n -> p (a n)")
        cand = q[:, :].rearrange("p (h n) -> p h n", h=PH)
        cand2 = qT[:, :, :].rearrange("p (h a) n -> p h (a n)", a=2)
        hot = scores2[:, :, :].rearrange("p a (b i) -> p (a b) i", i=TOPK)
        diag = sb("diag", [P, RV, P])
        tv = sb("top_values", [P, NS, TOPK])
        ti = sb("top_index", [P, NS, TOPK], U32)
        bv = sb("best_values", [P, PH, TOPK])
        bp = sb("best_pos", [P, PH, TOPK], U32)
        bij = sb("best_ij", [P, 2, NSEL], U32)
        eij = sb("expert_ij", [P, 2, NSEL])
        iota = sb("iota", [P, TOPK])
        shifted = sb("shifted", [P, PH, TOPK])
        mass = sb("gate_mass", [P, PH])
        minv = sb("gate_inv", [P, PH])
        gate_n, gate_c = sb("gate_next", [P, NSEL]), sb("gate_now", [P, NSEL])
        idx_n, idx_c = sb("index_next", [P, NSEL], I32), sb("index_now", [P, NSEL], I32)
        dots = sb("dots", [P, NSEL])
        gel = sb("gelu", [P, NSEL])
        wts = sb("expert_wts", [P, NSEL])
        eps = sb("eps2", [P, 1])
        ss, root, rstd = sb("ss2", [P, 1]), sb("root2", [P, 1]), sb("rstd2", [P, 1])
        ssy, rooty, rstdy = sb("ssy", [P, 1]), sb("rooty", [P, 1]), sb("rstdy", [P, 1])
        front = ctx.enter_context(nc.psum_tensor("front", [P, 4, HALF], F32))
        sums = ctx.enter_context(nc.psum_tensor("sums", [P, 2, HALF], F32))

        wo_in = [sem("wo_in0"), sem("wo_in1")]
        g2_in, keys_in, gf_in, eps_set, iota_set = sem("g2_in"), sem("keys_in"), sem("gf_in"), sem("eps2_set"), sem("iota_set")
        m_in, x_in = sem("m_in"), sem("xb_in")
        wq_in = [sem(f"wq_in{i}") for i in range(QG)]
        unit_full, unit_taken = sem("unit_full"), sem("unit_taken")
        x1_set, sq_set, root_set, rstd_set, h2_set = sem("x1_set"), sem("sq2_set"), sem("root2_set"), sem("rstd2_set"), sem("h2_set")
        search = sem("search")
        shift_set, gexp_set, gate_set = sem("shift_set"), sem("gexp_set"), sem("gate_n_set")
        idx_set, idx_moved, gate_moved, now_set = sem("idx_set"), sem("idx_moved"), sem("gate_moved"), sem("now_set")
        u_in = [sem(f"u_in{i}") for i in range(RU)]
        v_in = [sem(f"v_in{i}") for i in range(RV)]
        dot_set, gel_set, wts_set, diag_set = sem("dot_set"), sem("gel_set"), sem("expert_wts_set"), sem("diag_set")
        v_free, y_set, ysq_set, yroot_set, yrstd_set, yout_set = (sem("v_free"), sem("y_set"), sem("ysq_set"), sem("yroot_set"),
                                                                  sem("yrstd_set"), sem("yout_set"))
        y_stored, search_passed, pool_passed = sem("y_stored"), sem("search_passed"), sem("pool_passed")

        x_rows = x.rearrange("a (b p) d -> (a b) p d", p=P)
        out_rows = out.rearrange("a (b p) d -> (a b) p d", p=P)
        wq_rows = w_query[0].rearrange("(c p) n -> p c n", p=P)

        def unit(u, b):
            bank = front[:, u % 4, :]
            if u < 2:
                if u == 0:
                    nc.tensor.wait_ge(m_in, 16 * b + 16)
                nc.tensor.wait_ge(unit_taken, 14 * b)
                nc.tensor.wait_ge(wo_in[u], 16)
                for c in range(NC):
                    mm = nc.tensor.matmul(bank, mblk[:, c, :], wo[:, c, u * HALF:(u + 1) * HALF], start=(c == 0), stop=(c == NC - 1))
            elif u < 4:
                nc.tensor.wait_ge(h2_set, b + 1)
                for c in range(4):
                    k = 4 * (u - 2) + c
                    mm = nc.tensor.transpose(bank[:, c * P:(c + 1) * P], h2n[:, k * P:(k + 1) * P], ident[:, :])
            elif (u - 4) % 3 == 0:
                nc.tensor.wait_ge(unit_taken, 14 * b + max(2, u - 5))
                g = (u - 4) // 3
                nc.tensor.wait_ge(wq_in[g], 16)
                for c in range(NC):
                    mm = nc.tensor.matmul(bank, h2T[:, c, :], wq[:, c, g * HALF:(g + 1) * HALF], start=(c == 0), stop=(c == NC - 1))
            else:
                nc.tensor.wait_ge(unit_taken, 14 * b + u - 2)
                for c in range(GL):
                    k = GL * ((u - 4) // 3) + c
                    if (u - 4) % 3 == 1:
                        mm = nc.tensor.transpose(bank[:, c * P:(c + 1) * P], q[:, k * P:(k + 1) * P], ident[:, :])
                    else:
                        nc.tensor.wait_ge(keys_in, 16)
                        mm = nc.tensor.matmul(bank[:, c * P:(c + 1) * P], qT[:, k, :], keys[:, k, :], start=True, stop=True)
            mm.then_inc(unit_full, 1)

        def take(u, b):
            nc.scalar.wait_ge(unit_full, 16 * b + u + 1)
            nc.scalar.wait_ge(idx_set, QG * b)
            g = (u - 4) // 3
            if u < 4:
                dst = h2T[:, 4 * (u - 2):4 * (u - 1), :]
            elif (u - 4) % 3 == 0:
                dst = q[:, g * HALF:(g + 1) * HALF]
            elif (u - 4) % 3 == 1:
                dst = qT[:, GL * g:GL * (g + 1), :]
            else:
                dst = scores[:, GL * g:GL * (g + 1), :]
            nc.scalar.activation(dst, front[:, u % 4, :], ACT.Copy).then_inc(unit_taken, 1)

        def search_norm_act(b):
            nc.scalar.wait_ge(x1_set, 2 * b + 2)
            nc.scalar.wait_ge(idx_set, QG * b - 2 if not isinstance(b, int) or b else 0)
            nc.scalar.activation(junk, x1n[:, :], ACT.Square, accum_out=ss[:, :]).then_inc(sq_set, 1)
            nc.scalar.wait_ge(sq_set, b + 1)
            nc.scalar.activation(root[:, :], ss[:, :], ACT.Sqrt, scale=1.0 / D, bias=eps[:, 0:1]).then_inc(root_set, 1)

        def search_x1(b, u):
            nc.vector.wait_ge(unit_full, 16 * b + u + 1)
            nc.vector.wait_ge(x_in, 16 * b + 16)
            cols = slice(u * HALF, (u + 1) * HALF)
            nc.vector.tensor_tensor(x1n[:, cols], front[:, u, :], x1n[:, cols], ALU.add).then_inc(x1_set, 1)

        def search_h2(b):
            nc.vector.wait_ge(root_set, b + 1)
            nc.vector.reciprocal(rstd[:, :], root[:, :]).then_inc(rstd_set, 1)
            nc.vector.wait_ge(rstd_set, b + 1)
            nc.vector.scalar_tensor_tensor(h2n[:, :], x1n[:, :], rstd[:, 0:1], g2[:, :], op0=ALU.mult, op1=ALU.mult).then_inc(h2_set, 1)

        LISTS, SUMS, PICK = 5 * GL, 5 * GL + 1, 5 * GL + 1 + 5 * GH
        NSEARCH = PICK + 10
        PIECES = 20

        def search_piece(b, g, piece):
            def after_step(n):
                nc.vector.wait_ge(search, QG * NSEARCH * b + NSEARCH * g + n)
                nc.vector.sem_inc(search_passed, 1)

            lists, heads, experts = slice(GL * g, GL * g + GL), slice(GH * g, GH * g + GH), slice(GE * g, GE * g + GE)
            if piece < 5:
                if piece == 0:
                    nc.vector.wait_ge(unit_taken, 14 * b + 5 + 3 * g)
                if piece == 2 and GL * g + GL > NS - NC:
                    nc.vector.wait_ge(unit_full, 16 * b + 14)
                if piece or g or not isinstance(b, int) or b:
                    after_step(piece * GL)
                for l in range(GL * g, GL * g + GL):
                    if piece == 0:
                        step = nc.vector.max(tv[:, l, 0:8], scores[:, l, :])
                    elif piece == 1:
                        step = nc.vector.max_index(ti[:, l, 0:8], tv[:, l, 0:8], scores[:, l, :])
                    elif piece == 2:
                        step = nc.vector.match_replace(scores2[:, l, :], tv[:, l, 0:8], scores[:, l, :], LOWEST)
                    elif piece == 3:
                        step = nc.vector.max(tv[:, l, 8:16], scores2[:, l, :])
                    else:
                        step = nc.vector.max_index(ti[:, l, 8:16], tv[:, l, 8:16], scores2[:, l, :])
                    step.then_inc(search, 1)
            elif piece == 5:
                after_step(LISTS)
                first = tv[:, lists, :][:, 0::2, :].unsqueeze(3).to_broadcast([P, GH, TOPK, TOPK])
                second = tv[:, lists, :][:, 1::2, :].unsqueeze(2).to_broadcast([P, GH, TOPK, TOPK])
                nc.vector.tensor_tensor(cand[:, heads, :].rearrange("p h (i j) -> p h i j", j=TOPK), first, second, ALU.add).then_inc(search, 1)
            elif piece < 11:
                rnd = piece - 6
                after_step(SUMS + rnd * GH)
                for h in range(GH * g, GH * g + GH):
                    if rnd == 0:
                        step = nc.vector.max(bv[:, h, 0:8], cand[:, h, :])
                    elif rnd == 1:
                        step = nc.vector.max_index(bp[:, h, 0:8], bv[:, h, 0:8], cand[:, h, :])
                    elif rnd == 2:
                        step = nc.vector.match_replace(cand2[:, h, :], bv[:, h, 0:8], cand[:, h, :], LOWEST)
                    elif rnd == 3:
                        step = nc.vector.max(bv[:, h, 8:16], cand2[:, h, :])
                    else:
                        step = nc.vector.max_index(bp[:, h, 8:16], bv[:, h, 8:16], cand2[:, h, :])
                    step.then_inc(search, 1)
            elif piece == 11:
                after_step(PICK)
                flat = bp[:, heads, :].rearrange("p h k -> p (h k)")
                nc.vector.tensor_single_scalar(bij[:, 0, experts], flat, 4, ALU.logical_shift_right).then_inc(search, 1)
                nc.vector.tensor_single_scalar(bij[:, 1, experts], flat, TOPK - 1, ALU.bitwise_and).then_inc(search, 1)
                nc.vector.tensor_tensor(shifted[:, heads, :], bv[:, heads, :], bv[:, heads, 0:1].to_broadcast([P, GH, TOPK]), ALU.subtract).then_inc(shift_set, 1)
            elif piece < 18:
                side, part = (piece - 12) // 3, (piece - 12) % 3
                after_step(PICK + 2 + piece - 12)
                rows = hot[:, experts, :]
                if part == 0:
                    pos = bij[:, side, experts].unsqueeze(2).to_broadcast([P, GE, TOPK])
                    nc.vector.tensor_tensor(rows, pos, iota[:, :].unsqueeze(1).to_broadcast([P, GE, TOPK]), ALU.is_equal).then_inc(search, 1)
                elif part == 1:
                    rows4 = rows.rearrange("p (h k) i -> p h k i", h=GH)
                    key = ti[:, lists, :][:, side::2, :].unsqueeze(2).to_broadcast([P, GH, TOPK, TOPK])
                    nc.vector.tensor_tensor(rows4, rows4, key, ALU.mult).then_inc(search, 1)
                else:
                    nc.vector.tensor_reduce(eij[:, side, experts], rows, AX_X, ALU.add).then_inc(search, 1)
            elif piece == 18:
                after_step(PICK + 8)
                nc.vector.wait_ge(idx_moved, QG * (b - 1) + g + 1 if not isinstance(b, int) or b else 0)
                nc.vector.scalar_tensor_tensor(idx_n[:, experts], eij[:, 0, experts], float(NK), eij[:, 1, experts],
                                               op0=ALU.mult, op1=ALU.add).then_inc(idx_set, 1)
                nc.vector.wait_ge(gexp_set, QG * b + g + 1)
                nc.vector.tensor_reduce(mass[:, heads], shifted[:, heads, :], AX_X, ALU.add).then_inc(search, 1)
                after_step(PICK + 9)
                nc.vector.reciprocal(minv[:, heads], mass[:, heads]).then_inc(search, 1)
            else:
                after_step(PICK + 10)
                nc.vector.tensor_tensor(gate_n[:, experts].rearrange("p (h k) -> p h k", h=GH), shifted[:, heads, :],
                                        minv[:, heads].unsqueeze(2).to_broadcast([P, GH, TOPK]), ALU.mult).then_inc(gate_set, 1)

        def search_exp(b, g):
            heads = slice(GH * g, GH * g + GH)
            nc.scalar.wait_ge(shift_set, QG * b + g + 1)
            nc.scalar.activation(shifted[:, heads, :], shifted[:, heads, :], ACT.Exp).then_inc(gexp_set, 1)

        UNIT_AT = [4, 12, 20, 22, 24, 30, 32, 36, 42, 44, 48, 54, 56, 60, 66, 68]
        GROUP_AT = [34, 55, 76, 97]

        def unit_at(s):
            return UNIT_AT.index(s) if s in UNIT_AT else None

        def search_dve(s, b):
            if s in (UNIT_AT[0] + 2, UNIT_AT[1] + 2):
                search_x1(b, 0 if s < UNIT_AT[1] else 1)
            if s == UNIT_AT[1] + 3:
                search_h2(b)
            for g in range(QG):
                if GROUP_AT[g] <= s < GROUP_AT[g] + PIECES:
                    search_piece(b, g, s - GROUP_AT[g])

        def search_act(s, b):
            if s == UNIT_AT[1] + 2:
                search_norm_act(b)
            u = unit_at(s - 1) if s else None
            if u is not None and u >= 2:
                take(u, b)
            for g in range(QG):
                if s == GROUP_AT[g] + 14:
                    search_exp(b, g)

        def late_dve(s):
            for k in (2 * s, 2 * s + 1):
                if k < 2 * PIECES:
                    search_piece(0, 2 + k // PIECES, k % PIECES)

        def late_act(s):
            for g in range(2):
                if s == (g * PIECES + 12) // 2:
                    search_exp(0, 2 + g)

        block = ctx.enter_context(nc.Block())

        @block.sync
        def _(sp):
            def search_block(b):
                sp.wait_ge(unit_full, 16 * b)
                sp.wait_ge(idx_set, QG * b - 2 if not isinstance(b, int) else 0)
                sp.dma_start(mblk, mT_dram.rearrange("(c p) t -> p c t", p=P)[:, :, bass.ds(b * P, P)]).then_inc(m_in, 16)
                sp.wait_ge(now_set, 2 * b)
                sp.dma_start(x1n[:, :], x_rows[bass.ds(b, 1)][0]).then_inc(x_in, 16)

            for a in range(2):
                sp.dma_start(wo[:, :, a * HALF:(a + 1) * HALF], w_out[0].rearrange("(c p) n -> p c n", p=P)[:, :, a * HALF:(a + 1) * HALF]).then_inc(wo_in[a], 16)
                if a == 0:
                    search_block(0)
            sp.dma_start(g2[:, :], norm_ffn.to_broadcast([P, D])).then_inc(g2_in, 16)
            for g in range(QG):
                sp.dma_start(wq[:, :, g * HALF:(g + 1) * HALF], wq_rows[:, :, g * HALF:(g + 1) * HALF]).then_inc(wq_in[g], 16)
            sp.dma_start(keys[:, :, :], keysT).then_inc(keys_in, 16)
            sp.dma_start(gf[:, :], norm_final.rearrange("(a d) -> a d", a=1).to_broadcast([P, D])).then_inc(gf_in, 16)

            with sp.Fori(1, NB) as b:
                search_block(b)

        @block.gpsimd
        def _(pool):
            nc.gpsimd.iota(iota[:, :], [[1, TOPK]], base=0, channel_multiplier=0,
                           allow_small_or_imprecise_dtypes=True).then_inc(iota_set, 1)

            def gather_u(index, col, n, b):
                if b is not None:
                    pool.wait_ge(dot_set, SLOTS * b + n - RU + 1)
                    pool.sem_inc(pool_passed, 1)
                elif n >= RU:
                    pool.wait_ge(dot_set, n - RU + 1)
                pool.indirect_dma_start(u_rows[:, n % RU, :], None, expert_u[0], bass.IndirectOffsetOnAxis(index[:, col:col + 1], 0)).then_inc(u_in[n % RU], 16)

            def gather_v(n, b):
                pool.wait_ge(v_free, SLOTS * b + n + 1)
                pool.sem_inc(pool_passed, 1)
                pool.indirect_dma_start(v_rows[:, n % RV, :], None, expert_v[0], bass.IndirectOffsetOnAxis(idx_c[:, n:n + 1], 0)).then_inc(v_in[n % RV], 16)

            def retrieve(b, last):
                def move_indices(g):
                    if not isinstance(b, int) or b:
                        for n in range(RU):
                            pool.wait_ge(u_in[n], 16 * (SLOTS // RU) * (b - 1) + 16 * (GE // RU) * (g + 1))
                        for n in range(RV):
                            pool.wait_ge(v_in[n], 16 * (SLOTS // RV) * (b - 1) + 16 * (GE // RV) * (g + 1))
                    pool.wait_ge(idx_set, QG * b + g + 1)
                    pool.sem_inc(pool_passed, 1)
                    experts = slice(GE * g, GE * g + GE)
                    nc.gpsimd.tensor_copy(idx_c[:, experts], idx_n[:, experts]).then_inc(idx_moved, 1)
                    pool.wait_ge(idx_moved, QG * b + g + 1)
                    pool.sem_inc(pool_passed, 1)

                for s in range(SLOTS):
                    for g in range(QG):
                        if s == max(0, GE * g - TOPK):
                            move_indices(g)
                    if s + TOPK < SLOTS:
                        gather_u(idx_c, s + TOPK, s + TOPK, b)
                    elif not last:
                        if s + TOPK == SLOTS:
                            pool.wait_ge(idx_set, QG * (b + 1) + 1)
                        gather_u(idx_n, s + TOPK - SLOTS, s + TOPK, b)
                    gather_v(s, b)

            pool.wait_ge(idx_set, 1)
            for n in range(TOPK):
                gather_u(idx_n, n, n, None)
            retrieve(0, False)
            with pool.Fori(1, NB - 1) as b:
                retrieve(b, False)
            retrieve(NB - 1, True)

        @block.tensor
        def _(pe):
            pe.sem_inc(v_free, RV)
            for u in range(16):
                unit(u, 0)

            def retrieve(b, last):
                for s in range(SLOTS):
                    if s == 0:
                        pe.wait_ge(y_set, b)
                    pe.wait_ge(diag_set, SLOTS * b + s + 1)
                    pe.wait_ge(v_in[s % RV], 16 * (SLOTS // RV) * b + 16 * (s // RV + 1))
                    for a in range(2):
                        mm = nc.tensor.matmul(sums[:, a, :], diag[:, s % RV, :], v_rows[:, s % RV, a * HALF:(a + 1) * HALF],
                                              start=(s == 0), stop=(s == SLOTS - 1))
                    mm.then_inc(v_free, 1)
                    if not last and unit_at(s) is not None:
                        unit(unit_at(s), b + 1)

            retrieve(0, False)
            with pe.Fori(1, NB - 1) as b:
                retrieve(b, False)
            retrieve(NB - 1, True)

        @block.scalar
        def _(act):
            act.wait_ge(eps_set, 1)
            search_norm_act(0)
            for u in range(2, 16):
                take(u, 0)
                if u == 9:
                    search_exp(0, 0)

            def gelu(h, b):
                act.wait_ge(dot_set, SLOTS * b + TOPK * h + TOPK)
                hs = slice((h % PH) * TOPK, (h % PH) * TOPK + TOPK)
                nc.scalar.activation(gel[:, hs], dots[:, hs], ACT.Gelu).then_inc(gel_set, 1)

            def finish(b):
                act.wait_ge(y_set, b + 1)
                act.wait_ge(idx_set, min(QG * (b + 2), QG * NB) if isinstance(b, int) else QG * (b + 2))
                nc.scalar.activation(junk, x1c[:, :], ACT.Square, accum_out=ssy[:, :]).then_inc(ysq_set, 1)
                act.wait_ge(ysq_set, b + 1)
                nc.scalar.activation(rooty[:, :], ssy[:, :], ACT.Sqrt, scale=1.0 / D, bias=eps[:, 0:1]).then_inc(yroot_set, 1)
                act.wait_ge(yout_set, b + 1)
                act.dma_start(out_rows[bass.ds(b, 1)][0] if not isinstance(b, int) else out_rows[b], x1c[:, :]).then_inc(y_stored, 16)

            def retrieve(b, last):
                for s in range(SLOTS):
                    if s % TOPK == 0:
                        act.wait_ge(wts_set, PH * b + s // TOPK + 1)
                    act.wait_ge(v_free, SLOTS * b + s + 1)
                    nc.scalar.activation(diag[:, s % RV, :], ident[:, :], ACT.Copy, scale=wts[:, s:s + 1]).then_inc(diag_set, 1)
                    if s % TOPK == TOPK - 1 and not (last and s == SLOTS - 1):
                        gelu(s // TOPK + 1, b)
                    if isinstance(b, int) and b == 0:
                        late_act(s)
                    if not last:
                        search_act(s, b + 1)
                finish(b)

            search_exp(0, 1)
            gelu(0, 0)
            retrieve(0, False)
            with act.Fori(1, NB - 1) as b:
                retrieve(b, False)
            retrieve(NB - 1, True)
            act.wait_ge(y_stored, 16 * NB)

        @block.vector
        def _(dve):
            nc.vector.memset(eps[:, :], EPS).then_inc(eps_set, 1)
            dve.wait_ge(g2_in, 16)
            dve.wait_ge(iota_set, 1)
            for u in range(2):
                search_x1(0, u)
            search_h2(0)
            for piece in range(PIECES):
                search_piece(0, 0, piece)

            def dot(n, h2, b):
                row = u_rows[:, n % RU, :]
                dve.wait_ge(u_in[n % RU], 16 * (SLOTS // RU) * b + 16 * (n // RU + 1))
                nc.vector.tensor_tensor_reduce(row, row, h2, 1.0, 0.0, ALU.mult, ALU.add,
                                               dots[:, n % SLOTS:n % SLOTS + 1]).then_inc(dot_set, 1)

            def weigh(h, gate, b):
                dve.wait_ge(gel_set, PH * b + h + 1)
                hs = slice((h % PH) * TOPK, (h % PH) * TOPK + TOPK)
                if h:
                    dve.wait_ge(diag_set, SLOTS * b + TOPK * (h - PH + 1) if h >= PH else SLOTS * b)
                nc.vector.tensor_tensor(wts[:, hs], gel[:, hs], gate[:, hs], ALU.mult).then_inc(wts_set, 1)

            def retrieve(b, last):
                dve.wait_ge(dot_set, SLOTS * b + TOPK)
                nc.vector.tensor_copy(h2c[:, :], h2n[:, :]).then_inc(now_set, 1)
                dve.wait_ge(now_set, 2 * b + 1)
                for s in range(SLOTS):
                    for g in range(QG):
                        if s == max(0, GE * g - 2):
                            dve.wait_ge(wts_set, PH * b + max(1, 2 * g))
                            dve.wait_ge(gate_set, QG * b + g + 1)
                            experts = slice(GE * g, GE * g + GE)
                            nc.vector.tensor_copy(gate_c[:, experts], gate_n[:, experts]).then_inc(gate_moved, 1)
                    if s == 1:
                        dve.wait_ge(y_stored, 16 * b)
                        nc.vector.tensor_copy(x1c[:, :], x1n[:, :]).then_inc(now_set, 1)
                    n = s + TOPK
                    if n < SLOTS:
                        dot(n, h2c[:, :], b)
                    elif not last:
                        dot(n, h2n[:, :], b)
                    if isinstance(b, int) and b == 0:
                        late_dve(s)
                    if not last:
                        search_dve(s, b + 1)
                    if n % TOPK == TOPK - 1:
                        if n < SLOTS:
                            dve.wait_ge(gate_moved, QG * b + n // GE + 1)
                            weigh(n // TOPK, gate_c, b)
                        elif not last:
                            dve.wait_ge(gate_set, QG * (b + 1) + 1)
                            weigh(n // TOPK, gate_n, b)
                dve.wait_ge(now_set, 2 * b + 2)
                dve.wait_ge(v_free, SLOTS * b + SLOTS + RV)
                nc.vector.tensor_tensor(x1c[:, :], sums[:, :, :].rearrange("p a n -> p (a n)"), x1c[:, :], ALU.add).then_inc(y_set, 1)
                dve.wait_ge(yroot_set, b + 1)
                nc.vector.reciprocal(rstdy[:, :], rooty[:, :]).then_inc(yrstd_set, 1)
                dve.wait_ge(yrstd_set, b + 1)
                dve.wait_ge(gf_in, 16)
                nc.vector.scalar_tensor_tensor(x1c[:, :], x1c[:, :], rstdy[:, 0:1], gf[:, :], op0=ALU.mult, op1=ALU.mult).then_inc(yout_set, 1)

            for piece in range(PIECES):
                if piece < TOPK:
                    dot(piece, h2n[:, :], 0)
                search_piece(0, 1, piece)
            dve.wait_ge(gate_set, 1)
            weigh(0, gate_n, 0)
            retrieve(0, False)
            with dve.Fori(1, NB - 1) as b:
                retrieve(b, False)
            retrieve(NB - 1, True)


def constants(nc, ident, neg_suffix, neg_ones, masked, ident_r, neg_suffix_r, masked_r):
    with ExitStack() as ctx:
        filled = ctx.enter_context(nc.semaphore("filled"))
        rounded = ctx.enter_context(nc.semaphore("rounded"))
        block = ctx.enter_context(nc.Block())

        @block.gpsimd
        def _(pool):
            nc.gpsimd.memset(ident[:, :], 0.0).then_inc(filled, 1)
            nc.gpsimd.memset(neg_ones[:, :], -1.0).then_inc(filled, 1)
            nc.gpsimd.memset(neg_suffix[:, :], -1.0).then_inc(filled, 1)
            nc.gpsimd.memset(masked[:, :], MASKED).then_inc(filled, 1)
            pool.wait_ge(filled, 4)
            nc.gpsimd.affine_select(out=ident[:, :], in_=ident[:, :], compare_op=ALU.not_equal, fill=1.0,
                                    base=0, pattern=[[-1, P]], channel_multiplier=1).then_inc(filled, 1)
            nc.gpsimd.affine_select(out=neg_suffix[:, :], in_=neg_suffix[:, :], compare_op=ALU.is_ge, fill=0.0,
                                    base=0, pattern=[[-1, P]], channel_multiplier=1).then_inc(filled, 1)
            nc.gpsimd.affine_select(out=masked[:, :], in_=masked[:, :], compare_op=ALU.is_ge, fill=0.0,
                                    base=0, pattern=[[-1, P]], channel_multiplier=1).then_inc(filled, 1)

        @block.vector
        def _(dve):
            dve.wait_ge(filled, 7)
            nc.vector.tensor_copy(ident_r[:, :], ident[:, :]).then_inc(rounded, 1)
            nc.vector.tensor_copy(neg_suffix_r[:, :], neg_suffix[:, :]).then_inc(rounded, 1)
            nc.vector.tensor_copy(masked_r[:, :], masked[:, :]).then_inc(rounded, 1)
            dve.wait_ge(rounded, 3)


def program(nc, x, norm_mix, w_in, w_sb_proj, w_ca_proj, rel_reversed, w_out, norm_ffn, w_query, keysT,
            expert_u, expert_v, norm_final, out):
    def dram(name, shape):
        return nc.dram_tensor(name, shape, F32, kind="Internal").ap()

    qkT_dram = dram("qkT_dram", [2, 2, 2, WIDTH, S])
    v_dram = dram("v_dram", [2, S, WIDTH])
    oT_dram = dram("oT_dram", [2, WIDTH, S])
    mT_dram = dram("mT_dram", [D, S])
    ext_dram = dram("ext_dram", [HEADS, EXT])
    bias_dram = dram("bias_dram", [HEADS, P, EXT])
    with ExitStack() as ctx:
        ident, neg_suffix, neg_ones, masked = (ctx.enter_context(nc.sbuf_tensor(n, [P, P], F32))
                                               for n in ("ident", "neg_suffix", "neg_ones", "masked"))
        ident_r, neg_suffix_r, masked_r = (ctx.enter_context(nc.sbuf_tensor(n, [P, P], F32R))
                                           for n in ("ident_r", "neg_suffix_r", "masked_r"))
        constants(nc, ident, neg_suffix, neg_ones, masked, ident_r, neg_suffix_r, masked_r)
        ca_qk_in = [ctx.enter_context(nc.semaphore(f"ca_qk_in{h}")) for h in range(2)]
        wg_in = ctx.enter_context(nc.semaphore("gate_w_in"))
        with nc.sbuf_tensor("h_hi", [P, NC, S], F32R) as h_hi, nc.sbuf_tensor("h_lo", [P, NC, S], F32R) as h_lo:
            normalise_and_project(nc, x, norm_mix, w_in, rel_reversed, ident, h_hi, h_lo, qkT_dram, v_dram, ext_dram, bias_dram)
            with nc.sbuf_tensor("w_gate", [P, 2, NC, P], F32) as wg:
                with nc.sbuf_tensor("ca_qk", [HD, 2, 2, 2, S], F32R) as ca_qk:
                    stick_breaking(nc, qkT_dram, v_dram, neg_suffix_r, neg_ones, ident_r, masked_r, oT_dram, ca_qk, ca_qk_in)
                    chunk_attention(nc, qkT_dram, v_dram, ident, bias_dram, oT_dram, ca_qk, ca_qk_in, w_in, wg, wg_in)
                gate_and_merge(nc, w_in, w_sb_proj, w_ca_proj, h_hi, h_lo, oT_dram, mT_dram, wg, wg_in)
        route_and_retrieve(nc, x, w_out, norm_ffn, w_query, keysT, expert_u, expert_v, norm_final, ident, mT_dram, out)


_INS = ["x", "norm_mix", "w_in", "w_sb_proj", "w_ca_proj", "ca_rel_bias", "w_out", "norm_ffn", "peer_w_query",
        "peer_sub_keys", "peer_u", "peer_v", "norm_final"]


def kernel(**inputs):
    import numpy as np
    import concourse.bacc as bacc
    from concourse.bass_utils import run_bass_kernel_spmd

    nc = bacc.Bacc("TRN2", target_bir_lowering=False, num_devices=1)
    arrays, args = {}, []
    for name in _INS:
        a = np.asarray(inputs[name])
        if name == "ca_rel_bias":
            a = a[0, :, ::-1]
        if name == "peer_sub_keys":
            a = a[0].transpose(3, 0, 1, 2).reshape(P, NS, NK)
        a = np.ascontiguousarray(a)
        arrays[f"in_{name}"] = a
        args.append(nc.dram_tensor(f"in_{name}", a.shape, mybir.dt.from_np(a.dtype), kind="ExternalInput").ap())
    args.append(nc.dram_tensor("out_y", (1, S, D), F32, kind="ExternalOutput").ap())
    program(nc, *args)
    return run_bass_kernel_spmd(nc, [arrays], core_ids=[0]).results[0]["out_y"]
```
